# Optimizing a Trainium2 kernel written in Bass

```python
import math
import jax, jax.numpy as jnp
from jax import lax
import numpy as np

D_MODEL = 1024
BATCH = 1
SEQ = 256
DEPTH = 2

GRID_W = 64
CTX_LEN = 256
N_MIXERS = 4
Q_BLOCK = 128
ROPE_BASE = 10000.0
EPS = 1e-6
ADA_CHUNKS = 6

RET_HEADS = 4
RET_DK = D_MODEL // RET_HEADS
RET_DV = 2 * RET_DK
RET_CHUNK = 128

DIFF_HEADS = 8
DIFF_DH = D_MODEL // (2 * DIFF_HEADS)
DIFF_DV = 2 * DIFF_DH

NA_HEADS = 16
NA_DH = D_MODEL // NA_HEADS
NA_WIN_H = 8
NA_WIN_W = 16

MLA_HEADS = 16
MLA_Q_RANK = 256
MLA_KV_RANK = 128
MLA_NOPE = 64
MLA_ROPE = 32
MLA_V = 64
MLA_QK = MLA_NOPE + MLA_ROPE

FFN_HIDDEN = -(-8 * D_MODEL // (3 * 256)) * 256


def rms_norm(x):
    xf = x.astype(jnp.float32)
    return (xf * lax.rsqrt(jnp.mean(xf * xf, axis=-1, keepdims=True) + EPS)).astype(x.dtype)

def rms_norm_gain(x, g):
    return rms_norm(x) * g.astype(x.dtype)

def modulate(x, shift, scale):
    return rms_norm(x) * (1.0 + scale) + shift

def swiglu(h, w_in, w_out):
    a, g = jnp.split(h @ w_in, 2, axis=-1)
    return (jax.nn.silu(a) * g) @ w_out

def rope_2d(x):
    n, d = x.shape[1], x.shape[-1]
    half = d // 2
    quarter = half // 2
    pos = jnp.arange(n)
    row = (pos // GRID_W).astype(jnp.float32)
    col = (pos % GRID_W).astype(jnp.float32)
    inv_freq = jnp.power(ROPE_BASE, -jnp.arange(quarter, dtype=jnp.float32) / quarter)
    bshape = (n,) + (1,) * (x.ndim - 3) + (quarter,)

    def rot(t, p):
        ang = (p[:, None] * inv_freq[None, :]).reshape(bshape)
        cos, sin = jnp.cos(ang).astype(t.dtype), jnp.sin(ang).astype(t.dtype)
        t1, t2 = t[..., :quarter], t[..., quarter:]
        return jnp.concatenate([t1 * cos - t2 * sin, t2 * cos + t1 * sin], axis=-1)

    return jnp.concatenate([rot(x[..., :half], row), rot(x[..., half:], col)], axis=-1)

def map_query_blocks(fn, q):
    b, n = q.shape[0], q.shape[1]
    qb = jnp.moveaxis(q.reshape((b, n // Q_BLOCK, Q_BLOCK) + q.shape[2:]), 1, 0)
    out = jnp.moveaxis(lax.map(fn, qb), 0, 1)
    return out.reshape((b, n) + out.shape[3:])

def softmax_attend(q, k, v, scale):
    s = jnp.einsum('bqhd,bkhd->bhqk', q, k).astype(jnp.float32) * scale
    p = jax.nn.softmax(s, axis=-1).astype(v.dtype)
    return jnp.einsum('bhqk,bkhv->bqhv', p, v)

def chunk_retention(q, k, v, log_gamma, s0):
    b, n, h, _ = q.shape
    dv = v.shape[-1]
    nc = n // RET_CHUNK
    f32 = jnp.float32

    def chunks(t):
        return jnp.moveaxis(t.astype(f32).reshape(b, nc, RET_CHUNK, h, t.shape[-1]), 1, 0)

    idx = jnp.arange(RET_CHUNK, dtype=f32)
    rel = idx[:, None] - idx[None, :]
    d_intra = jnp.where(rel >= 0, jnp.exp(jnp.maximum(rel, 0.0) * log_gamma[:, None, None]), 0.0)
    d_cross = jnp.exp((idx + 1.0)[None, :] * log_gamma[:, None]).T[None, :, :, None]
    d_state = jnp.exp((RET_CHUNK - 1.0 - idx)[None, :] * log_gamma[:, None]).T[None, :, :, None]
    d_chunk = jnp.exp(RET_CHUNK * log_gamma)[None, :, None, None]

    def step(s, qkv):
        qc, kc, vc = qkv
        att = jnp.einsum('bihd,bjhd->bhij', qc, kc) * d_intra
        o = jnp.einsum('bhij,bjhv->bihv', att, vc) + jnp.einsum('bihd,bhdv->bihv', qc, s) * d_cross
        s = s * d_chunk + jnp.einsum('bjhd,bjhv->bhdv', kc * d_state, vc)
        return s, o

    _, o = lax.scan(step, s0.astype(f32), (chunks(q), chunks(k), chunks(v)))
    return jnp.moveaxis(o, 0, 1).reshape(b, n, h, dv)

def retention_output(o, g, norm_g, w_out):
    b, n, h, dv = o.shape
    of = o.astype(jnp.float32)
    mu = jnp.mean(of, axis=-1, keepdims=True)
    var = jnp.mean(jnp.square(of - mu), axis=-1, keepdims=True)
    on = ((of - mu) * lax.rsqrt(var + EPS)).astype(g.dtype).reshape(b, n, h * dv) * norm_g
    return (on * jax.nn.silu(g)) @ w_out

def retention_mixer(h_ctx, h_lat, w_in, decay_logit, norm_g, w_out, need_ctx):
    f32 = jnp.float32
    nqk = RET_HEADS * RET_DK
    splits = [nqk, 2 * nqk, 2 * nqk + RET_HEADS * RET_DV]

    def proj(h):
        b, n, _ = h.shape
        q, k, v, g = jnp.split(h @ w_in, splits, axis=-1)
        return (q.reshape(b, n, RET_HEADS, RET_DK),
                k.reshape(b, n, RET_HEADS, RET_DK) * (RET_DK ** -0.5),
                v.reshape(b, n, RET_HEADS, RET_DV), g)

    qc, kc, vc, gc = proj(h_ctx)
    ql, kl, vl, gl = proj(h_lat)
    ql, kl = rope_2d(ql), rope_2d(kl)
    log_gamma = jax.nn.log_sigmoid(decay_logit.astype(f32))
    lf, lb = log_gamma[0], log_gamma[1]
    n_ctx = h_ctx.shape[1]
    pos = jnp.arange(n_ctx, dtype=f32)
    kcf, vcf = kc.astype(f32), vc.astype(f32)
    w_f = jnp.exp((n_ctx - 1.0 - pos)[:, None] * lf[None, :])[None, :, :, None]
    w_b = jnp.exp(pos[:, None] * lb[None, :])[None, :, :, None]
    s_f = jnp.einsum('blhk,blhv->bhkv', kcf * w_f, vcf)
    s_b = jnp.einsum('blhk,blhv->bhkv', kcf * w_b, vcf)
    o_lat = (chunk_retention(ql, kl, vl, lf, s_f)
             + chunk_retention(ql[:, ::-1], kl[:, ::-1], vl[:, ::-1], lb, s_b)[:, ::-1])
    y_lat = retention_output(o_lat, gl, norm_g, w_out)
    if not need_ctx:
        return None, y_lat
    rel = pos[:, None] - pos[None, :]
    d_bi = (jnp.where(rel >= 0, jnp.exp(jnp.maximum(rel, 0.0) * lf[:, None, None]), 0.0)
            + jnp.where(rel <= 0, jnp.exp(jnp.maximum(-rel, 0.0) * lb[:, None, None]), 0.0))
    att = jnp.einsum('bihd,bjhd->bhij', qc.astype(f32), kcf) * d_bi
    o_ctx = jnp.einsum('bhij,bjhv->bihv', att, vcf)
    return retention_output(o_ctx, gc, norm_g, w_out), y_lat

def diff_attend(q, k, v, lam, scale):
    s = jnp.einsum('bqhmd,bkhmd->bhmqk', q, k).astype(jnp.float32) * scale
    p = jax.nn.softmax(s, axis=-1)
    p = p[:, :, 0] - lam * p[:, :, 1]
    return jnp.einsum('bhqk,bkhv->bqhv', p.astype(v.dtype), v)

def diff_attention_mixer(h_ctx, h_lat, w_in, q_norm_g, k_norm_g, lam_vecs, subln_g, w_out,
                         lambda_init, need_ctx):
    nq = DIFF_HEADS * 2 * DIFF_DH

    def proj(h):
        b, n, _ = h.shape
        q, k, v = jnp.split(h @ w_in, [nq, 2 * nq], axis=-1)
        q = rms_norm_gain(q.reshape(b, n, DIFF_HEADS, 2, DIFF_DH), q_norm_g)
        k = rms_norm_gain(k.reshape(b, n, DIFF_HEADS, 2, DIFF_DH), k_norm_g)
        return q, k, v.reshape(b, n, DIFF_HEADS, DIFF_DV)

    qc, kc, vc = proj(h_ctx)
    ql, kl, vl = proj(h_lat)
    ql, kl = rope_2d(ql), rope_2d(kl)
    lv = lam_vecs.astype(jnp.float32)
    lam = jnp.exp(jnp.sum(lv[0] * lv[1])) - jnp.exp(jnp.sum(lv[2] * lv[3])) + lambda_init
    scale = DIFF_DH ** -0.5

    def out(o):
        b, n = o.shape[0], o.shape[1]
        o = rms_norm_gain(o, subln_g) * (1.0 - lambda_init)
        return o.reshape(b, n, DIFF_HEADS * DIFF_DV) @ w_out

    k_all = jnp.concatenate([kc, kl], axis=1)
    v_all = jnp.concatenate([vc, vl], axis=1)
    y_lat = out(map_query_blocks(lambda qb: diff_attend(qb, k_all, v_all, lam, scale), ql))
    if not need_ctx:
        return None, y_lat
    return out(diff_attend(qc, kc, vc, lam, scale)), y_lat

def neighborhood_mixer(h_ctx, h_lat, w_in, q_norm_g, k_norm_g, rel_bias, w_out, need_ctx):
    def proj(h):
        b, n, _ = h.shape
        q, k, v = jnp.split(h @ w_in, 3, axis=-1)
        q = rms_norm_gain(q.reshape(b, n, NA_HEADS, NA_DH), q_norm_g)
        k = rms_norm_gain(k.reshape(b, n, NA_HEADS, NA_DH), k_norm_g)
        return q, k, v.reshape(b, n, NA_HEADS, NA_DH)

    qc, kc, vc = proj(h_ctx)
    ql, kl, vl = proj(h_lat)
    scale = NA_DH ** -0.5
    b, n = ql.shape[0], ql.shape[1]
    rows = n // GRID_W
    wh = min(NA_WIN_H, rows)
    n_loc = wh * NA_WIN_W

    def grid(t):
        return t.reshape(b, rows, GRID_W, NA_HEADS, NA_DH)

    kg, vg = grid(kl), grid(vl)
    col = np.arange(GRID_W)
    col_start = np.clip(col - NA_WIN_W // 2, 0, GRID_W - NA_WIN_W)
    col_idx = col_start[:, None] + np.arange(NA_WIN_W)[None, :]
    dc_idx = col_idx - col[:, None] + (NA_WIN_W - 1)

    def row_block(args):
        r, q_row = args
        r0 = jnp.clip(r - NA_WIN_H // 2, 0, rows - wh)
        k_win = lax.dynamic_slice_in_dim(kg, r0, wh, axis=1)[:, :, col_idx]
        v_win = lax.dynamic_slice_in_dim(vg, r0, wh, axis=1)[:, :, col_idx]
        dr_idx = r0 + jnp.arange(wh) - r + (NA_WIN_H - 1)
        bias = rel_bias[:, dr_idx[:, None, None], dc_idx[None, :, :]].transpose(0, 2, 1, 3)
        s_loc = (jnp.einsum('bqhd,brqwhd->bhqrw', q_row, k_win).astype(jnp.float32) * scale
                 + bias.astype(jnp.float32))
        s_ctx = jnp.einsum('bqhd,bkhd->bhqk', q_row, kc).astype(jnp.float32) * scale
        s = jnp.concatenate([s_loc.reshape(b, NA_HEADS, GRID_W, n_loc), s_ctx], axis=-1)
        p = jax.nn.softmax(s, axis=-1).astype(v_win.dtype)
        p_loc = p[..., :n_loc].reshape(b, NA_HEADS, GRID_W, wh, NA_WIN_W)
        return (jnp.einsum('bhqrw,brqwhv->bqhv', p_loc, v_win)
                + jnp.einsum('bhqk,bkhv->bqhv', p[..., n_loc:], vc))

    o = lax.map(row_block, (jnp.arange(rows), jnp.moveaxis(grid(ql), 1, 0)))
    y_lat = jnp.moveaxis(o, 0, 1).reshape(b, n, NA_HEADS * NA_DH) @ w_out
    if not need_ctx:
        return None, y_lat
    y_ctx = softmax_attend(qc, kc, vc, scale).reshape(b, -1, NA_HEADS * NA_DH) @ w_out
    return y_ctx, y_lat

def split_qk_norm(t, g):
    return jnp.concatenate([rms_norm(t[..., :MLA_NOPE]), rms_norm(t[..., MLA_NOPE:])], axis=-1) * g.astype(t.dtype)

def rotate_rope_part(t):
    return jnp.concatenate([t[..., :MLA_NOPE], rope_2d(t[..., MLA_NOPE:])], axis=-1)

def mla_mixer(h_ctx, h_lat, w_down, q_norm_g, kv_norm_g, w_uq, w_ukv, qk_norm_q, qk_norm_k,
              w_out, need_ctx):
    def keys_values(z, rotate):
        b, n, _ = z.shape
        c_kv = z[..., MLA_Q_RANK:MLA_Q_RANK + MLA_KV_RANK]
        k_rope = z[..., MLA_Q_RANK + MLA_KV_RANK:]
        kv = (rms_norm_gain(c_kv, kv_norm_g) @ w_ukv).reshape(b, n, MLA_HEADS, MLA_NOPE + MLA_V)
        k_rope = jnp.broadcast_to(k_rope[:, :, None, :], (b, n, MLA_HEADS, MLA_ROPE))
        k = split_qk_norm(jnp.concatenate([kv[..., :MLA_NOPE], k_rope], axis=-1), qk_norm_k)
        return (rotate_rope_part(k) if rotate else k), kv[..., MLA_NOPE:]

    def queries(z, rotate):
        b, n, _ = z.shape
        q = (rms_norm_gain(z[..., :MLA_Q_RANK], q_norm_g) @ w_uq).reshape(b, n, MLA_HEADS, MLA_QK)
        q = split_qk_norm(q, qk_norm_q)
        return rotate_rope_part(q) if rotate else q

    scale = MLA_QK ** -0.5
    z_ctx = h_ctx @ w_down
    z_lat = h_lat @ w_down
    kc, vc = keys_values(z_ctx, False)
    kl, vl = keys_values(z_lat, True)
    ql = queries(z_lat, True)
    k_all = jnp.concatenate([kc, kl], axis=1)
    v_all = jnp.concatenate([vc, vl], axis=1)
    b, n = ql.shape[0], ql.shape[1]
    o = map_query_blocks(lambda qb: softmax_attend(qb, k_all, v_all, scale), ql)
    y_lat = o.reshape(b, n, MLA_HEADS * MLA_V) @ w_out
    if not need_ctx:
        return None, y_lat
    o_ctx = softmax_attend(queries(z_ctx, False), kc, vc, scale)
    return o_ctx.reshape(b, -1, MLA_HEADS * MLA_V) @ w_out, y_lat

def first_inputs(seed: int = 0) -> dict:
    key = jax.random.key(seed)
    keys = iter(jax.random.split(key, 40))
    f32 = jnp.float32

    def normal(shape, scale):
        return jax.random.normal(next(keys), shape, f32) * scale

    def gain(shape):
        return 1.0 + normal(shape, 0.02)

    d = D_MODEL
    n_ret, n_diff, n_na, n_mla = [len(range(m, DEPTH, N_MIXERS)) for m in range(N_MIXERS)]
    gam = 1.0 - 2.0 ** (-5.0 - np.arange(RET_HEADS, dtype=np.float32))
    decay_logit0 = jnp.asarray(np.log(gam / (1.0 - gam)), f32)
    ret_cols = 2 * RET_HEADS * RET_DK + 2 * RET_HEADS * RET_DV
    diff_cols = 2 * DIFF_HEADS * 2 * DIFF_DH + DIFF_HEADS * DIFF_DV
    mla_down_cols = MLA_Q_RANK + MLA_KV_RANK + MLA_ROPE
    return {
        'x': normal((BATCH, SEQ, d), 1.0),
        'c': normal((BATCH, d), 1.0),
        'ctx': normal((BATCH, CTX_LEN, d), 1.0),
        'c_ctx': normal((d,), 1.0),
        'ada_w': normal((DEPTH, d, ADA_CHUNKS * d), 0.5 * d ** -0.5),
        'ada_b': normal((DEPTH, ADA_CHUNKS * d), 0.02),
        'ret_w_in': normal((n_ret, d, ret_cols), d ** -0.5),
        'ret_decay_logit': decay_logit0 + normal((n_ret, 2, RET_HEADS), 0.1),
        'ret_norm_g': gain((n_ret, RET_HEADS * RET_DV)),
        'ret_w_out': normal((n_ret, RET_HEADS * RET_DV, d), (RET_HEADS * RET_DV) ** -0.5),
        'diff_w_in': normal((n_diff, d, diff_cols), d ** -0.5),
        'diff_q_norm_g': gain((n_diff, DIFF_DH)),
        'diff_k_norm_g': gain((n_diff, DIFF_DH)),
        'diff_lambda': normal((n_diff, 4, DIFF_DH), 0.1),
        'diff_subln_g': gain((n_diff, DIFF_DV)),
        'diff_w_out': normal((n_diff, DIFF_HEADS * DIFF_DV, d), (DIFF_HEADS * DIFF_DV) ** -0.5),
        'na_w_in': normal((n_na, d, 3 * NA_HEADS * NA_DH), d ** -0.5),
        'na_q_norm_g': gain((n_na, NA_DH)),
        'na_k_norm_g': gain((n_na, NA_DH)),
        'na_rel_bias': normal((n_na, NA_HEADS, 2 * NA_WIN_H - 1, 2 * NA_WIN_W - 1), 0.1),
        'na_w_out': normal((n_na, NA_HEADS * NA_DH, d), (NA_HEADS * NA_DH) ** -0.5),
        'mla_w_down': normal((n_mla, d, mla_down_cols), d ** -0.5),
        'mla_q_norm_g': gain((n_mla, MLA_Q_RANK)),
        'mla_kv_norm_g': gain((n_mla, MLA_KV_RANK)),
        'mla_w_uq': normal((n_mla, MLA_Q_RANK, MLA_HEADS * MLA_QK), MLA_Q_RANK ** -0.5),
        'mla_w_ukv': normal((n_mla, MLA_KV_RANK, MLA_HEADS * (MLA_NOPE + MLA_V)), MLA_KV_RANK ** -0.5),
        'mla_qk_norm_q': gain((n_mla, MLA_QK)),
        'mla_qk_norm_k': gain((n_mla, MLA_QK)),
        'mla_w_out': normal((n_mla, MLA_HEADS * MLA_V, d), (MLA_HEADS * MLA_V) ** -0.5),
        'ffn_w_in': normal((DEPTH, d, 2 * FFN_HIDDEN), d ** -0.5),
        'ffn_w_out': normal((DEPTH, FFN_HIDDEN, d), FFN_HIDDEN ** -0.5),
    }

def first_block(x, c, ctx, c_ctx, ada_w, ada_b,
              ret_w_in, ret_decay_logit, ret_norm_g, ret_w_out,
              diff_w_in, diff_q_norm_g, diff_k_norm_g, diff_lambda, diff_subln_g, diff_w_out,
              na_w_in, na_q_norm_g, na_k_norm_g, na_rel_bias, na_w_out,
              mla_w_down, mla_q_norm_g, mla_kv_norm_g, mla_w_uq, mla_w_ukv,
              mla_qk_norm_q, mla_qk_norm_k, mla_w_out,
              ffn_w_in, ffn_w_out):
    s_lat = jax.nn.silu(c)[:, None, :]
    s_ctx = jax.nn.silu(c_ctx)[None, None, :]
    x_lat, x_ctx = x, ctx
    for i in range(DEPTH):
        need_ctx = i < DEPTH - 1
        mod_l = jnp.split(s_lat @ ada_w[i] + ada_b[i], ADA_CHUNKS, axis=-1)
        mod_c = jnp.split(s_ctx @ ada_w[i] + ada_b[i], ADA_CHUNKS, axis=-1)
        h_lat = modulate(x_lat, mod_l[0], mod_l[1])
        h_ctx = modulate(x_ctx, mod_c[0], mod_c[1])
        kind, j = i % N_MIXERS, i // N_MIXERS
        if kind == 0:
            y_ctx, y_lat = retention_mixer(h_ctx, h_lat, ret_w_in[j], ret_decay_logit[j],
                                           ret_norm_g[j], ret_w_out[j], need_ctx)
        elif kind == 1:
            lambda_init = 0.8 - 0.6 * math.exp(-0.3 * i)
            y_ctx, y_lat = diff_attention_mixer(h_ctx, h_lat, diff_w_in[j], diff_q_norm_g[j],
                                                diff_k_norm_g[j], diff_lambda[j], diff_subln_g[j],
                                                diff_w_out[j], lambda_init, need_ctx)
        elif kind == 2:
            y_ctx, y_lat = neighborhood_mixer(h_ctx, h_lat, na_w_in[j], na_q_norm_g[j],
                                              na_k_norm_g[j], na_rel_bias[j], na_w_out[j], need_ctx)
        else:
            y_ctx, y_lat = mla_mixer(h_ctx, h_lat, mla_w_down[j], mla_q_norm_g[j], mla_kv_norm_g[j],
                                     mla_w_uq[j], mla_w_ukv[j], mla_qk_norm_q[j], mla_qk_norm_k[j],
                                     mla_w_out[j], need_ctx)
        x_lat = x_lat + mod_l[2] * y_lat
        x_lat = x_lat + mod_l[5] * swiglu(modulate(x_lat, mod_l[3], mod_l[4]), ffn_w_in[i], ffn_w_out[i])
        if need_ctx:
            x_ctx = x_ctx + mod_c[2] * y_ctx
            x_ctx = x_ctx + mod_c[5] * swiglu(modulate(x_ctx, mod_c[3], mod_c[4]), ffn_w_in[i], ffn_w_out[i])
    return x_lat


N_MIXERS_2 = 2
D_FF = 4 * D_MODEL
CONV_WIDTH = 31
CONV_DIM = D_MODEL
MLSTM_INNER = 2 * D_MODEL
MLSTM_HEADS = 4
MLSTM_HEAD_DIM = MLSTM_INNER // MLSTM_HEADS
QKV_CONV_WIDTH = 5
CHUNK = 128
N_A = (DEPTH + 1) // 2
N_B = DEPTH // 2
ALPHA = (2 * DEPTH) ** 0.25
BETA = (8 * DEPTH) ** -0.25
LN_EPS = 1e-5


def layer_norm(x, g, b):
    xf = x.astype(jnp.float32)
    mu = jnp.mean(xf, axis=-1, keepdims=True)
    var = jnp.mean(jnp.square(xf - mu), axis=-1, keepdims=True)
    return ((xf - mu) * lax.rsqrt(var + LN_EPS) * g.astype(jnp.float32) + b.astype(jnp.float32)).astype(x.dtype)

def adaln(cvec, w, b):
    return jnp.split(jax.nn.silu(cvec) @ w + b, 6, axis=-1)

def modulate_2(x, shift, scale):
    return x * (1 + scale) + shift

def dwconv(x, w):
    return lax.conv_general_dilated(x, w[:, None, :], window_strides=(1,), padding='SAME',
                                    dimension_numbers=('NWC', 'WIO', 'NWC'),
                                    feature_group_count=x.shape[-1])

def sq_relu_mlp(u, w1, w2):
    return jnp.square(jax.nn.relu(u @ w1)) @ w2

def conformer_conv(u, rows, w_pw1, b_pw1, w_dw, b_dw, ln_g, ln_b, w_pw2, b_pw2):
    a = u @ w_pw1 + b_pw1
    a = a[..., :CONV_DIM] * jax.nn.sigmoid(a[..., CONV_DIM:])
    bsz, s, ch = a.shape
    if rows is None:
        a = dwconv(a, w_dw)
    else:
        a = dwconv(a.reshape(bsz * rows, GRID_W, ch), w_dw).reshape(bsz, s, ch)
    a = jax.nn.silu(layer_norm(a + b_dw, ln_g, ln_b))
    return a @ w_pw2 + b_pw2

def mlstm_chunk_scan(q, k, v, i_pre, f_pre, state):
    bsz, nh, s, dh = q.shape
    nc = s // CHUNK

    def to_chunks(t):
        return jnp.moveaxis(t.reshape(bsz, nh, nc, CHUNK, *t.shape[3:]), 2, 0)

    lf = jax.nn.log_sigmoid(f_pre)
    lower = jnp.tril(jnp.ones((CHUNK, CHUNK), dtype=bool))

    def step(carry, xs):
        C, n, m = carry
        qc, kc, vc, ic, lfc = xs
        bcum = jnp.cumsum(lfc, axis=-1)
        dlog = bcum[..., :, None] - bcum[..., None, :] + ic[..., None, :]
        dlog = jnp.where(lower, dlog, -jnp.inf)
        inter = bcum + m[..., None]
        m_row = jnp.maximum(inter, jnp.max(dlog, axis=-1))
        scores = jnp.einsum('bhtd,bhsd->bhts', qc, kc) * jnp.exp(dlog - m_row[..., None])
        w_inter = jnp.exp(inter - m_row)
        num = jnp.einsum('bhts,bhsd->bhtd', scores, vc) + w_inter[..., None] * jnp.einsum('bhtd,bhde->bhte', qc, C)
        den = jnp.sum(scores, axis=-1) + w_inter * jnp.einsum('bhtd,bhd->bht', qc, n)
        h = num / jnp.maximum(jnp.abs(den), jnp.exp(-m_row))[..., None]
        b_last = bcum[..., -1]
        dk = b_last[..., None] - bcum + ic
        m_new = jnp.maximum(b_last + m, jnp.max(dk, axis=-1))
        wk = jnp.exp(dk - m_new[..., None])[..., None] * kc
        decay = jnp.exp(b_last + m - m_new)
        C_new = decay[..., None, None] * C + jnp.einsum('bhsd,bhse->bhde', wk, vc)
        n_new = decay[..., None] * n + jnp.sum(wk, axis=2)
        return (C_new, n_new, m_new), h

    state, h = lax.scan(step, state, (to_chunks(q), to_chunks(k), to_chunks(v), to_chunks(i_pre), to_chunks(lf)))
    h = jnp.moveaxis(h, 0, 2).reshape(bsz, nh, s, dh)
    return h, state

def mlstm_features(u, w_up, w_conv, b_conv, w_q, w_k, w_v, w_gate, b_gate, w_o, b_o):
    up = u @ w_up
    xm, z = up[..., :MLSTM_INNER], up[..., MLSTM_INNER:]
    xc = jax.nn.silu(dwconv(xm, w_conv) + b_conv)
    q, k, v = xc @ w_q, xc @ w_k, xm @ w_v
    gates = jnp.concatenate([q, k, v], axis=-1) @ w_gate + b_gate
    o = jax.nn.sigmoid(xm @ w_o + b_o)
    return xc, z, q, k, v, gates, o

def to_heads(t):
    bsz, s, _ = t.shape
    return jnp.transpose(t.reshape(bsz, s, MLSTM_HEADS, MLSTM_HEAD_DIM), (0, 2, 1, 3)).astype(jnp.float32)

def bidir_scan(feats, states):
    _, _, q, k, v, gates, _ = feats
    qh = to_heads(q)
    kh = to_heads(k) * (MLSTM_HEAD_DIM ** -0.5)
    vh = to_heads(v)
    g = jnp.moveaxis(gates.astype(jnp.float32), -1, 1)
    i_f, f_f, i_b, f_b = jnp.split(g, 4, axis=1)
    h_f, st_f = mlstm_chunk_scan(qh, kh, vh, i_f, f_f, states[0])
    flip = lambda t: jnp.flip(t, axis=2)
    h_b, st_b = mlstm_chunk_scan(flip(qh), flip(kh), flip(vh), flip(i_b), flip(f_b), states[1])
    return h_f, flip(h_b), (st_f, st_b)

def mlstm_output(feats, h_f, h_b, gn_g, skip, w_down):
    xc, z, _, _, _, _, o = feats
    bsz, s, _ = o.shape
    from_heads = lambda t: jnp.transpose(t, (0, 2, 1, 3)).reshape(bsz, s, MLSTM_INNER)
    of = o.astype(jnp.float32)
    hsum = of[..., :MLSTM_INNER] * from_heads(h_f) + of[..., MLSTM_INNER:] * from_heads(h_b)
    hh = hsum.reshape(bsz, s, MLSTM_HEADS, MLSTM_HEAD_DIM)
    mu = jnp.mean(hh, axis=-1, keepdims=True)
    var = jnp.mean(jnp.square(hh - mu), axis=-1, keepdims=True)
    hn = ((hh - mu) * lax.rsqrt(var + LN_EPS)).reshape(bsz, s, MLSTM_INNER) * gn_g.astype(jnp.float32)
    y = (hn.astype(xc.dtype) + skip * xc) * jax.nn.silu(z)
    return y @ w_down

def mlstm_mixer(u, uc, need_ctx, w_up, w_conv, b_conv, w_q, w_k, w_v, w_gate, b_gate, w_o, b_o, gn_g, skip, w_down):
    p_in = (w_up, w_conv, b_conv, w_q, w_k, w_v, w_gate, b_gate, w_o, b_o)
    bsz = u.shape[0]
    zero_state = (jnp.zeros((bsz, MLSTM_HEADS, MLSTM_HEAD_DIM, MLSTM_HEAD_DIM), jnp.float32),
                  jnp.zeros((bsz, MLSTM_HEADS, MLSTM_HEAD_DIM), jnp.float32),
                  jnp.zeros((bsz, MLSTM_HEADS), jnp.float32))
    fc = mlstm_features(uc, *p_in)
    hf_c, hb_c, ctx_states = bidir_scan(fc, (zero_state, zero_state))
    fl = mlstm_features(u, *p_in)
    hf, hb, _ = bidir_scan(fl, ctx_states)
    y = mlstm_output(fl, hf, hb, gn_g, skip, w_down).astype(u.dtype)
    yc = mlstm_output(fc, hf_c, hb_c, gn_g, skip, w_down).astype(u.dtype) if need_ctx else None
    return y, yc

def second_inputs(seed: int = 0) -> dict:
    key = jax.random.key(seed)
    ks = iter(jax.random.split(key, 48))

    def nrm(shape, scale):
        return jax.random.normal(next(ks), shape, jnp.float32) * scale

    D, E, H = D_MODEL, MLSTM_INNER, MLSTM_HEADS
    i_bias = nrm((N_B, 2, H), 0.1)
    f_bias = jnp.linspace(3.0, 6.0, H)[None, None, :] + nrm((N_B, 2, H), 0.1)
    b_gate = jnp.concatenate([i_bias[:, 0], f_bias[:, 0], i_bias[:, 1], f_bias[:, 1]], axis=-1)
    return {
        'x': nrm((BATCH, SEQ, D), 1.0),
        'c': nrm((BATCH, D), 1.0),
        'ctx': nrm((BATCH, CTX_LEN, D), 1.0),
        'c_ctx': nrm((D,), 1.0),
        'ada_w': nrm((DEPTH, D, 6 * D), 0.5 * D ** -0.5),
        'ada_b': nrm((DEPTH, 6 * D), 0.02),
        'ln1_g': 1.0 + nrm((DEPTH, D), 0.05),
        'ln1_b': nrm((DEPTH, D), 0.02),
        'ln2_g': 1.0 + nrm((DEPTH, D), 0.05),
        'ln2_b': nrm((DEPTH, D), 0.02),
        'mlp_w1': nrm((DEPTH, D, D_FF), D ** -0.5),
        'mlp_w2': nrm((DEPTH, D_FF, D), BETA * D_FF ** -0.5),
        'conv_w_pw1': nrm((N_A, D, 2 * CONV_DIM), D ** -0.5),
        'conv_b_pw1': nrm((N_A, 2 * CONV_DIM), 0.02),
        'conv_w_dw': nrm((N_A, CONV_WIDTH, CONV_DIM), CONV_WIDTH ** -0.5),
        'conv_b_dw': nrm((N_A, CONV_DIM), 0.02),
        'conv_ln_g': 1.0 + nrm((N_A, CONV_DIM), 0.05),
        'conv_ln_b': nrm((N_A, CONV_DIM), 0.02),
        'conv_w_pw2': nrm((N_A, CONV_DIM, D), BETA * CONV_DIM ** -0.5),
        'conv_b_pw2': nrm((N_A, D), 0.02),
        'ml_w_up': nrm((N_B, D, 2 * E), D ** -0.5),
        'ml_w_conv': nrm((N_B, QKV_CONV_WIDTH, E), QKV_CONV_WIDTH ** -0.5),
        'ml_b_conv': nrm((N_B, E), 0.02),
        'ml_w_q': nrm((N_B, E, E), E ** -0.5),
        'ml_w_k': nrm((N_B, E, E), E ** -0.5),
        'ml_w_v': nrm((N_B, E, E), E ** -0.5),
        'ml_w_gate': nrm((N_B, 3 * E, 4 * H), (3 * E) ** -0.5),
        'ml_b_gate': b_gate,
        'ml_w_o': nrm((N_B, E, 2 * E), E ** -0.5),
        'ml_b_o': nrm((N_B, 2 * E), 0.02),
        'ml_gn_g': 1.0 + nrm((N_B, E), 0.05),
        'ml_skip': 1.0 + nrm((N_B, E), 0.05),
        'ml_w_down': nrm((N_B, E, D), BETA * E ** -0.5),
    }

def second_block(x, c, ctx, c_ctx, ada_w, ada_b, ln1_g, ln1_b, ln2_g, ln2_b, mlp_w1, mlp_w2,
              conv_w_pw1, conv_b_pw1, conv_w_dw, conv_b_dw, conv_ln_g, conv_ln_b, conv_w_pw2, conv_b_pw2,
              ml_w_up, ml_w_conv, ml_b_conv, ml_w_q, ml_w_k, ml_w_v, ml_w_gate, ml_b_gate, ml_w_o, ml_b_o,
              ml_gn_g, ml_skip, ml_w_down):
    rows = x.shape[1] // GRID_W
    h, hc = x, ctx
    for i in range(DEPTH):
        need_ctx = i < DEPTH - 1
        j = i // N_MIXERS_2
        sh1, sc1, g1, sh2, sc2, g2 = adaln(c[:, None, :], ada_w[i], ada_b[i])
        csh1, csc1, cg1, csh2, csc2, cg2 = adaln(c_ctx, ada_w[i], ada_b[i])
        u = modulate_2(h, sh1, sc1)
        uc = modulate_2(hc, csh1, csc1)
        if i % N_MIXERS_2 == 0:
            cp = (conv_w_pw1[j], conv_b_pw1[j], conv_w_dw[j], conv_b_dw[j], conv_ln_g[j], conv_ln_b[j],
                  conv_w_pw2[j], conv_b_pw2[j])
            y = conformer_conv(u, rows, *cp)
            yc = conformer_conv(uc, None, *cp) if need_ctx else None
        else:
            y, yc = mlstm_mixer(u, uc, need_ctx, ml_w_up[j], ml_w_conv[j], ml_b_conv[j], ml_w_q[j], ml_w_k[j],
                                ml_w_v[j], ml_w_gate[j], ml_b_gate[j], ml_w_o[j], ml_b_o[j], ml_gn_g[j],
                                ml_skip[j], ml_w_down[j])
        h = layer_norm(ALPHA * h + g1 * y, ln1_g[i], ln1_b[i])
        h = layer_norm(ALPHA * h + g2 * sq_relu_mlp(modulate_2(h, sh2, sc2), mlp_w1[i], mlp_w2[i]), ln2_g[i], ln2_b[i])
        if need_ctx:
            hc = layer_norm(ALPHA * hc + cg1 * yc, ln1_g[i], ln1_b[i])
            hc = layer_norm(ALPHA * hc + cg2 * sq_relu_mlp(modulate_2(hc, csh2, csc2), mlp_w1[i], mlp_w2[i]),
                            ln2_g[i], ln2_b[i])
    return h


def setup_inputs(seed=0):
    out = dict(first_inputs(seed))
    for name, value in second_inputs(seed + 1).items():
        if name != "x":
            out[name + "_2"] = value
    return out


def reference(
    x, c, ctx, c_ctx, ada_w, ada_b, ret_w_in, ret_decay_logit, ret_norm_g, ret_w_out, diff_w_in,
    diff_q_norm_g, diff_k_norm_g, diff_lambda, diff_subln_g, diff_w_out, na_w_in, na_q_norm_g,
    na_k_norm_g, na_rel_bias, na_w_out, mla_w_down, mla_q_norm_g, mla_kv_norm_g, mla_w_uq,
    mla_w_ukv, mla_qk_norm_q, mla_qk_norm_k, mla_w_out, ffn_w_in, ffn_w_out, c_2, ctx_2,
    c_ctx_2, ada_w_2, ada_b_2, ln1_g_2, ln1_b_2, ln2_g_2, ln2_b_2, mlp_w1_2, mlp_w2_2,
    conv_w_pw1_2, conv_b_pw1_2, conv_w_dw_2, conv_b_dw_2, conv_ln_g_2, conv_ln_b_2,
    conv_w_pw2_2, conv_b_pw2_2, ml_w_up_2, ml_w_conv_2, ml_b_conv_2, ml_w_q_2, ml_w_k_2,
    ml_w_v_2, ml_w_gate_2, ml_b_gate_2, ml_w_o_2, ml_b_o_2, ml_gn_g_2, ml_skip_2, ml_w_down_2,
):
    x = first_block(
        x, c, ctx, c_ctx, ada_w, ada_b, ret_w_in, ret_decay_logit, ret_norm_g, ret_w_out,
        diff_w_in, diff_q_norm_g, diff_k_norm_g, diff_lambda, diff_subln_g, diff_w_out, na_w_in,
        na_q_norm_g, na_k_norm_g, na_rel_bias, na_w_out, mla_w_down, mla_q_norm_g,
        mla_kv_norm_g, mla_w_uq, mla_w_ukv, mla_qk_norm_q, mla_qk_norm_k, mla_w_out, ffn_w_in,
        ffn_w_out,
    )
    return second_block(
        x, c_2, ctx_2, c_ctx_2, ada_w_2, ada_b_2, ln1_g_2, ln1_b_2, ln2_g_2, ln2_b_2, mlp_w1_2,
        mlp_w2_2, conv_w_pw1_2, conv_b_pw1_2, conv_w_dw_2, conv_b_dw_2, conv_ln_g_2,
        conv_ln_b_2, conv_w_pw2_2, conv_b_pw2_2, ml_w_up_2, ml_w_conv_2, ml_b_conv_2, ml_w_q_2,
        ml_w_k_2, ml_w_v_2, ml_w_gate_2, ml_b_gate_2, ml_w_o_2, ml_b_o_2, ml_gn_g_2, ml_skip_2,
        ml_w_down_2,
    )


_drawn_inputs = setup_inputs


def setup_inputs(seed=0):
    import zlib

    import numpy as np

    out = dict(_drawn_inputs(seed))
    spreads = {}
    factors = {'ret_norm_g': 8.0,
     'diff_q_norm_g': 8.0,
     'diff_k_norm_g': 8.0,
     'diff_lambda': 8.0,
     'diff_subln_g': 24.052,
     'ada_b_2': 2.995,
     'conv_b_pw1_2': 8.0,
     'conv_b_dw_2': 8.0,
     'conv_ln_g_2': 35.719,
     'conv_ln_b_2': 41.824,
     'conv_b_pw2_2': 22.635,
     'ml_b_conv_2': 8.0,
     'ml_b_o_2': 26.115,
     'ml_gn_g_2': 28.546,
     'ml_skip_2': 28.586}
    for name, (base, spread) in spreads.items():
        noise = np.random.default_rng([zlib.crc32(name.encode()), seed]).standard_normal(out[name].shape)
        drawn = base * np.exp(spread * noise) if base else spread * noise
        out[name] = __import__('jax').numpy.asarray(drawn.astype(out[name].dtype))
    for name, factor in factors.items():
        out[name] = (out[name] * factor).astype(out[name].dtype)
    return out
```

```python
import math
from contextlib import ExitStack

import numpy as np

import concourse.bass as bass
from concourse import mybir

P = 128
D = 1024
LAT = 256
CTX = 256
TOK = LAT + CTX
DC = D // P
GRID_W = 64
RET_HEADS, RET_DK, RET_DV = 4, 256, 512
DIFF_HEADS, DIFF_DH, DIFF_DV = 8, 64, 128
FFN = 2816
FFN_C = FFN // P
MLP_HALF_C = 16
CONV_W, CONV_ROWS = 31, LAT // GRID_W
CONV_PAD = CONV_W // 2
ROW_PADDED = GRID_W + 2 * CONV_PAD
CONV_IN = CONV_ROWS * ROW_PADDED + CTX + 2 * CONV_PAD
CONV_OUT = CONV_IN - 2 * CONV_PAD
CONV_CTX = CONV_ROWS * ROW_PADDED
ML_INNER, ML_HEADS, ML_DH, ML_TAPS = 2048, 4, 512, 5
MLC = ML_INNER // P
ML_IN = LAT + CTX + 2 * (ML_TAPS - 1)
ML_OUT = ML_IN - (ML_TAPS - 1)
ML_CTX = LAT + ML_TAPS - 1
LAMBDA_INIT = 0.8 - 0.6 * math.exp(-0.3)
ALPHA = 4 ** 0.25
EPS, LN_EPS = 1e-6, 1e-5
ADA_TILES = 48

PHASES = [("ret_qk", 16), ("ret_v", 16), ("ret_g", 16), ("ret_out", 16), ("ffn0_in", 44), ("ffn0_out", 22),
          ("diff_qk", 16), ("diff_v", 8), ("diff_out", 8), ("ffn1_in", 44), ("ffn1_out", 22),
          ("pw1", 16), ("pw2", 8),
          ("mlp0a_in", 16), ("mlp0a_out", 16), ("mlp0b_in", 16), ("mlp0b_out", 16),
          ("up_x", 16), ("up_z", 16), ("ml_v", 32), ("ml_o", 64), ("ml_q", 32), ("ml_k", 32), ("down", 16),
          ("mlp1a_in", 16), ("mlp1a_out", 16), ("mlp1b_in", 16), ("mlp1b_out", 16)]
FIRST = {}
_n = 0
for _name, _count in PHASES:
    FIRST[_name] = _n
    _n += _count
N_TILES = _n
COUNT = dict(PHASES)
SLOTS = 4
LOOKAHEAD = SLOTS - 1
ADA_FIRST = 16

VEC_LAYOUT = [("ret_norm_g", 16), ("diff_q_g", 1), ("diff_k_g", 1), ("subln_g", 1), ("ada_b", 4 * ADA_TILES),
              ("decay", 8), ("b_pw1", 16), ("w_dw", 8 * CONV_W), ("b_dw", 8), ("conv_ln_g", 8),
              ("conv_ln_b", 8), ("b_pw2", 8), ("ln1_g", 16), ("ln1_b", 16), ("ln2_g", 16), ("ln2_b", 16),
              ("ml_b_conv", 16), ("ml_w_conv", 16 * ML_TAPS), ("gn_g", 16), ("skip", 16), ("b_gate", 1)]
VEC = {}
_n = 0
for _name, _count in VEC_LAYOUT:
    VEC[_name] = _n
    _n += _count
N_VEC = _n


def program(nc, weights, ada, c_rows_d, x_t, ctx2_t, vecs_d, consts_d, ret_rope_d, ret_decay_d, diff_tab_d, lam_d,
            b_o_d, w_gate_d, sel_d, out_d):
    F32 = mybir.dt.float32
    F32R = mybir.dt.float32r
    ACT = mybir.ActivationFunctionType
    ALU = mybir.AluOpType
    AX = mybir.AxisListType
    MUL, ADD, SUB, MAX, MIN = ALU.mult, ALU.add, ALU.subtract, ALU.max, ALU.min

    ctx = ExitStack()
    with ctx:
        base = (nc.sbuf_base + 31) // 32 * 32

        def at(name, shape, offset, dt=F32):
            return nc.alloc_sbuf_tensor_at(name, shape, dt, offset=base + offset)

        K = 1024
        RAW = at("w_raw", [P, SLOTS, 1024], 0)
        WHI = at("w_hi", [P, SLOTS, 1024], 16 * K, F32R)
        WLO = at("w_lo", [P, SLOTS, 1024], 32 * K, F32R)
        X = at("x_res", [P, DC, TOK], 48 * K)
        H_AT, ARENA, TMP_AT, CONST_AT = 64 * K, 96 * K, 192 * K, 202 * K
        HHI = at("h_hi", [P, DC, TOK], H_AT, F32R)
        HLO = at("h_lo", [P, DC, TOK], H_AT + 16 * K, F32R)
        TMP = at("tmp", [P, 2560], TMP_AT)
        IDENT = at("ident", [P, P], CONST_AT)
        ONES = at("ones", [P, P], CONST_AT + 512)
        MOD = at("mod", [P, 4 * 2 * ADA_TILES], CONST_AT + 1024)
        VECS = at("vecs", [P, N_VEC], CONST_AT + 1024 + 1536)
        assert base + CONST_AT + 1024 + 1536 + 4 * N_VEC <= nc.sbuf_usable_end

        def ada_area(name, offset):
            return (at(f"ada_junk_{name}", [P, 1024], offset), at(f"ada_ring_{name}", [P, 2, 1024], offset + 4 * K),
                    at(f"ada_rows_{name}", [P, 2, 1024], offset + 12 * K))

        C_ROWS = at("c_rows", [P, 4, 1024], ARENA + 80 * K)
        AREA_A = (at("ada_junk_a", [P, 1024], ARENA + 68 * K), at("ada_ring_a", [P, 2, 1024], ARENA + 72 * K),
                  C_ROWS[:, 0:2, :])
        AREA_B, AREA_E, AREA_F = (ada_area("b", H_AT), ada_area("e", ARENA + 44 * K), ada_area("f", ARENA + 64 * K))
        AREA_G = (at("ada_junk_g", [P, 1024], 48 * K), at("ada_ring_g", [P, 2, 1024], 52 * K),
                  at("ada_rows_g", [P, 2, 1024], ARENA + 88 * K))
        ADA_RAW = at("ada_first", [P, ADA_FIRST, 1024], ARENA)

        QK = at("ret_qk_sb", [P, 16, TOK], ARENA)
        RV = at("ret_v_sb", [P, 4, 2048], ARENA + 32 * K)
        RG = at("ret_gate", [P, 16, TOK], ARENA + 64 * K)
        ROPE = at("ret_rope", [P, 2, 2, LAT], ARENA + 64 * K)
        DECAY_E = at("ret_dist", [P, 6, 512], H_AT)
        DECAY_D = at("ret_decay", [P, 2, 2, 512], H_AT + 12 * K)
        ATT = at("ret_att", [P, 6, LAT], H_AT + 20 * K)
        ON = at("ret_on", [P, 2, 512], H_AT + 26 * K)
        RSTAT = at("ret_stat", [P, 32], H_AT + 30 * K)
        LG = at("log_gamma", [P, 8], H_AT + 30 * K + 256)
        YHI = at("ret_y_hi", [P, 16, TOK], ARENA, F32R)
        YLO = at("ret_y_lo", [P, 16, TOK], ARENA + 32 * K, F32R)
        FHI = at("ffn_hi", [P, FFN_C, TOK], ARENA, F32R)
        FLO = at("ffn_lo", [P, FFN_C, TOK], ARENA + FFN_C * TOK * 4, F32R)
        FHI1 = at("ffn1_hi", [P, FFN_C, LAT], ARENA, F32R)
        FLO1 = at("ffn1_lo", [P, FFN_C, LAT], ARENA + FFN_C * LAT * 4, F32R)
        DQ = at("diff_q", [P, 8, LAT], ARENA)
        DK = at("diff_k", [P, 8, TOK], ARENA + 8 * K)
        DV = at("diff_v", [P, 4, 1024], ARENA + 24 * K)
        DO = at("diff_o", [P, 8, LAT], ARENA + 40 * K)
        DOHI = at("diff_o_hi", [P, 8, LAT], ARENA + 48 * K, F32R)
        DOLO = at("diff_o_lo", [P, 8, LAT], ARENA + 56 * K, F32R)
        DTAB = at("diff_tab", [P, 768], ARENA + 64 * K)
        D_COS, D_SIN = DTAB[:, 0:LAT], DTAB[:, LAT:2 * LAT]
        D_BLOCK, D_ROT = DTAB[:, 512:640], DTAB[:, 640:768]
        DRAWB = at("diff_raw", [P, 4, TOK], ARENA + 68 * K)
        DSQ = at("diff_sq", [P, 2, TOK], ARENA + 76 * K)
        DRST = at("diff_rst", [P, 2, TOK], ARENA + 80 * K)
        DRT = at("diff_rt", [P, LAT], ARENA + 84 * K)
        DE = at("diff_e", [P, 2, 2, TOK], ARENA + 68 * K)
        DP = at("diff_p", [P, 2, TOK], ARENA + 76 * K)
        DPT = at("diff_pt", [P, 2, TOK], ARENA + 80 * K)
        DLAM = at("diff_lam", [P, 256], ARENA + 86 * K)
        DCOL = at("diff_col", [P, 64], ARENA + 88 * K)
        CIN = at("conv_in", [P, 8, CONV_IN], ARENA)
        CACC = at("conv_acc", [P, 2, CONV_OUT], ARENA + 24 * K)
        CZ = at("conv_z", [P, 8, TOK], ARENA + 32 * K)
        MHI = at("mlp_hi", [P, MLP_HALF_C, TOK], ARENA, F32R)
        MLO = at("mlp_lo", [P, MLP_HALF_C, TOK], ARENA + 32 * K, F32R)
        XMHI = at("xm_hi", [P, MLC, TOK], ARENA, F32R)
        XMLO = at("xm_lo", [P, MLC, TOK], ARENA + 32 * K, F32R)
        MZ = at("ml_z", [P, MLC, LAT], ARENA + 64 * K)
        MV = at("ml_v", [P, 4, 2048], H_AT)
        BO = at("ml_b_o", [P, 4096], ARENA + 64 * K)
        MOG = at("ml_o_grp", [P, 2, 2, 1024], ARENA + 80 * K)
        XCL = at("ml_xc_lat", [P, MLC, LAT], ARENA + 64 * K)
        MQ = at("ml_q", [P, MLC, LAT], ARENA + 80 * K)
        MQC = at("ml_q_ctx", [P, 8, LAT], TMP_AT)
        XC = at("ml_xc", [P, MLC, TOK], H_AT)
        MK = at("ml_k", [P, MLC, TOK], H_AT)
        MV2 = at("ml_v2", [P, 4, 2048], ARENA)
        MH = at("ml_h", [P, 2, 2, 2048], ARENA + 32 * K)
        ROWS = at("ml_rows", [4, 16, 512], ARENA + 32 * K)
        MPTS = [at("ml_p_f", [P, 4, LAT], TMP_AT), at("ml_p_b", [P, 4, LAT], TMP_AT + 4 * K)]

        def MPT(d):
            return MPTS[d][:, :, :]
        MO2 = at("ml_o2", [P, 2, 4096], H_AT)
        MZ2 = at("ml_z2", [P, MLC, LAT], ARENA + 80 * K)
        MYHI = at("ml_y_hi", [P, MLC, LAT], ARENA, F32R)
        MYLO = at("ml_y_lo", [P, MLC, LAT], ARENA + 16 * K, F32R)

        M_PAD, M_ACC = TMP[:, 0:ML_IN], TMP[:, 520:520 + ML_OUT]
        COLS_AT = 4 * 512
        M_COLS, M_TRI = TMP[:, COLS_AT:COLS_AT + 48], TMP[:, COLS_AT + 256:COLS_AT + 512]
        M_DEN, M_NEG = TMP[:, COLS_AT + 48:COLS_AT + 49], TMP[:, COLS_AT + 49:COLS_AT + 50]
        GN_STATS, GN_AGGR = TMP[:, COLS_AT + 64:COLS_AT + 112], TMP[:, COLS_AT + 112:COLS_AT + 128]
        GN_VAR, GN_RSTD = TMP[:, COLS_AT + 128:COLS_AT + 136], TMP[:, COLS_AT + 136:COLS_AT + 144]
        GN_NMR = TMP[:, COLS_AT + 144:COLS_AT + 152]
        LS_RET = [TMP[:, COLS_AT + 8 * i:COLS_AT + 8 * i + 8] for i in range(5)]

        z_spill = nc.dram_tensor("z_spill", (P, MLC, LAT), F32).ap()
        v_spill = nc.dram_tensor("v_spill", (P, 4, 2048), F32).ap()
        c_spill = nc.dram_tensor("c_spill", (P, 4, 1024), F32).ap()
        x_spill = nc.dram_tensor("x_spill", (P, DC, TOK), F32).ap()
        o_spill = nc.dram_tensor("o_spill", (P, 2, 4096), F32).ap()

        PS = [ctx.enter_context(nc.psum_tensor(f"bank{i}", [P, 512], F32)) for i in range(8)]

        sems = {}

        def S(name):
            if name not in sems:
                sems[name] = ctx.enter_context(nc.semaphore(name))
            return sems[name]

        raw_full = [S(f"raw_full{s}") for s in range(SLOTS)]
        ada_full = [S(f"ada_full{s}") for s in range(2)]

        def vec(name, c=0, n=1):
            return VECS[:, VEC[name] + c:VEC[name] + c + n]

        def mod(layer, chunk, c, stream):
            a = layer * 2 * ADA_TILES + (chunk * DC + c) * 2 + stream
            return MOD[:, a:a + 1]

        STREAMS = ((0, slice(0, LAT)), (1, slice(LAT, TOK)))

        def streams(T):
            return STREAMS[:T // LAT]

        def tmp(i, n=512):
            return TMP[:, 512 * i:512 * i + n]

        def raw_full_value(n, slot):
            return 4 * (n - slot) + 16

        def tiles(eng, total, body, f):
            n = total // body
            if n > 1:
                with eng.Fori(0, n) as i:
                    for s in range(body):
                        f(i * body + s, i, s)
            else:
                for s in range(n * body):
                    f(s, 0, s)
            for s in range(total - n * body):
                f(n * body + s, n, s)

        class Chain:

            def __init__(self, eng, sem):
                self.eng, self.sem, self.at = eng, sem, 0

            def __call__(self, ins):
                self.at = self.at + 1
                ins.then_inc(self.sem, 1)
                self.eng.wait_ge(self.sem, self.at)

        block = ctx.enter_context(nc.Block())

        @block.sync
        def _(sp):
            sp.dma_start(C_ROWS[:, 0:2, :], c_rows_d[:, 0:2, :]).then_inc(S("c_rows_in"), 16)
            for n in range(ADA_FIRST):
                sp.dma_start(ADA_RAW[:, n, :], ada[n]).then_inc(S(f"ada_first{n // DC}"), 16)
            for n in range(SLOTS):
                sp.dma_start(RAW[:, n, :], weights[n]).then_inc(raw_full[n], 16)
            sp.dma_start(C_ROWS[:, 2:4, :], c_rows_d[:, 2:4, :]).then_inc(S("c_rows2_in"), 16)
            for n in range(SLOTS, SLOTS + LOOKAHEAD):
                sp.wait_ge(S("w_lo_done"), n + 1 - SLOTS)
                sp.dma_start(RAW[:, n % SLOTS, :], weights[n]).then_inc(raw_full[n % SLOTS], 16)

            def load_ada(g, slot, area):
                sp.dma_start(area[1][:, slot, :], ada[g + ADA_FIRST]).then_inc(ada_full[slot], 16)

            def rows_and_ada(g, layer, area):
                first = 0 if layer < 2 else 2
                sp.wait_ge(S("ada_used"), g)
                sp.dma_start(area[2][:, :, :], c_spill[:, first:first + 2, :]).then_inc(S("c_rows_back"), 16)
                for slot in range(2):
                    load_ada(g + slot, slot, area)

            def load_phase(ph, n_ada=0, g0=0, area=None, goes_on=False, at_tile=0):
                n0 = FIRST[ph] + SLOTS + LOOKAHEAD + at_tile
                total = COUNT[ph] - at_tile - (SLOTS if ph == PHASES[-1][0] else 0)
                if ph == "ffn0_in" and not at_tile:
                    total = n_ada
                paired = n_ada if goes_on or not n_ada else n_ada - 4

                def step(t, s, with_ada):
                    slot = (n0 + s) % SLOTS
                    sp.wait_ge(S("w_lo_done"), t + (n0 + 1 - SLOTS))
                    sp.dma_start(RAW[:, slot, :], weights[t + n0]).then_inc(raw_full[slot], 16)
                    if with_ada:
                        sp.wait_ge(S("ada_used"), t + (g0 + 1))
                        load_ada(t + (g0 + 2), s % 2, area)

                tiles(sp, paired, 4, lambda t, i, s: step(t, s, True))
                for t in range(paired, n_ada):
                    step(t, t, t < n_ada - 2)
                tiles(sp, total - n_ada, 4, lambda t, i, s: step(t + n_ada, s + n_ada, False))

            for slot in range(2):
                load_ada(slot, slot, AREA_A)
            load_phase("ret_qk", 16, 0, AREA_A, goes_on=True)
            sp.wait_ge(S("silu_c_done"), 2)
            sp.dma_start(c_spill, C_ROWS[:, :, :]).then_inc(S("spilled"), 16)
            load_phase("ret_v", 16, 16, AREA_A)
            load_phase("ret_g")
            sp.wait_ge(S("spilled"), 16)
            sp.wait_ge(S("ret_y_done"), 16)
            rows_and_ada(32, 1, AREA_B)
            load_phase("ret_out", 16, 32, AREA_B)
            sp.wait_ge(S("x_upd"), DC)
            sp.dma_start(x_spill, X[:, :, :]).then_inc(S("spilled"), 16)
            sp.wait_ge(S("spilled"), 32)
            sp.wait_ge(S("raw_done"), 2 * DC)
            rows_and_ada(48, 1, AREA_G)
            load_phase("ffn0_in", 32, 48, AREA_G)
            rows_and_ada(80, 3, AREA_G)
            load_phase("ffn0_in", 12, 80, AREA_G, at_tile=32)
            sp.wait_ge(S("tile_done"), FIRST["ffn0_out"])
            rows_and_ada(92, 3, AREA_B)
            sp.dma_start(X[:, :, :], x_spill).then_inc(S("x_back"), 16)
            load_phase("ffn0_out", 22, 92, AREA_B)
            load_phase("diff_qk")
            load_phase("diff_v")
            load_phase("diff_out")
            load_phase("ffn1_in")
            rows_and_ada(114, 3, AREA_E)
            load_phase("ffn1_out", 6, 114, AREA_E)
            load_phase("pw1")
            load_phase("pw2")
            rows_and_ada(120, 3, AREA_F)
            load_phase("mlp0a_in", 16, 120, AREA_F, goes_on=True)
            load_phase("mlp0a_out", 16, 136, AREA_F, goes_on=True)
            load_phase("mlp0b_in", 16, 152, AREA_F, goes_on=True)
            load_phase("mlp0b_out", 8, 168, AREA_F)
            for ph, _ in PHASES[PHASES.index(("up_x", 16)):]:
                load_phase(ph)
            sp.wait_ge(S("x_final"), DC)
            sp.dma_start(out_d, X[:, :, 0:LAT]).then_inc(S("out_stored"), 16)
            sp.wait_ge(S("out_stored"), 16)

        @block.gpsimd
        def _(pool):
            pool.dma_start(VECS[:, :], vecs_d).then_inc(S("vecs_in"), 16)
            pool.dma_start(X[:, :, :], x_t).then_inc(S("x_in"), 16)
            pool.dma_start(IDENT[:, :], consts_d[0]).then_inc(S("consts_in"), 16)
            pool.dma_start(ONES[:, :], consts_d[1]).then_inc(S("consts_in"), 16)
            pool.dma_start(ROPE[:, :, :, :], ret_rope_d).then_inc(S("consts_in"), 16)

            def lo_split(m, T):
                for c in range(DC):
                    pool.wait_ge(S("h_hi_done"), m * DC + c + 1)
                    pool.tensor_tensor(HLO[:, c, 0:T], tmp(c % 2, T), HHI[:, c, 0:T].bitcast(F32), SUB)\
                        .then_inc(S("h_lo_done"), 1)

            lo_split(0, TOK)
            pool.wait_ge(S("tile_done"), FIRST["ret_g"] + COUNT["ret_g"])
            pool.dma_start(DECAY_E[:, :, :], ret_decay_d).then_inc(S("decay_in"), 16)
            lo_split(1, TOK)
            lo_split(2, TOK)
            pool.wait_ge(S("tile_done"), FIRST["ffn0_out"] + COUNT["ffn0_out"])
            pool.dma_start(DTAB[:, :], diff_tab_d).then_inc(S("diff_tab_in"), 16)
            pool.dma_start(DLAM[:, :], lam_d).then_inc(S("diff_tab_in"), 16)
            for h in range(DIFF_HEADS):
                pool.wait_ge(S("do_hi_done"), h + 1)
                pool.tensor_tensor(DOLO[:, h, :], DO[:, h, :], DOHI[:, h, :].bitcast(F32), SUB)\
                    .then_inc(S("do_lo_done"), 1)
            lo_split(3, LAT)
            pool.wait_ge(S("h_lo_done"), 3 * DC)
            pool.dma_start(X[:, :, LAT:TOK], ctx2_t).then_inc(S("ctx2_in"), 16)
            pool.wait_ge(S("tile_done"), FIRST["ffn1_out"] + COUNT["ffn1_out"])
            pool.memset(CIN[:, :, :], 0.0).then_inc(S("conv_zero"), 1)
            lo_split(4, TOK)
            lo_split(5, TOK)
            lo_split(6, TOK)
            pool.dma_start(X[:, 0:3, LAT:TOK], w_gate_d).then_inc(S("gate_w_in"), 16)
            pool.wait_ge(S("z_free"), 8 + MLC)
            pool.dma_start(z_spill, MZ[:, :, :]).then_inc(S("z_spilled"), 16)
            pool.wait_ge(S("z_spilled"), 16)
            pool.dma_start(BO[:, :], b_o_d).then_inc(S("b_o_in"), 16)
            pool.wait_ge(S("v_done"), 16)
            pool.dma_start(v_spill, MV[:, :, :]).then_inc(S("v_spilled"), 16)
            for g in range(4):
                pool.wait_ge(S("o_done"), 4 * (g + 1))
                pool.dma_start(o_spill[:, :, 1024 * g:1024 * (g + 1)], MOG[:, g % 2, :, :])\
                    .then_inc(S(f"o_spilled{g % 2}"), 16)
            pool.wait_ge(S("tile_done"), FIRST["ml_k"] + COUNT["ml_k"])
            pool.wait_ge(S("v_spilled"), 16)
            pool.dma_start(MV2[:, :, :], v_spill).then_inc(S("v_back"), 16)
            pool.dma_start(ROWS[0:4, 10, :], sel_d).then_inc(S("v_back"), 16)
            pool.wait_ge(S("rows_done"), 2)
            pool.dma_start(tmp(4)[:, 256:512], consts_d[2:4].rearrange("a p n -> p a n")).then_inc(S("tri_in"), 16)
            pool.wait_ge(S("ml_scores_done"), ML_HEADS)
            for g in range(2):
                pool.wait_ge(S(f"o_spilled{g}"), 32)
            pool.dma_start(MO2[:, :, :], o_spill).then_inc(S("o_back"), 16)
            pool.dma_start(MZ2[:, :, :], z_spill).then_inc(S("o_back"), 16)
            lo_split(7, LAT)

        @block.tensor
        def _(pe):
            mm = nc.tensor.matmul

            def split_mm(out, lhs, rhs, start, stop):
                mm(out, lhs[0], rhs[0], start=start, stop=False)
                mm(out, lhs[0], rhs[1], start=False, stop=False)
                return mm(out, lhs[1], rhs[0], start=False, stop=stop)

            def w(slot, a, n):
                return WHI[:, slot, a:a + n], WLO[:, slot, a:a + n]

            def gemm_rows(ph, T, m, free, body=8):
                g0, kinds = FIRST[ph], len(free)
                for name in free:
                    pe.sem_inc(S(name), 8 // kinds)

                def tile(t, i, s):
                    slot, bank = (g0 + s) % SLOTS, s % 8
                    pe.wait_ge(S("w_lo_done"), t + (g0 + 1))
                    pe.wait_ge(S(free[s % kinds]), i * (body // kinds) + (s // kinds + 1))
                    for k in range(DC):
                        if s == 0:
                            pe.wait_ge(S("h_lo_done"), m * DC + k + 1)
                        last = split_mm(PS[bank][:, 0:T], w(slot, k * P, P), (HHI[:, k, 0:T], HLO[:, k, 0:T]),
                                        k == 0, k == DC - 1)
                    last.then_inc(S("tile_done"), 1)

                tiles(pe, COUNT[ph], body, tile)

            def gemm_cols(ph, T, hi, lo, ready, ready_base):
                g0, n = FIRST[ph], COUNT[ph]
                for k in range(n):
                    slot = (g0 + k) % SLOTS
                    pe.wait_ge(S("w_lo_done"), g0 + k + 1)
                    pe.wait_ge(S(ready), ready_base + k + 1)
                    for o in range(DC):
                        last = split_mm(PS[o][:, 0:T], w(slot, o * P, P), (hi[:, k, 0:T], lo[:, k, 0:T]),
                                        k == 0, k == n - 1)
                        if k == n - 1 and o < DC - 1:
                            last.then_inc(S("bank_done"), 1)
                    last.then_inc(S("tile_done"), 1)

            def gemm_tokens(ph, group, n_k, hi, lo, n_t, bank0, first_wait):
                g0 = FIRST[ph] + group * n_k
                for k in range(n_k):
                    slot = (g0 + k) % SLOTS
                    pe.wait_ge(S("w_lo_done"), g0 + k + 1)
                    if k == 0:
                        first_wait()
                    for t in range(n_t):
                        tok = slice(t * P, (t + 1) * P)
                        for half in range(2):
                            last = split_mm(PS[bank0 + 2 * t + half][:, :], (hi[:, k, tok], lo[:, k, tok]),
                                            w(slot, half * 512, 512), k == 0, k == n_k - 1)
                            if k == n_k - 1 and (t, half) != (n_t - 1, 1):
                                last.then_inc(S("bank_done"), 1)
                    last.then_inc(S("tile_done"), 1)

            def square_sums(q, T, bank):
                for c in range(DC):
                    pe.wait_ge(S("sq_done"), q * DC + c + 1)
                    mm(PS[bank][:, 0:T], ONES[:, :], tmp(3 + c % 2, T), start=c == 0, stop=c == DC - 1)\
                        .then_inc(S("sq_used"), 1)

            def feature_sums(z, T, ready, ready_base, bank):
                for c in range(DC):
                    pe.wait_ge(S(ready), ready_base + c + 1)
                    last = mm(PS[bank][:, 0:T], ONES[:, :], z[:, c, 0:T], start=c == 0, stop=c == DC - 1)
                last.then_inc(S("ln_sum_done"), 1)

            pe.wait_ge(S("consts_in"), 48)
            square_sums(0, TOK, 0)
            pe.wait_ge(S("var_done"), 1)
            gemm_rows("ret_qk", TOK, 0, ["qk_free"], 16)
            for grp in range(2):
                def rv_free(grp=grp):
                    if grp == 0:
                        pe.wait_ge(S("qk_free"), 8 + 16)
                    else:
                        pe.wait_ge(S("rv_free"), 8)
                gemm_tokens("ret_v", grp, 8, HHI, HLO, 4, 0, rv_free)
            pe.wait_ge(S("rv_free"), 16)
            gemm_rows("ret_g", TOK, 0, ["rg_free"])
            pe.wait_ge(S("rg_free"), 8 + 16)

            pe.wait_ge(S("qk_rope_done"), 16)
            for h in range(RET_HEADS):
                if h:
                    pe.wait_ge(S("att_done"), 3 * h)
                for b, (key0, q0) in enumerate(((0, 0), (LAT, 0), (LAT, LAT))):
                    for j in range(2):
                        for d in range(2):
                            last = mm(PS[b][:, j * LAT:(j + 1) * LAT],
                                      QK[:, 8 + 2 * h + d, key0 + j * P:key0 + (j + 1) * P],
                                      QK[:, 2 * h + d, q0:q0 + LAT], start=d == 0, stop=d == 1)
                    last.then_inc(S("score_done"), 1)

                def ret_values(t):
                    pe.wait_ge(S("att_done"), 3 * h + (2 if t < 2 else 3))
                    if h:
                        pe.wait_ge(S("on_done"), 4 * (h - 1) + t + 1)
                    i0 = (t % 2) * P
                    keys = ((0, 0), (1, 1), (2, 2), (3, 3)) if t < 2 else ((4, 2), (5, 3))
                    for n, (a, v) in enumerate(keys):
                        last = mm(PS[3 + t][:, :], ATT[:, a, i0:i0 + P], RV[:, v, 512 * h:512 * (h + 1)],
                                  start=n == 0, stop=n == len(keys) - 1)
                    last.then_inc(S("ret_o_done"), 1)

                for t in range(4):
                    ret_values(t)
                for t in range(4):
                    pe.wait_ge(S("on_done"), 4 * h + t + 1)
                    if h or t:
                        pe.wait_ge(S("ret_y_done"), 4 * h + t)
                    for f in range(4):
                        last = nc.tensor.transpose(PS[7][:, f * P:(f + 1) * P], ON[:, t % 2, f * P:(f + 1) * P],
                                                   IDENT[:, :])
                    last.then_inc(S("on_t_done"), 1)
            pe.wait_ge(S("ret_y_done"), 16)
            gemm_cols("ret_out", TOK, YHI, YLO, "ret_y_lo_done", 0)

            def ffn(layer, T, q, m, xbase, in_free):
                pe.wait_ge(S("x_upd"), xbase)
                square_sums(q, T, 0)
                pe.wait_ge(S("var_done"), q + 1)
                gemm_rows(f"ffn{layer}_in", T, m, in_free)
                for name in in_free:
                    pe.wait_ge(S(name), 4 + 22)
                fhi, flo = (FHI, FLO) if layer == 0 else (FHI1, FLO1)
                gemm_cols(f"ffn{layer}_out", T, fhi, flo, "f_lo_done", FFN_C * layer)

            ffn(0, TOK, 1, 1, 8, ["ffn0_a_free", "ffn0_g_free"])

            pe.wait_ge(S("x_upd"), 16)
            square_sums(2, TOK, 0)
            pe.wait_ge(S("var_done"), 3)
            pe.wait_ge(S("diff_tab_in"), 32)
            g0 = FIRST["diff_qk"]
            for t in range(16 + 3):
                if t < 16:
                    T = TOK if t < 8 else LAT
                    slot = (g0 + t) % SLOTS
                    pe.wait_ge(S("w_lo_done"), g0 + t + 1)
                    if t >= 4:
                        pe.wait_ge(S("dqk_raw"), t - 3)
                    for k in range(DC):
                        if t == 0:
                            pe.wait_ge(S("h_lo_done"), 2 * DC + k + 1)
                        last = split_mm(PS[t % 4][:, 0:T], w(slot, k * P, P), (HHI[:, k, 0:T], HLO[:, k, 0:T]),
                                        k == 0, k == DC - 1)
                    last.then_inc(S("tile_done"), 1)
                u = t - 1
                if 0 <= u < 16:
                    T = TOK if u < 8 else LAT
                    pe.wait_ge(S("dqk_sq"), u + 1)
                    if u >= 2:
                        pe.wait_ge(S("dqk_var"), u - 1)
                    mm(PS[4 + u % 2][:, 0:T], D_BLOCK, DSQ[:, u % 2, 0:T], start=True, stop=True)\
                        .then_inc(S("dqk_stat"), 1)
                u = t - 3
                if 0 <= u < 16:
                    pe.wait_ge(S("dqk_norm"), u + 1)
                    if u >= 2:
                        pe.wait_ge(S("dqk_rope"), u - 1)
                    src = DK[:, u, 0:LAT] if u < 8 else DQ[:, u - 8, :]
                    mm(PS[6 + u % 2][:, 0:LAT], D_ROT, src, start=True, stop=True).then_inc(S("dqk_rot"), 1)

            def dv_free():
                pe.wait_ge(S("dqk_rope"), 16)
            gemm_tokens("diff_v", 0, 8, HHI, HLO, 4, 0, dv_free)
            pe.wait_ge(S("dv_free"), 8)
            for u in range(16 + 2):
                if u < 16:
                    h, t = u // 2, u % 2
                    if u >= 2:
                        pe.wait_ge(S("d_exp"), 2 * (u - 1))
                    for m in range(2):
                        part = slice(64 * m, 64 * (m + 1))
                        mm(PS[2 * (u % 2) + m][:, :], DQ[part, h, t * P:(t + 1) * P], DK[part, h, :],
                           start=True, stop=True).then_inc(S("d_score"), 1)
                a = u - 1
                if 0 <= a < 16:
                    pe.wait_ge(S("d_p"), a + 1)
                    if a >= 2:
                        pe.wait_ge(S("d_pt"), a - 1)
                    for c in range(4):
                        last = nc.tensor.transpose(PS[4 + a % 2][:, c * P:(c + 1) * P],
                                                   DP[:, a % 2, c * P:(c + 1) * P], IDENT[:, :])
                    last.then_inc(S("d_tr"), 1)
                b = u - 2
                if 0 <= b < 16:
                    h, t = b // 2, b % 2
                    pe.wait_ge(S("d_pt"), b + 1)
                    if h >= 2:
                        pe.wait_ge(S("d_ocopy"), h - 1)
                    for c in range(4):
                        last = mm(PS[6 + h % 2][:, t * P:(t + 1) * P], DV[:, c, h * P:(h + 1) * P],
                                  DPT[:, b % 2, c * P:(c + 1) * P], start=c == 0, stop=c == 3)
                    last.then_inc(S("d_pv"), 1)
            for h in range(DIFF_HEADS):
                pe.wait_ge(S("do_sq"), h + 1)
                if h >= 2:
                    pe.wait_ge(S("do_var"), h - 1)
                mm(PS[h % 2][:, 0:LAT], ONES[:, :], tmp(3 + h % 2, LAT), start=True, stop=True)\
                    .then_inc(S("do_stat"), 1)
            pe.wait_ge(S("do_var"), 8)
            gemm_cols("diff_out", LAT, DOHI, DOLO, "do_lo_done", 0)
            ffn(1, LAT, 3, 3, 24, ["ffn1_a_free", "ffn1_g_free"])

            pe.wait_ge(S("x_upd"), 32)
            gemm_rows("pw1", TOK, 4, ["pw1_gate_free", "pw1_a_free"], 16)
            pe.wait_ge(S("pw1_a_free"), 4 + 8)
            feature_sums(CZ, TOK, "conv_z_done", 0, 0)
            square_sums(4, TOK, 1)
            pe.wait_ge(S("var_done"), 5)
            gemm_cols("pw2", TOK, HHI, HLO, "cz_lo_done", 0)

            def mlp(j, T, q, m, xbase):
                feature_sums(X, T, "x_upd", xbase, 0)
                square_sums(q, T, 1)
                pe.wait_ge(S("var_done"), q + 1)
                for n, half in enumerate("ab"):
                    if n:
                        pe.wait_ge(S("x_upd"), xbase + 16)
                    gemm_rows(f"mlp{j}{half}_in", T, m, [f"mlp{j}{half}_free"])
                    pe.wait_ge(S(f"mlp{j}{half}_free"), 8 + 16)
                    gemm_cols(f"mlp{j}{half}_out", T, MHI, MLO, f"mlp{j}{half}_free", 8)
                feature_sums(X, T, "x_upd", xbase + 16, 0)
                square_sums(q + 1, T, 1)
                pe.wait_ge(S("var_done"), q + 2)

            mlp(0, TOK, 5, 5, 32 + 0)

            gemm_rows("up_x", TOK, 6, ["up_free"])
            pe.wait_ge(S("up_free"), 8 + 16)
            gemm_rows("up_z", LAT, 6, ["z_free"])
            pe.wait_ge(S("z_free"), 8 + 16)
            for grp in range(2):
                def mv_free(grp=grp):
                    if grp:
                        pe.wait_ge(S("v_done"), 8)
                gemm_tokens("ml_v", grp, 16, XMHI, XMLO, 4, 0, mv_free)
            pe.wait_ge(S("v_done"), 16)
            pe.wait_ge(S("gate_w_in"), 16)

            def gate_part(part, f):
                return X[:, part, LAT + 16 * f:LAT + 16 * f + 16]

            for f in range(MLC + 1):
                if f < MLC:
                    if f >= 2:
                        pe.wait_ge(S("vt_done"), f - 1)
                    for t in range(4):
                        last = nc.tensor.transpose(PS[1 + f % 2][:, t * P:(t + 1) * P],
                                                   MV[:, t, f * P:(f + 1) * P], IDENT[:, :])
                    last.then_inc(S("vt_tr"), 1)
                if f:
                    pe.wait_ge(S("vt_done"), f)
                    last = mm(PS[0][0:16, :], gate_part(2, f - 1), tmp((f - 1) % 2), start=f == 1, stop=f == MLC)
                    last.then_inc(S("gate_mm"), 1)
            for grp in range(4):
                def mo_free(grp=grp):
                    if grp == 0:
                        pe.wait_ge(S("gate_acc"), 1)
                    elif grp >= 2:
                        pe.wait_ge(S("o_add"), 4 * (grp - 1))
                gemm_tokens("ml_o", grp, 16, XMHI, XMLO, 2, 4 * (grp % 2), mo_free)
            pe.wait_ge(S("o_add"), 16)

            def gemm_inner(ph, grp, x_base, kdone):
                g0 = FIRST[ph] + 16 * grp
                for k in range(MLC):
                    slot = (g0 + k) % SLOTS
                    pe.wait_ge(S("w_lo_done"), g0 + k + 1)
                    pe.wait_ge(S("xc_lo_done"), k + 1)
                    for o in range(DC):
                        last = split_mm(PS[o][:, :], w(slot, o * P, P), (XMHI[:, k, :], XMLO[:, k, :]),
                                        k == 0, k == MLC - 1)
                        if k == MLC - 1 and o < DC - 1:
                            last.then_inc(S("bank_done"), 1)
                    last.then_inc(S("tile_done"), 1)
                pe.wait_ge(S(kdone), 8 * (grp + 1))

            for grp in range(2):
                gemm_inner("ml_q", grp, 0, "q_done")
                for c in range(DC):
                    wg = gate_part(0, 8 * grp + c)
                    mm(PS[0][0:16, 0:LAT], wg, MQ[:, 8 * grp + c, :], start=c == 0, stop=c == DC - 1)\
                        .then_inc(S("gate_mm"), 1)
                for c in range(DC):
                    wg = gate_part(0, 8 * grp + c)
                    mm(PS[0][0:16, LAT:TOK], wg, MQC[:, c, :], start=c == 0, stop=c == DC - 1)\
                        .then_inc(S("gate_mm"), 1)
                pe.wait_ge(S("gate_acc"), 2 + grp)
            for grp in range(2):
                gemm_inner("ml_k", grp, 0, "k_done")
                for c in range(DC):
                    mm(PS[0][0:16, :], gate_part(1, 8 * grp + c), MK[:, 8 * grp + c, :], start=c == 0, stop=c == DC - 1)\
                        .then_inc(S("gate_mm"), 1)
                pe.wait_ge(S("gate_acc"), 4 + grp)

            for g in range(4):
                mm(PS[g][0:4, :], IDENT[0:16, 4 * g:4 * g + 4], tmp(4)[0:16, :], start=True, stop=True)\
                    .then_inc(S("gate_rows"), 1)
            pe.wait_ge(S("rows_done"), 2)
            for d in range(2):
                for j in range(6):
                    row = ROWS[0:4, 12 + d, j * P:(j + 1) * P] if j < 4 else \
                        ROWS[0:4, 14 + d, (j - 4) * P:(j - 3) * P]
                    last = mm(PS[4][:, (d * 6 + j) * 4:(d * 6 + j) * 4 + 4], row, IDENT[0:4, 0:4],
                              start=True, stop=True)
            last.then_inc(S("ml_cols"), 1)
            pe.wait_ge(S("v_back"), 32)
            for d in range(2):
                for h in range(ML_HEADS):
                    n = d * 4 + h
                    if n >= 2:
                        pe.wait_ge(S("rb_copy"), n - 1)
                    mm(PS[5 + n % 2][:, 0:LAT], ROWS[0:4, 10, h * P:(h + 1) * P], ROWS[0:4, 14 + d, LAT:2 * LAT],
                       start=True, stop=True).then_inc(S("rb_mm"), 1)
            pe.wait_ge(S("rb_copy"), 8)
            pe.wait_ge(S("ml_cols_copy"), 1)
            for h in range(ML_HEADS):
                if h:
                    pe.wait_ge(S("ml_p"), 4 * h)
                for j in range(4):
                    for d in range(4):
                        last = mm(PS[j // 2][:, (j % 2) * LAT:(j % 2 + 1) * LAT],
                                  MK[:, 4 * h + d, j * P:(j + 1) * P], MQ[:, 4 * h + d, :],
                                  start=d == 0, stop=d == 3)
                last.then_inc(S("ml_scores_done"), 1)
                for d in range(2):
                    pe.wait_ge(S("ml_p"), 4 * h + 2 * d + 2)
                    for t in range(2):
                        n = h * 4 + d * 2 + t
                        if n >= 2:
                            pe.wait_ge(S("ml_h_done"), n - 1)
                        keys = [j for j in range(4) if j >= 2 or (j <= t if d == 0 else j >= t)]
                        for i, j in enumerate(keys):
                            p_t = MPT(d)[:, j, t * P:(t + 1) * P]
                            mm(PS[4 + n % 2][:, 0:1], p_t, ONES[:, 0:1], start=i == 0, stop=i == len(keys) - 1)
                        for i, j in enumerate(keys):
                            p_t = MPT(d)[:, j, t * P:(t + 1) * P]
                            last = mm(PS[6 + n % 2][:, :], p_t, MV2[:, j, 512 * h:512 * (h + 1)],
                                      start=i == 0, stop=i == len(keys) - 1)
                        last.then_inc(S("ml_num"), 1)
            for f in range(MLC):
                pe.wait_ge(S("hn_done"), 8)
                if f >= 2:
                    pe.wait_ge(S("ml_y_done"), f - 1)
                for t in range(2):
                    last = nc.tensor.transpose(PS[f % 2][:, t * P:(t + 1) * P], MH[:, 0, t, f * P:(f + 1) * P],
                                               IDENT[:, :])
                last.then_inc(S("hn_tr"), 1)
            pe.wait_ge(S("ml_y_done"), 16)
            gemm_cols("down", LAT, MYHI, MYLO, "ml_y_lo", 0)
            mlp(1, LAT, 7, 7, 32 + 8 + 16)


        @block.scalar
        def _(act):
            def f(out, in_, func, **kw):
                return nc.scalar.activation(out, in_, func, **kw)

            own = Chain(act, S("act_own"))

            def hi(n, slot, first=False):
                act.wait_ge(raw_full[slot], raw_full_value(n, slot))
                if not first:
                    act.wait_ge(S("tile_done"), n - LOOKAHEAD)
                f(WHI[:, slot, :], RAW[:, slot, :], ACT.Copy).then_inc(S("w_hi_done"), 1)

            def hi_ahead(ph, t, s):
                n0 = FIRST[ph] + LOOKAHEAD
                hi(t + n0, (n0 + s) % SLOTS, first=isinstance(t, int) and t + n0 < SLOTS)

            def weights_only(ph):
                tiles(act, COUNT[ph], SLOTS, lambda t, i, s: hi_ahead(ph, t, s))

            def squares(q, T, z, ready, ready_base):
                for c in range(DC):
                    act.wait_ge(S(ready), ready_base + c + 1)
                    if c >= 2:
                        act.wait_ge(S("sq_used"), q * DC + c - 1)
                    f(tmp(3 + c % 2, T), z[:, c, 0:T], ACT.Square).then_inc(S("sq_done"), 1)
                act.wait_ge(S("var_done"), q + 1)
                f(tmp(2, T), tmp(2, T), ACT.Sqrt).then_inc(S("std_done"), 1)

            def h_hi(m, T):
                for c in range(DC):
                    act.wait_ge(S("raw_done"), m * DC + c + 1)
                    f(HHI[:, c, 0:T], tmp(c % 2, T), ACT.Copy).then_inc(S("h_hi_done"), 1)

            def log_sigmoid(q, a, e, u, l):
                act.wait_ge(S("ls_abs"), q + 1)
                f(e, a, ACT.Exp, scale=-1.0).then_inc(S("ls_exp"), 1)
                act.wait_ge(S("ls_u"), q + 1)
                f(l, u, ACT.Ln).then_inc(S("ls_ln"), 1)

            act.wait_ge(S("vecs_in"), 16)
            act.wait_ge(S("c_rows_in"), 16)
            f(C_ROWS[:, 0:2, :], C_ROWS[:, 0:2, :], ACT.Silu).then_inc(S("silu_c_done"), 1)
            act.wait_ge(S("c_rows2_in"), 16)
            f(C_ROWS[:, 2:4, :], C_ROWS[:, 2:4, :], ACT.Silu).then_inc(S("silu_c_done"), 1)
            act.wait_ge(S("x_in"), 16)
            for n in range(LOOKAHEAD):
                hi(n, n, first=True)
            for c in range(DC):
                if c >= 2:
                    act.wait_ge(S("sq_used"), c - 1)
                f(tmp(3 + c % 2), X[:, c, :], ACT.Square).then_inc(S("sq_done"), 1)
            act.wait_ge(S("var_done"), 1)
            f(tmp(2), tmp(2), ACT.Sqrt).then_inc(S("std_done"), 1)
            h_hi(0, TOK)

            for t in range(16):
                hi_ahead("ret_qk", t, t)
            weights_only("ret_v")

            def ret_gate(t, i, s):
                hi_ahead("ret_g", t, s)
                act.wait_ge(S("tile_done"), t + (FIRST["ret_g"] + 1))
                f(RG[:, t, :], PS[s % 8][:, :], ACT.Silu).then_inc(S("rg_free"), 1)
            tiles(act, 16, 8, ret_gate)

            log_sigmoid(0, LS_RET[0], LS_RET[1], LS_RET[2], LS_RET[3])
            act.wait_ge(S("log_gamma_done"), 1)
            act.wait_ge(S("decay_in"), 16)
            for h in range(RET_HEADS):
                if h:
                    act.wait_ge(S("decay_used"), h)
                for n, (table, col) in enumerate(((0, h), (1, 4 + h), (4, h), (5, 4 + h))):
                    last = f(tmp(n), DECAY_E[:, table, :], ACT.Exp, scale=LG[:, col:col + 1])
                last.then_inc(S("decay_exp"), 1)
                for t in range(4):
                    n = 4 * h + t
                    st = 16 * (t % 2)
                    act.wait_ge(S("ret_var"), n + 1)
                    f(RSTAT[:, st + 9:st + 10], RSTAT[:, st + 8:st + 9], ACT.Sqrt).then_inc(S("ret_std"), 1)
                    act.wait_ge(S("ret_nmr"), n + 1)
                    if n >= 2:
                        act.wait_ge(S("on_t_done"), n - 1)
                    f(ON[:, t % 2, :], PS[3 + t][:, :], ACT.Identity, scale=RSTAT[:, st + 10:st + 11],
                      bias=RSTAT[:, st + 11:st + 12]).then_inc(S("on_done"), 1)
            act.wait_ge(S("ret_y_done"), 16)
            for c in range(16):
                f(YHI[:, c, :], RG[:, c, :], ACT.Copy).then_inc(S("ret_y_hi_done"), 1)
            weights_only("ret_out")

            def ffn(layer, T, q, m, x0):
                squares(q, T, X, "x_upd", x0)
                h_hi(m, T)
                ph = f"ffn{layer}_in"
                fhi = FHI if layer == 0 else FHI1

                def tile(t, i, s):
                    hi_ahead(ph, t, s)
                    p = i * 4 + s // 2
                    if s % 2 == 0:
                        act.wait_ge(S("tile_done"), t + (FIRST[ph] + 1))
                        act.wait_ge(S(f"ffn{layer}_g_free"), p + 3)
                        f(tmp(3 + s // 2 % 2, T), PS[s][:, 0:T], ACT.Silu).then_inc(S(f"ffn{layer}_a_free"), 1)
                    else:
                        act.wait_ge(S(f"ffn{layer}_g_free"), p + 5)
                        f(fhi[:, p, 0:T], tmp(s // 2 % 2, T), ACT.Copy).then_inc(S("f_hi_done"), 1)
                tiles(act, COUNT[ph], 8, tile)
                weights_only(f"ffn{layer}_out")

            ffn(0, TOK, 1, 1, 0)

            squares(2, TOK, X, "x_upd", 8)
            h_hi(2, TOK)
            for t in range(16 + 3):
                if t < 16:
                    T = TOK if t < 8 else LAT
                    hi_ahead("diff_qk", t, t)
                    act.wait_ge(S("dqk_raw"), t + 1)
                    if t >= 2:
                        act.wait_ge(S("dqk_stat"), t - 1)
                    f(DSQ[:, t % 2, 0:T], DRAWB[:, t % 4, 0:T], ACT.Square).then_inc(S("dqk_sq"), 1)
                u = t - 1
                if 0 <= u < 16:
                    T = TOK if u < 8 else LAT
                    act.wait_ge(S("dqk_var"), u + 1)
                    f(DRST[:, u % 2, 0:T], DRST[:, u % 2, 0:T], ACT.Sqrt).then_inc(S("dqk_std"), 1)
            weights_only("diff_v")
            act.wait_ge(S("lam_dot"), 1)
            f(DCOL[:, 2:4], DCOL[:, 2:4], ACT.Exp).then_inc(S("lam_exp"), 1)
            scale = DIFF_DH ** -0.5
            for u in range(16 + 1):
                if u < 16:
                    for m in range(2):
                        col = 4 + 2 * (u % 2) + m
                        act.wait_ge(S("d_max"), 2 * u + m + 1)
                        if m == 0 and u >= 2:
                            act.wait_ge(S("d_p"), u - 1)
                        f(DE[:, u % 2, m, :], PS[2 * (u % 2) + m][:, :], ACT.Exp, scale=scale,
                          bias=DCOL[:, col:col + 1], accum_out=DCOL[:, col + 4:col + 5]).then_inc(S("d_exp"), 1)
                a = u - 1
                if 0 <= a < 16:
                    act.wait_ge(S("d_tr"), a + 1)
                    if a >= 2:
                        act.wait_ge(S("d_pv"), a - 1)
                    f(DPT[:, a % 2, :], PS[4 + a % 2][:, :], ACT.Copy).then_inc(S("d_pt"), 1)
            for h in range(DIFF_HEADS + 1):
                if h < DIFF_HEADS:
                    act.wait_ge(S("d_ocopy"), h + 1)
                    if h >= 2:
                        act.wait_ge(S("do_stat"), h - 1)
                    f(tmp(3 + h % 2, LAT), DO[:, h, :], ACT.Square).then_inc(S("do_sq"), 1)
                g = h - 1
                if 0 <= g:
                    act.wait_ge(S("do_var"), g + 1)
                    f(tmp(1 + g % 2, LAT), tmp(1 + g % 2, LAT), ACT.Sqrt).then_inc(S("do_std"), 1)
            for h in range(DIFF_HEADS):
                act.wait_ge(S("do_norm"), h + 1)
                f(DOHI[:, h, :], DO[:, h, :], ACT.Copy).then_inc(S("do_hi_done"), 1)
            weights_only("diff_out")
            ffn(1, LAT, 3, 3, 16)

            h_hi(4, TOK)
            for t in range(16):
                p, bank = t // 2, t % 8
                hi_ahead("pw1", t, t)
                if t % 2 == 0:
                    act.wait_ge(S("tile_done"), FIRST["pw1"] + t + 1)
                    act.wait_ge(S("pw1_a_free"), p + 3)
                    f(tmp(3 + p % 2), PS[bank][:, :], ACT.Sigmoid, bias=vec("b_pw1", 8 + p))\
                        .then_inc(S("pw1_gate_free"), 1)
                else:
                    act.wait_ge(S("conv_acc_done"), p + 1)
                    f(CZ[:, p, 0:LAT].rearrange("p (r w) -> p r w", w=GRID_W),
                      CACC[:, 0, 0:CONV_CTX].rearrange("p (r w) -> p r w", w=ROW_PADDED)[:, :, 0:GRID_W],
                      ACT.Identity, bias=vec("b_dw", p))
                    f(CZ[:, p, LAT:TOK], CACC[:, 0, CONV_CTX:CONV_CTX + CTX], ACT.Identity, bias=vec("b_dw", p))\
                        .then_inc(S("conv_z_done"), 1)
            squares(4, TOK, CZ, "z_centered", 0)
            for c in range(DC):
                act.wait_ge(S("cz_norm"), c + 1)
                if c >= 2:
                    act.wait_ge(S("cz_lo_done"), c - 1)
                own(f(tmp(c % 2), CZ[:, c, :], ACT.Silu, scale=vec("conv_ln_g", c), bias=vec("conv_ln_b", c)))
                f(HHI[:, c, :], tmp(c % 2), ACT.Copy).then_inc(S("cz_hi_done"), 1)
            weights_only("pw2")

            def mlp(j, T, q, m, ln):
                squares(q, T, X, "z_centered", ln * DC)
                h_hi(m, T)
                for n, half in enumerate("ab"):
                    ph, free, done = f"mlp{j}{half}_in", S(f"mlp{j}{half}_free"), 16 * (2 * j + n)

                    def tile(t, i, s):
                        hi_ahead(ph, t, s)
                        act.wait_ge(S("tile_done"), t + (FIRST[ph] + 1))
                        act.wait_ge(free, t + 7)
                        f(tmp(3 + s % 2, T), PS[s][:, 0:T], ACT.Relu).then_inc(S("m_relu_done"), 1)
                        act.wait_ge(S("m_relu_done"), t + (done + 1))
                        f(MHI[:, t, 0:T], tmp(3 + s % 2, T), ACT.Square).then_inc(S("m_hi_done"), 1)
                    tiles(act, 16, 8, tile)
                    weights_only(f"mlp{j}{half}_out")
                squares(q + 1, T, X, "z_centered", (ln + 1) * DC)

            mlp(0, TOK, 5, 5, 1)

            h_hi(6, TOK)

            def up_x(t, i, s):
                hi_ahead("up_x", t, s)
                act.wait_ge(S("tile_done"), t + (FIRST["up_x"] + 1))
                f(XMHI[:, t, :], PS[s][:, :], ACT.Copy).then_inc(S("up_hi_done"), 1)
            tiles(act, 16, 8, up_x)

            def up_z(t, i, s):
                hi_ahead("up_z", t, s)
                act.wait_ge(S("tile_done"), t + (FIRST["up_z"] + 1))
                f(MZ[:, t, :], PS[s][:, 0:LAT], ACT.Silu).then_inc(S("z_free"), 1)
            tiles(act, 16, 8, up_z)
            weights_only("ml_v")
            for c in range(MLC):
                act.wait_ge(S("vt_tr"), c + 1)
                if c >= 2:
                    act.wait_ge(S("gate_mm"), c - 1)
                f(tmp(c % 2), PS[1 + c % 2][:, :], ACT.Copy).then_inc(S("vt_done"), 1)
            def x_conv(k):
                act.wait_ge(S("mconv_done"), k + 1)
                f(XC[:, k, 0:LAT], M_ACC[:, 0:LAT], ACT.Silu, bias=vec("ml_b_conv", k))
                f(XC[:, k, LAT:TOK], M_ACC[:, ML_CTX:ML_CTX + CTX], ACT.Silu, bias=vec("ml_b_conv", k))\
                    .then_inc(S("xc_done"), 1)

            for g in range(4):
                for k in range(16):
                    t = 16 * g + k
                    hi_ahead("ml_o", t, t)
                    if t >= 5 and t % 4 == 1:
                        x_conv((t - 5) // 4)
                for n in range(4):
                    t, half = n // 2, n % 2
                    o = MOG[:, g % 2, t, half * 512:(half + 1) * 512]
                    act.wait_ge(S("o_add"), 4 * g + n + 1)
                    f(o, o, ACT.Sigmoid).then_inc(S("o_done"), 1)
            x_conv(MLC - 1)
            act.wait_ge(S("tile_done"), FIRST["ml_q"])
            for k in range(-2, 32):
                if k >= 0:
                    hi_ahead("ml_q", k, k)
                if k + 2 < MLC:
                    f(XMHI[:, k + 2, :], XC[:, k + 2, :], ACT.Copy).then_inc(S("xc_hi_done"), 1)
            weights_only("ml_k")
            for d in range(2):
                log_sigmoid(1 + d, ROWS[0:4, 4, :], ROWS[0:4, 5, :], ROWS[0:4, 6, :], ROWS[0:4, 7, :])
            for n in range(8):
                act.wait_ge(S("rb_mm"), n + 1)
                f(X[:, n, LAT:TOK], PS[5 + n % 2][:, 0:LAT], ACT.Copy).then_inc(S("rb_copy"), 1)
            act.wait_ge(S("ml_cols_copy"), 1)
            for d in range(2):
                a = (d * 6 + 4) * 4
                last = f(M_COLS[:, a:a + 8], M_COLS[:, a:a + 8], ACT.Exp)
            last.then_inc(S("exp_m_done"), 1)
            for h in range(ML_HEADS):
                for d in range(2):
                    act.wait_ge(S("ml_arg"), 2 * h + d + 1)
                    f(MPT(d), MPT(d), ACT.Exp).then_inc(S("ml_exp"), 1)
            act.wait_ge(S("gn_var"), 1)
            f(GN_VAR, GN_VAR, ACT.Sqrt).then_inc(S("gn_std"), 1)
            act.wait_ge(S("gn_nmr"), 1)
            for t in range(2):
                for h in range(ML_HEADS):
                    r = t * ML_HEADS + h
                    z = MH[:, 0, t, 512 * h:512 * (h + 1)]
                    f(z, z, ACT.Identity, scale=GN_RSTD[:, r:r + 1], bias=GN_NMR[:, r:r + 1])\
                        .then_inc(S("hn_done"), 1)
            for c in range(MLC):
                act.wait_ge(S("ml_y_raw"), c + 1)
                f(MYHI[:, c, :], tmp(c % 2, LAT), ACT.Copy).then_inc(S("ml_y_hi"), 1)
            weights_only("down")
            mlp(1, LAT, 7, 7, 3)

        @block.vector
        def _(dve):
            V = nc.vector
            own = Chain(dve, S("dve_own"))
            banks = [0]

            def lo(n, slot):
                dve.wait_ge(S("w_hi_done"), n + 1)
                V.tensor_tensor(WLO[:, slot, :], RAW[:, slot, :], WHI[:, slot, :].bitcast(F32), SUB)\
                    .then_inc(S("w_lo_done"), 1)

            def lo_ahead(ph, t, s):
                n0 = FIRST[ph] + LOOKAHEAD
                lo(t + n0, (n0 + s) % SLOTS)

            def ada_product(a, tile, area):
                junk, _, rows = area
                for st in range(2):
                    ins = V.scalar_tensor_tensor(junk[:, :] if st == 0 else tile, tile, 1.0, rows[:, st, :], MUL, MUL,
                                                 accum_out=MOD[:, bass.ds(a * 2 + st, 1)])
                return ins

            def ada_tile(t, i, s, body, g0, area):
                dve.wait_ge(ada_full[s % 2], i * (8 * body) + 16 * ((g0 + s) // 2 + 1))
                if g0 or not isinstance(t, int) or t:
                    dve.wait_ge(S("ada_used"), t + g0)
                ada_product(t + (g0 + ADA_FIRST), area[1][:, s % 2, :], area).then_inc(S("ada_used"), 1)

            def ada_finish(a0, a1):
                for st in range(2):
                    own(V.tensor_tensor(MOD[:, 2 * a0 + st:2 * a1:2], MOD[:, 2 * a0 + st:2 * a1:2],
                                        vec("ada_b", a0, a1 - a0), ADD))
                for a in range(a0, a1, DC):
                    if a // DC % 6 in (1, 4):
                        own(V.tensor_scalar(MOD[:, 2 * a:2 * (a + DC)], MOD[:, 2 * a:2 * (a + DC)], 1.0, None, ADD))

            def rows_back(n):
                dve.wait_ge(S("c_rows_back"), 16 * n)

            def weights_only(ph, n_ada=0, g0=0, area=None):
                def both(t, i, s):
                    lo_ahead(ph, t, s)
                    ada_tile(t, i, s, SLOTS, g0, area)
                tiles(dve, n_ada, SLOTS, both)
                tiles(dve, COUNT[ph] - n_ada, SLOTS, lambda t, i, s: lo_ahead(ph, t + n_ada, s + n_ada))

            def bank_ready(ph, o, n_banks, tiles_in):
                if o < n_banks - 1:
                    banks[0] += 1
                    dve.wait_ge(S("bank_done"), banks[0])
                else:
                    dve.wait_ge(S("tile_done"), FIRST[ph] + tiles_in)

            def variance(q, T, bank, eps):
                dve.wait_ge(S("sq_used"), DC * (q + 1))
                V.tensor_scalar(tmp(2, T), PS[bank][:, 0:T], 1.0 / D, eps, MUL, ADD).then_inc(S("var_done"), 1)
                dve.wait_ge(S("std_done"), q + 1)
                own(V.reciprocal(tmp(2, T), tmp(2, T)))

            def modulate(m, T, layer, first, normed, alpha=None):
                for c in range(DC):
                    if c >= 2:
                        dve.wait_ge(S("h_lo_done"), m * DC + c - 1)
                    src = X[:, c, :]
                    if normed:
                        own(V.tensor_tensor(tmp(c % 2, T), X[:, c, 0:T], tmp(2, T), MUL))
                        src = tmp(c % 2)
                    for st, cols in streams(T):
                        last = V.tensor_scalar(tmp(c % 2)[:, cols], src[:, cols], mod(layer, first + 1, c, st),
                                               mod(layer, first, c, st), MUL, ADD)
                    last.then_inc(S("raw_done"), 1)
                if alpha is not None:
                    dve.wait_ge(S("raw_done"), (m + 1) * DC)
                    own(V.tensor_scalar(X[:, :, 0:alpha], X[:, :, 0:alpha], ALPHA, None, MUL))

            def residual(ph, T, layer, gate, x0, bias=None):
                for o in range(DC):
                    bank_ready(ph, o, DC, COUNT[ph])
                    for st, cols in streams(T):
                        g = mod(layer, gate, o, st)
                        if bias is None:
                            last = V.scalar_tensor_tensor(X[:, o, cols], PS[o][:, cols], g, X[:, o, cols], MUL, ADD)
                        else:
                            own(V.tensor_scalar(tmp(0)[:, cols], PS[o][:, cols], vec(bias, o), g, ADD, MUL))
                            last = V.tensor_tensor(X[:, o, cols], X[:, o, cols], tmp(0)[:, cols], ADD)
                    last.then_inc(S("x_upd"), 1)
                    if bias is not None:
                        dve.wait_ge(S("x_upd"), x0 + o + 1)
                dve.wait_ge(S("x_upd"), x0 + DC)

            def layer_norm(ln, q, T, z):
                dve.wait_ge(S("ln_sum_done"), ln + 1)
                own(V.tensor_scalar(tmp(2, T), PS[0][:, 0:T], 1.0 / D, None, MUL))
                for c in range(DC):
                    V.tensor_tensor(z[:, c, 0:T], z[:, c, 0:T], tmp(2, T), SUB).then_inc(S("z_centered"), 1)
                dve.wait_ge(S("z_centered"), DC * (ln + 1))
                variance(q, T, 1, LN_EPS)

            def log_sigmoid(q, x, a, e, u, l, t1, out):
                V.scalar_tensor_tensor(a, x, -1.0, x, MUL, MAX).then_inc(S("ls_abs"), 1)
                dve.wait_ge(S("ls_exp"), q + 1)
                V.tensor_scalar(u, e, 1.0, None, ADD).then_inc(S("ls_u"), 1)
                dve.wait_ge(S("ls_u"), q + 1)
                own(V.tensor_scalar(t1, u, -1.0, None, ADD))
                own(V.tensor_tensor(e, e, t1, SUB))
                own(V.reciprocal(t1, u))
                own(V.tensor_tensor(e, e, t1, MUL))
                dve.wait_ge(S("ls_ln"), q + 1)
                own(V.tensor_tensor(e, e, l, ADD))
                own(V.tensor_scalar(a, x, 0.0, None, MIN))
                own(V.tensor_tensor(out, a, e, SUB))

            dve.wait_ge(S("silu_c_done"), 1)
            for n in range(ADA_FIRST):
                dve.wait_ge(S(f"ada_first{n // DC}"), 16 * DC)
                own(ada_product(n, ADA_RAW[:, n, :], AREA_A))
            dve.wait_ge(S("vecs_in"), 16)
            ada_finish(0, ADA_FIRST)
            for n in range(LOOKAHEAD):
                lo(n, n)
            dve.wait_ge(S("x_in"), 16)
            variance(0, TOK, 0, EPS)
            modulate(0, TOK, 0, 0, True)

            dve.wait_ge(S("consts_in"), 48)
            rot = tmp(4, LAT)
            for t in range(16):
                lo_ahead("ret_qk", t, t)
                dve.wait_ge(S("tile_done"), FIRST["ret_qk"] + t + 1)
                ps, par = PS[t % 8], t % 2
                V.tensor_tensor(QK[:, t, 0:LAT], ps[:, 0:LAT], ROPE[:, 0, par, :], MUL)
                V.tensor_tensor(rot[0:64, :], ps[64:128, 0:LAT], ROPE[64:128, 1, par, :], MUL)
                V.tensor_tensor(rot[64:128, :], ps[0:64, 0:LAT], ROPE[0:64, 1, par, :], MUL)
                V.tensor_copy(QK[:, t, LAT:TOK], ps[:, LAT:TOK]).then_inc(S("qk_free"), 1)
                dve.wait_ge(S("qk_free"), 8 + t + 1)
                V.tensor_tensor(QK[:, t, 0:LAT], QK[:, t, 0:LAT], rot, ADD).then_inc(S("qk_rope_done"), 1)
                dve.wait_ge(S("qk_rope_done"), t + 1)
                ada_tile(t, 0, t, 16, 0, AREA_A)
            for grp in range(2):
                for k in range(8):
                    lo_ahead("ret_v", 8 * grp + k, 8 * grp + k)
                    ada_tile(8 * grp + k, 0, 8 * grp + k, 16, 16, AREA_A)
                for b in range(8):
                    bank_ready("ret_v", b, 8, 8 * (grp + 1))
                    V.tensor_copy(RV[:, b // 2, 1024 * grp + 512 * (b % 2):1024 * grp + 512 * (b % 2) + 512],
                                  PS[b][:, :]).then_inc(S("rv_free"), 1)

            dve.wait_ge(S("ada_used"), 32)
            ada_finish(ADA_FIRST, 48)

            def ret_gate(t, i, s):
                lo_ahead("ret_g", t, s)
                dve.wait_ge(S("rg_free"), t + 9)
                V.tensor_scalar(RG[:, t, :], RG[:, t, :], VECS[:, bass.ds(t + VEC["ret_norm_g"], 1)], None, MUL)\
                    .then_inc(S("rg_scaled"), 1)
            tiles(dve, 16, 8, ret_gate)
            dve.wait_ge(S("rg_scaled"), 16)

            log_sigmoid(0, vec("decay", 0, 8), *LS_RET, LG[:, :])
            dve.sem_inc(S("log_gamma_done"), 1)
            dve.wait_ge(S("decay_in"), 16)
            for h in range(RET_HEADS):
                same, cross = DECAY_D[:, h % 2, 0, :], DECAY_D[:, h % 2, 1, :]
                dve.wait_ge(S("decay_exp"), h + 1)
                own(V.tensor_tensor(same, tmp(0), DECAY_E[:, 2, :], MUL))
                own(V.tensor_tensor(tmp(1), tmp(1), DECAY_E[:, 3, :], MUL))
                own(V.tensor_tensor(same, same, tmp(1), ADD))
                V.tensor_tensor(cross, tmp(2), tmp(3), ADD).then_inc(S("decay_used"), 1)
                dve.wait_ge(S("decay_used"), h + 1)
                if h:
                    dve.wait_ge(S("ret_o_done"), 4 * h)
                for b, decay in enumerate((same, cross, same)):
                    dve.wait_ge(S("score_done"), 3 * h + b + 1)
                    V.scalar_tensor_tensor(ATT[:, 2 * b:2 * b + 2, :].rearrange("p a n -> p (a n)"), PS[b][:, :],
                                           RET_DK ** -0.5, decay, MUL, MUL).then_inc(S("att_done"), 1)
                for t in range(4):
                    n, st = 4 * h + t, 16 * (t % 2)
                    dve.wait_ge(S("ret_o_done"), n + 1)
                    if n >= 2:
                        dve.wait_ge(S("on_done"), n - 1)
                    own(V.bn_stats(RSTAT[:, st:st + 6], PS[3 + t][:, :]))
                    own(V.bn_aggr(RSTAT[:, st + 6:st + 8], RSTAT[:, st:st + 6]))
                    V.tensor_scalar(RSTAT[:, st + 8:st + 9], RSTAT[:, st + 7:st + 8], EPS, None, ADD)\
                        .then_inc(S("ret_var"), 1)
                    dve.wait_ge(S("ret_std"), n + 1)
                    own(V.reciprocal(RSTAT[:, st + 10:st + 11], RSTAT[:, st + 9:st + 10]))
                    V.scalar_tensor_tensor(RSTAT[:, st + 11:st + 12], RSTAT[:, st + 6:st + 7], -1.0,
                                           RSTAT[:, st + 10:st + 11], MUL, MUL).then_inc(S("ret_nmr"), 1)
                for t in range(4):
                    dve.wait_ge(S("on_t_done"), 4 * h + t + 1)
                    y = RG[:, 4 * h:4 * h + 4, t * P:(t + 1) * P]
                    V.tensor_tensor(y, PS[7][:, :].rearrange("p (f n) -> p f n", f=4), y, MUL)\
                        .then_inc(S("ret_y_done"), 1)
            dve.wait_ge(S("ret_y_done"), 16)
            for c in range(16):
                dve.wait_ge(S("ret_y_hi_done"), c + 1)
                V.tensor_tensor(YLO[:, c, :], RG[:, c, :], YHI[:, c, :].bitcast(F32), SUB)\
                    .then_inc(S("ret_y_lo_done"), 1)
            rows_back(1)
            weights_only("ret_out", 16, 32, AREA_B)
            dve.wait_ge(S("ada_used"), 48)
            ada_finish(48, 64)
            residual("ret_out", TOK, 0, 2, 0)

            def ffn(layer, T, q, m, x0):
                variance(q, T, 0, EPS)
                modulate(m, T, layer, 3, True)
                ph = f"ffn{layer}_in"
                fhi, flo = (FHI, FLO) if layer == 0 else (FHI1, FLO1)

                def tile(t, i, s, t0=0):
                    lo_ahead(ph, t + t0, s + t0)
                    if layer == 0:
                        ada_tile(t, i, s, 8, 48 + t0, AREA_G)
                    if s % 2:
                        p = i * 4 + (s // 2 + t0 // 2)
                        raw = tmp(s // 2 % 2, T)
                        dve.wait_ge(S("tile_done"), t + (FIRST[ph] + t0 + 1))
                        dve.wait_ge(S(f"ffn{layer}_a_free"), p + 5)
                        V.tensor_tensor(raw, PS[s % 8][:, 0:T], tmp(3 + s // 2 % 2, T), MUL)\
                            .then_inc(S(f"ffn{layer}_g_free"), 1)
                        dve.wait_ge(S("f_hi_done"), p + (FFN_C * layer + 1))
                        V.tensor_tensor(flo[:, p, 0:T], raw, fhi[:, p, 0:T].bitcast(F32), SUB)\
                            .then_inc(S("f_lo_done"), 1)
                        dve.wait_ge(S("f_lo_done"), p + (FFN_C * layer + 1))
                if layer == 0:
                    rows_back(2)
                    tiles(dve, 32, 8, tile)
                    rows_back(3)
                    tiles(dve, 12, 8, lambda t, i, s: tile(t, i, s, 32))
                    rows_back(4)
                    weights_only("ffn0_out", 22, 92, AREA_B)
                    dve.wait_ge(S("ada_used"), 114)
                    ada_finish(64, 128)
                    dve.wait_ge(S("x_back"), 16)
                else:
                    tiles(dve, COUNT[ph], 8, tile)
                    rows_back(5)
                    weights_only("ffn1_out", 6, 114, AREA_E)
                    dve.wait_ge(S("ada_used"), 120)
                    ada_finish(128, 136)
                residual(f"ffn{layer}_out", T, layer, 5, x0)

            ffn(0, TOK, 1, 1, 8)

            variance(2, TOK, 0, EPS)
            modulate(2, TOK, 1, 0, True)
            dve.wait_ge(S("diff_tab_in"), 32)
            for t in range(16 + 3):
                if t < 16:
                    T = TOK if t < 8 else LAT
                    lo_ahead("diff_qk", t, t)
                    dve.wait_ge(S("tile_done"), FIRST["diff_qk"] + t + 1)
                    if t >= 4:
                        dve.wait_ge(S("dqk_sq"), t - 3)
                        dve.wait_ge(S("dqk_norm"), t - 3)
                    V.tensor_copy(DRAWB[:, t % 4, 0:T], PS[t % 4][:, 0:T]).then_inc(S("dqk_raw"), 1)
                u = t - 1
                if 0 <= u < 16:
                    T = TOK if u < 8 else LAT
                    dve.wait_ge(S("dqk_stat"), u + 1)
                    if u >= 2:
                        dve.wait_ge(S("dqk_norm"), u - 1)
                    V.tensor_scalar(DRST[:, u % 2, 0:T], PS[4 + u % 2][:, 0:T], 1.0 / DIFF_DH, EPS, MUL, ADD)\
                        .then_inc(S("dqk_var"), 1)
                u = t - 2
                if 0 <= u < 16:
                    T = TOK if u < 8 else LAT
                    dst = DK[:, u, :] if u < 8 else DQ[:, u - 8, :]
                    dve.wait_ge(S("dqk_std"), u + 1)
                    own(V.reciprocal(DRST[:, u % 2, 0:T], DRST[:, u % 2, 0:T]))
                    V.scalar_tensor_tensor(dst, DRAWB[:, u % 4, 0:T], vec("diff_k_g" if u < 8 else "diff_q_g"),
                                           DRST[:, u % 2, 0:T], MUL, MUL).then_inc(S("dqk_norm"), 1)
                u = t - 3
                if 0 <= u < 16:
                    dst = DK[:, u, 0:LAT] if u < 8 else DQ[:, u - 8, :]
                    dve.wait_ge(S("dqk_rot"), u + 1)
                    V.tensor_tensor(DRT[:, :], PS[6 + u % 2][:, 0:LAT], D_SIN, MUL)
                    own(V.tensor_tensor(dst, dst, D_COS, MUL))
                    V.tensor_tensor(dst, dst, DRT[:, :], ADD).then_inc(S("dqk_rope"), 1)
                    dve.wait_ge(S("dqk_rope"), u + 1)
            for k in range(8):
                lo_ahead("diff_v", k, k)
            for b in range(8):
                bank_ready("diff_v", b, 8, 8)
                V.tensor_copy(DV[:, b // 2, 512 * (b % 2):512 * (b % 2) + 512], PS[b][:, :]).then_inc(S("dv_free"), 1)
            own(V.tensor_tensor(DLAM[:, 0:64], DLAM[:, 0:64], DLAM[:, 64:128], MUL))
            own(V.tensor_tensor(DLAM[:, 128:192], DLAM[:, 128:192], DLAM[:, 192:256], MUL))
            own(V.reduce_sum(DCOL[:, 2:3], DLAM[:, 0:64], AX.X))
            V.reduce_sum(DCOL[:, 3:4], DLAM[:, 128:192], AX.X).then_inc(S("lam_dot"), 1)
            own(V.tensor_scalar(DCOL[:, 1:2], vec("subln_g"), 1.0 - LAMBDA_INIT, None, MUL))
            dve.wait_ge(S("lam_exp"), 1)
            own(V.tensor_tensor(DCOL[:, 0:1], DCOL[:, 3:4], DCOL[:, 2:3], SUB))
            own(V.tensor_scalar(DCOL[:, 0:1], DCOL[:, 0:1], -LAMBDA_INIT, None, ADD))
            scale = DIFF_DH ** -0.5
            for u in range(16 + 2):
                if u < 16:
                    if u >= 2:
                        dve.wait_ge(S("d_exp"), 2 * (u - 1))
                    for m in range(2):
                        col = 4 + 2 * (u % 2) + m
                        dve.wait_ge(S("d_score"), 2 * u + m + 1)
                        own(V.reduce_max(DCOL[:, col + 12:col + 13], PS[2 * (u % 2) + m][:, :], AX.X))
                        V.tensor_scalar(DCOL[:, col:col + 1], DCOL[:, col + 12:col + 13], -scale, None, MUL)\
                            .then_inc(S("d_max"), 1)
                a = u - 1
                if 0 <= a < 16:
                    c = 8 + 2 * (a % 2)
                    dve.wait_ge(S("d_exp"), 2 * (a + 1))
                    own(V.reciprocal(DCOL[:, c + 16:c + 18], DCOL[:, c:c + 2]))
                    own(V.tensor_tensor(DCOL[:, c + 17:c + 18], DCOL[:, c + 17:c + 18], DCOL[:, 0:1], MUL))
                    if a >= 2:
                        dve.wait_ge(S("d_tr"), a - 1)
                    own(V.tensor_scalar(DP[:, a % 2, :], DE[:, a % 2, 0, :], DCOL[:, c + 16:c + 17], None, MUL))
                    V.scalar_tensor_tensor(DP[:, a % 2, :], DE[:, a % 2, 1, :], DCOL[:, c + 17:c + 18],
                                           DP[:, a % 2, :], MUL, ADD).then_inc(S("d_p"), 1)
                    dve.wait_ge(S("d_p"), a + 1)
                b = u - 2
                if 0 <= b < 16 and b % 2:
                    h = b // 2
                    dve.wait_ge(S("d_pv"), b + 1)
                    V.tensor_copy(DO[:, h, :], PS[6 + h % 2][:, 0:LAT]).then_inc(S("d_ocopy"), 1)
            for h in range(DIFF_HEADS + 1):
                if h < DIFF_HEADS:
                    dve.wait_ge(S("do_stat"), h + 1)
                    if h >= 2:
                        dve.wait_ge(S("do_norm"), h - 1)
                    V.tensor_scalar(tmp(1 + h % 2, LAT), PS[h % 2][:, 0:LAT], 1.0 / DIFF_DV, EPS, MUL, ADD)\
                        .then_inc(S("do_var"), 1)
                g = h - 1
                if 0 <= g:
                    dve.wait_ge(S("do_std"), g + 1)
                    own(V.reciprocal(tmp(1 + g % 2, LAT), tmp(1 + g % 2, LAT)))
                    V.scalar_tensor_tensor(DO[:, g, :], DO[:, g, :], DCOL[:, 1:2], tmp(1 + g % 2, LAT), MUL, MUL)\
                        .then_inc(S("do_norm"), 1)
            weights_only("diff_out")
            residual("diff_out", LAT, 1, 2, 16)
            ffn(1, LAT, 3, 3, 24)

            dve.wait_ge(S("ctx2_in"), 16)
            modulate(4, TOK, 2, 0, False, alpha=TOK)
            dve.wait_ge(S("conv_zero"), 1)
            for t in range(16):
                lo_ahead("pw1", t, t)
                if t % 2 == 0:
                    continue
                p, ps = t // 2, PS[t % 8]
                dve.wait_ge(S("tile_done"), FIRST["pw1"] + t + 1)
                dve.wait_ge(S("pw1_gate_free"), 4 + p + 1)
                V.scalar_tensor_tensor(
                    CIN[:, p, 0:CONV_CTX].rearrange("p (r w) -> p r w", w=ROW_PADDED)[:, :, CONV_PAD:CONV_PAD + GRID_W],
                    ps[:, 0:LAT].rearrange("p (r w) -> p r w", w=GRID_W), vec("b_pw1", p),
                    tmp(3 + p % 2)[:, 0:LAT].rearrange("p (r w) -> p r w", w=GRID_W), ADD, MUL)
                V.scalar_tensor_tensor(CIN[:, p, CONV_CTX + CONV_PAD:CONV_CTX + CONV_PAD + CTX], ps[:, LAT:TOK],
                                       vec("b_pw1", p), tmp(3 + p % 2)[:, LAT:TOK], ADD, MUL)\
                    .then_inc(S("pw1_a_free"), 1)
                dve.wait_ge(S("pw1_a_free"), 4 + p + 1)
                if p:
                    dve.wait_ge(S("conv_z_done"), p)
                for j in range(CONV_W):
                    acc, x_j, w_j = CACC[:, j % 2, :], CIN[:, p, j:j + CONV_OUT], vec("w_dw", p * CONV_W + j)
                    if j < 2:
                        ins = V.tensor_scalar(acc, x_j, w_j, None, MUL)
                    else:
                        ins = V.scalar_tensor_tensor(acc, x_j, w_j, acc, MUL, ADD)
                    own.at += 1
                    ins.then_inc(S("dve_own"), 1)
                    if j:
                        dve.wait_ge(S("dve_own"), own.at - 1)
                dve.wait_ge(S("dve_own"), own.at)
                V.tensor_tensor(CACC[:, 0, :], CACC[:, 0, :], CACC[:, 1, :], ADD).then_inc(S("conv_acc_done"), 1)
                dve.wait_ge(S("conv_acc_done"), p + 1)
            dve.wait_ge(S("conv_z_done"), 8)
            layer_norm(0, 4, TOK, CZ)
            for c in range(DC):
                V.tensor_tensor(CZ[:, c, :], CZ[:, c, :], tmp(2), MUL).then_inc(S("cz_norm"), 1)
            for c in range(DC):
                dve.wait_ge(S("cz_hi_done"), c + 1)
                V.tensor_tensor(HLO[:, c, :], tmp(c % 2), HHI[:, c, :].bitcast(F32), SUB).then_inc(S("cz_lo_done"), 1)
            weights_only("pw2")
            residual("pw2", TOK, 2, 2, 32, bias="b_pw2")

            def norm_x(ln, q, T, g, b, j, final=False):
                layer_norm(ln, q, T, X)
                for c in range(DC):
                    own(V.tensor_tensor(X[:, c, 0:T], X[:, c, 0:T], tmp(2, T), MUL))
                    last = V.tensor_scalar(X[:, c, 0:T], X[:, c, 0:T], vec(g, 8 * j + c), vec(b, 8 * j + c), MUL, ADD)
                    if final:
                        last.then_inc(S("x_final"), 1)
                    else:
                        own(last)

            def mlp(j, T, q, m, ln, x0):
                layer = 2 + j
                norm_x(ln, q, T, "ln1_g", "ln1_b", j)
                modulate(m, T, layer, 3, False, alpha=T)
                for n, half in enumerate("ab"):
                    ph, free, done = f"mlp{j}{half}_in", S(f"mlp{j}{half}_free"), 16 * (2 * j + n)

                    def tile(t, i, s):
                        lo_ahead(ph, t, s)
                        if j == 0:
                            ada_tile(t, i, s, 8, 120 + 32 * n, AREA_F)
                        raw, r = tmp(s % 2, T), tmp(3 + s % 2, T)
                        dve.wait_ge(S("m_relu_done"), t + (done + 1))
                        V.tensor_tensor(raw, r, r, MUL).then_inc(S("m_sq_done"), 1)
                        dve.wait_ge(S("m_sq_done"), t + (done + 1))
                        dve.wait_ge(S("m_hi_done"), t + (done + 1))
                        V.tensor_tensor(MLO[:, t, 0:T], raw, MHI[:, t, 0:T].bitcast(F32), SUB).then_inc(free, 1)
                        dve.wait_ge(free, t + 9)
                    if j == 0 and n == 0:
                        rows_back(6)
                    tiles(dve, 16, 8, tile)
                    if j == 0 and n == 0:
                        dve.wait_ge(S("ada_used"), 136)
                        ada_finish(136, 144)
                        weights_only("mlp0a_out", 16, 136, AREA_F)
                    elif j == 0:
                        weights_only("mlp0b_out", 8, 168, AREA_F)
                        dve.wait_ge(S("ada_used"), 176)
                        ada_finish(144, 192)
                    else:
                        weights_only(f"mlp{j}{half}_out")
                    residual(f"mlp{j}{half}_out", T, layer, 5, x0 + 8 * n)
                norm_x(ln + 1, q + 1, T, "ln2_g", "ln2_b", j, final=j == 1)

            mlp(0, TOK, 5, 5, 1, 40)

            modulate(6, TOK, 3, 0, False, alpha=LAT)

            def up_x(t, i, s):
                lo_ahead("up_x", t, s)
                dve.wait_ge(S("up_hi_done"), t + 1)
                V.tensor_tensor(XMLO[:, t, :], PS[s][:, :], XMHI[:, t, :].bitcast(F32), SUB).then_inc(S("up_free"), 1)
            tiles(dve, 16, 8, up_x)
            weights_only("up_z")
            for grp in range(2):
                for k in range(16):
                    lo_ahead("ml_v", 16 * grp + k, 16 * grp + k)
                for b in range(8):
                    bank_ready("ml_v", b, 8, 16 * (grp + 1))
                    a = 1024 * grp + 512 * (b % 2)
                    V.tensor_copy(MV[:, b // 2, a:a + 512], PS[b][:, :]).then_inc(S("v_done"), 1)

            GT = tmp(4)[0:16, :]

            def gate_add(n, mms):
                dve.wait_ge(S("gate_mm"), mms)
                if n == 0:
                    ins = V.tensor_scalar(GT, PS[0][0:16, :], vec("b_gate")[0:16, :], None, ADD)
                else:
                    ins = V.tensor_tensor(GT, PS[0][0:16, :], GT, ADD)
                ins.then_inc(S("gate_acc"), 1)
                dve.wait_ge(S("gate_acc"), n + 1)

            gate_add(0, 16)
            dve.wait_ge(S("b_o_in"), 16)
            own(V.memset(M_PAD, 0.0))
            dve.wait_ge(S("v_spilled"), 16)

            def conv_chunk(k):
                for dst, cols in ((2, slice(0, LAT)), (ML_CTX + 2, slice(LAT, TOK))):
                    last = V.tensor_tensor(M_PAD[:, dst:dst + LAT], XMHI[:, k, cols].bitcast(F32),
                                           XMLO[:, k, cols].bitcast(F32), ADD)
                own(last)
                if k:
                    dve.wait_ge(S("xc_done"), k)
                for j in range(ML_TAPS):
                    x_j, w_j = M_PAD[:, j:j + ML_OUT], vec("ml_w_conv", k * ML_TAPS + j)
                    if j == 0:
                        own(V.tensor_scalar(M_ACC, x_j, w_j, None, MUL))
                    elif j < ML_TAPS - 1:
                        own(V.scalar_tensor_tensor(M_ACC, x_j, w_j, M_ACC, MUL, ADD))
                    else:
                        V.scalar_tensor_tensor(M_ACC, x_j, w_j, M_ACC, MUL, ADD).then_inc(S("mconv_done"), 1)
                        dve.wait_ge(S("mconv_done"), k + 1)

            for g in range(4):
                for k in range(16):
                    lo_ahead("ml_o", 16 * g + k, 16 * g + k)
                    if k % 4 == 3:
                        conv_chunk(4 * g + k // 4)
                if g >= 2:
                    dve.wait_ge(S(f"o_spilled{g % 2}"), 16)
                for n in range(4):
                    bank_ready("ml_o", n, 4, 16 * (g + 1))
                    a = 1024 * g + 512 * (n % 2)
                    V.tensor_tensor(MOG[:, g % 2, n // 2, 512 * (n % 2):512 * (n % 2) + 512], PS[4 * (g % 2) + n][:, :],
                                    BO[:, a:a + 512], ADD).then_inc(S("o_add"), 1)
            for grp in range(2):
                for k in range(-2 if grp == 0 else 0, MLC):
                    if k >= 0:
                        lo_ahead("ml_q", MLC * grp + k, MLC * grp + k)
                    if grp == 0 and k + 2 < MLC:
                        dve.wait_ge(S("xc_hi_done"), k + 3)
                        V.tensor_tensor(XMLO[:, k + 2, :], XC[:, k + 2, :], XMHI[:, k + 2, :].bitcast(F32), SUB)\
                            .then_inc(S("xc_lo_done"), 1)
                if grp == 0:
                    for g in range(2):
                        dve.wait_ge(S(f"o_spilled{g}"), 32)
                    own(V.tensor_copy(XCL[:, :, :], XC[:, :, 0:LAT]))
                if grp:
                    dve.wait_ge(S("gate_mm"), 32)
                for o in range(DC):
                    bank_ready("ml_q", o, 8, MLC * (grp + 1))
                    V.tensor_copy(MQ[:, 8 * grp + o, :], PS[o][:, 0:LAT])
                    V.tensor_copy(MQC[:, o, :], PS[o][:, LAT:TOK]).then_inc(S("q_done"), 1)
                gate_add(1 + grp, 16 + 16 * (grp + 1))
            for grp in range(2):
                for k in range(MLC):
                    lo_ahead("ml_k", MLC * grp + k, MLC * grp + k)
                for o in range(DC):
                    bank_ready("ml_k", o, 8, MLC * (grp + 1))
                    V.tensor_copy(MK[:, 8 * grp + o, :], PS[o][:, :]).then_inc(S("k_done"), 1)
                gate_add(3 + grp, 48 + 8 * (grp + 1))

            def R(i):
                return ROWS[0:4, i, :]

            dve.wait_ge(S("gate_rows"), 4)
            own(V.memset(R(11), 0.0))
            for d in range(2):
                for g, dst in ((2 * d, R(d)), (2 * d + 1, R(2 + d))):
                    if d == 0:
                        own(V.tensor_copy(dst[:, 0:CTX], PS[g][0:4, LAT:TOK]))
                        own(V.tensor_copy(dst[:, CTX:TOK], PS[g][0:4, 0:LAT]))
                    else:
                        own(V.tensor_copy(dst, PS[g][0:4, ::-1]))
                log_sigmoid(1 + d, R(2 + d), R(4), R(5), R(6), R(7), R(8), R(4))
                own(V.tensor_tensor_scan(R(8), R(4), R(11), 0.0, ADD, ADD))
                own(V.tensor_tensor(R(5), R(d), R(8), SUB))
                own(V.tensor_tensor_scan(R(9), R(5), R(5), 0.0, MAX, MAX))
                own(V.tensor_tensor(R(6), R(8), R(9), ADD))
                own(V.tensor_scalar(R(6), R(6), -1.0, None, MUL))
                own(V.tensor_scalar(R(9), R(9), -1.0, None, MUL))
                if d == 0:
                    own(V.tensor_copy(R(12)[:, 0:LAT], R(5)[:, CTX:TOK]))
                    own(V.tensor_copy(R(12)[:, LAT:TOK], R(5)[:, 0:CTX]))
                    own(V.tensor_copy(R(14)[:, 0:LAT], R(6)[:, CTX:TOK]))
                    V.tensor_copy(R(14)[:, LAT:TOK], R(9)[:, CTX:TOK]).then_inc(S("rows_done"), 1)
                else:
                    own(V.tensor_copy(R(13), ROWS[0:4, 5, ::-1]))
                    own(V.tensor_copy(R(15)[:, 0:LAT], ROWS[0:4, 6, ::-1][:, 0:LAT]))
                    V.tensor_copy(R(15)[:, LAT:TOK], ROWS[0:4, 9, ::-1][:, 0:LAT]).then_inc(S("rows_done"), 1)
                dve.wait_ge(S("rows_done"), d + 1)
            dve.wait_ge(S("ml_cols"), 1)
            V.tensor_copy(M_COLS, PS[4][:, 0:48]).then_inc(S("ml_cols_copy"), 1)
            dve.wait_ge(S("ml_cols_copy"), 1)
            dve.wait_ge(S("exp_m_done"), 1)
            dve.wait_ge(S("rb_copy"), 8)
            dve.wait_ge(S("tri_in"), 16)
            for h in range(ML_HEADS):
                for d in range(2):
                    if h:
                        dve.wait_ge(S("ml_num"), 4 * (h - 1) + 2 * d + 2)
                    for j in range(4):
                        col = (d * 6 + j) * 4 + h
                        last = V.tensor_scalar(MPT(d)[:, j, :], X[:, d * 4 + h, LAT:TOK], M_COLS[:, col:col + 1], 0.0,
                                               ADD, MIN)
                    last.then_inc(S("ml_arg"), 1)
                for d in range(2):
                    dve.wait_ge(S("ml_exp"), 2 * h + d + 1)
                    for t in range(2):
                        diag = MPT(d)[:, t, t * P:(t + 1) * P]
                        own(V.tensor_tensor(diag, diag, M_TRI[:, d * P:(d + 1) * P], MUL))
                    dve.wait_ge(S("ml_scores_done"), h + 1)
                    for b in range(2):
                        p_b = MPT(d)[:, 2 * b:2 * b + 2, :].rearrange("p a n -> p (a n)")
                        V.scalar_tensor_tensor(p_b, PS[b][:, :], ML_DH ** -0.5, p_b, MUL, MUL).then_inc(S("ml_p"), 1)
                for d in range(2):
                    for t in range(2):
                        n = 4 * h + 2 * d + t
                        dve.wait_ge(S("ml_num"), n + 1)
                        den = M_DEN
                        em = (d * 6 + 4 + t) * 4 + h
                        own(V.tensor_scalar(M_NEG, PS[4 + n % 2][:, 0:1], -1.0, M_COLS[:, em:em + 1], MUL, MAX))
                        own(V.tensor_tensor(den, PS[4 + n % 2][:, 0:1], M_NEG, MAX))
                        own(V.reciprocal(den, den))
                        V.tensor_scalar(MH[:, d, t, 512 * h:512 * (h + 1)], PS[6 + n % 2][:, :], den, None, MUL)\
                            .then_inc(S("ml_h_done"), 1)
                        dve.wait_ge(S("ml_h_done"), n + 1)
            dve.wait_ge(S("o_back"), 32)
            for t in range(2):
                for d in range(2):
                    own(V.tensor_tensor(MH[:, d, t, :], MH[:, d, t, :], MO2[:, t, 2048 * d:2048 * (d + 1)], MUL))
                own(V.tensor_tensor(MH[:, 0, t, :], MH[:, 0, t, :], MH[:, 1, t, :], ADD))
                for h in range(ML_HEADS):
                    r = t * ML_HEADS + h
                    own(V.bn_stats(GN_STATS[:, 6 * r:6 * r + 6], MH[:, 0, t, 512 * h:512 * (h + 1)]))
                    own(V.bn_aggr(GN_AGGR[:, 2 * r:2 * r + 2], GN_STATS[:, 6 * r:6 * r + 6]))
            V.tensor_scalar(GN_VAR, GN_AGGR[:, 1:16:2], LN_EPS, None, ADD).then_inc(S("gn_var"), 1)
            dve.wait_ge(S("gn_std"), 1)
            own(V.reciprocal(GN_RSTD, GN_VAR))
            V.scalar_tensor_tensor(GN_NMR, GN_AGGR[:, 0:16:2], -1.0, GN_RSTD, MUL, MUL).then_inc(S("gn_nmr"), 1)
            for c in range(MLC):
                y = tmp(c % 2, LAT)
                if c >= 2:
                    dve.wait_ge(S("ml_y_lo"), c - 1)
                own(V.tensor_scalar(y, XCL[:, c, :], vec("skip", c), None, MUL))
                dve.wait_ge(S("hn_tr"), c + 1)
                V.scalar_tensor_tensor(y, PS[c % 2][:, 0:LAT], vec("gn_g", c), y, MUL, ADD).then_inc(S("ml_y_done"), 1)
                dve.wait_ge(S("ml_y_done"), c + 1)
                V.tensor_tensor(y, y, MZ2[:, c, :], MUL).then_inc(S("ml_y_raw"), 1)
                dve.wait_ge(S("ml_y_raw"), c + 1)
                dve.wait_ge(S("ml_y_hi"), c + 1)
                V.tensor_tensor(MYLO[:, c, :], y, MYHI[:, c, :].bitcast(F32), SUB).then_inc(S("ml_y_lo"), 1)
            weights_only("down")
            residual("down", LAT, 3, 2, 56)
            mlp(1, LAT, 7, 7, 3, 64)


def _rope_angles(quarter):
    inv = np.power(np.float32(10000.0), -np.arange(quarter, dtype=np.float32) / np.float32(quarter))
    pos = np.arange(LAT)
    row = (pos // GRID_W).astype(np.float32)
    col = (pos % GRID_W).astype(np.float32)
    return row[None, :] * inv[:, None], col[None, :] * inv[:, None]


def _constants():
    f32 = np.float32
    p = np.arange(P)
    ident = np.eye(P, dtype=f32)
    ones = np.ones((P, P), f32)
    tri_f = (p[None, :] >= p[:, None]).astype(f32)
    tri_b = (p[None, :] <= p[:, None]).astype(f32)
    consts = np.stack([ident, ones, tri_f, tri_b])
    ret_rope = np.zeros((P, 2, 2, LAT), f32)
    for par, ang in enumerate(_rope_angles(RET_DK // 4)):
        ret_rope[:, 0, par] = np.cos(np.concatenate([ang, ang]))
        ret_rope[:, 1, par] = np.sin(np.concatenate([ang, -ang]))
    j = (np.arange(2) * P)[None, :, None] + p[:, None, None]
    i = np.arange(LAT)[None, None, :]
    ret_decay = np.stack([np.maximum(i - j, 0), np.maximum(j - i, 0), i >= j, i <= j,
                          CTX + i - j, LAT - i + j], axis=1).astype(f32).reshape(P, 6, 512)
    row, col = _rope_angles(DIFF_DH // 4)
    ang = np.concatenate([row, row, col, col] * 2)
    block = (p[:, None] // DIFF_DH == p[None, :] // DIFF_DH).astype(f32)
    rot = np.zeros((P, P), f32)
    for m in range(P):
        if m % 32 < 16:
            rot[m + 16, m] = -1.0
        else:
            rot[m - 16, m] = 1.0
    diff_tab = np.concatenate([np.cos(ang), np.sin(ang), block, rot], axis=1).astype(f32)
    sel = np.repeat(np.eye(ML_HEADS, dtype=f32), P, axis=1)
    return consts, ret_rope, ret_decay, diff_tab, sel


def _rows(w):
    n = w.shape[1] // P
    return w.reshape(DC, P, n, P).transpose(2, 1, 0, 3).reshape(n, P, 1024)


def _pairs(a, b):
    return np.stack([a, b], axis=1).reshape(-1, P, 1024)


def _cols(w):
    k, n = w.shape
    return w.reshape(k // P, P, n // 1024, 1024).transpose(2, 0, 1, 3).reshape(-1, P, 1024)


def _chunks(v):
    return v.reshape(-1, P).T


def kernel(**inputs):
    import concourse.bacc as bacc
    from concourse.bass_utils import run_bass_kernel_spmd

    a = {k: np.asarray(v) for k, v in inputs.items()}
    f32 = np.float32

    def ffn(layer):
        w = a["ffn_w_in"][layer]
        return [_pairs(_rows(w[:, :FFN]), _rows(w[:, FFN:])), _cols(a["ffn_w_out"][layer])]

    def mlp(j):
        w1, w2 = _rows(a["mlp_w1_2"][j]), _cols(a["mlp_w2_2"][j])
        return [w1[:16], w2[:16], w1[16:], w2[16:]]

    ret, diff, pw1 = a["ret_w_in"][0], a["diff_w_in"][0], a["conv_w_pw1_2"][0]
    up = a["ml_w_up_2"][0]
    diff_rows = _rows(diff[:, :2048])
    parts = [_rows(ret[:, :2048]), _cols(ret[:, 2048:4096]), _rows(ret[:, 4096:]), _cols(a["ret_w_out"][0]),
             *ffn(0), diff_rows[8:], diff_rows[:8], _cols(diff[:, 2048:]), _cols(a["diff_w_out"][0]), *ffn(1),
             _pairs(_rows(pw1[:, D:]), _rows(pw1[:, :D])), _cols(a["conv_w_pw2_2"][0]), *mlp(0),
             _rows(up[:, :ML_INNER]), _rows(up[:, ML_INNER:]), _cols(a["ml_w_v_2"][0]), _cols(a["ml_w_o_2"][0]),
             _cols(a["ml_w_q_2"][0]), _cols(a["ml_w_k_2"][0]), _cols(a["ml_w_down_2"][0]), *mlp(1),
             np.zeros((LOOKAHEAD, P, 1024), f32)]
    weights = np.concatenate(parts)
    assert weights.shape[0] == N_TILES + LOOKAHEAD
    ada = np.concatenate([w.T.reshape(ADA_TILES, P, D) for w in (a["ada_w"][0], a["ada_w"][1],
                                                                 a["ada_w_2"][0], a["ada_w_2"][1])])
    c_rows = np.broadcast_to(np.stack([a["c"][0], a["c_ctx"], a["c_2"][0], a["c_ctx_2"]])[None], (P, 4, D))

    def tokens(x):
        return x.T.reshape(DC, P, -1).transpose(1, 0, 2)

    x_t = np.concatenate([tokens(a["x"][0]), tokens(a["ctx"][0])], axis=2)
    ctx2_t = tokens(a["ctx_2"][0])
    b_gate = np.zeros((P, 1), f32)
    b_gate[:16, 0] = a["ml_b_gate_2"][0]
    named = {
        "ret_norm_g": _chunks(a["ret_norm_g"][0]),
        "diff_q_g": np.tile(a["diff_q_norm_g"][0], 2)[:, None],
        "diff_k_g": np.tile(a["diff_k_norm_g"][0], 2)[:, None],
        "subln_g": a["diff_subln_g"][0][:, None],
        "ada_b": np.concatenate([_chunks(a["ada_b"][0]), _chunks(a["ada_b"][1]), _chunks(a["ada_b_2"][0]),
                                 _chunks(a["ada_b_2"][1])], axis=1),
        "decay": np.broadcast_to(a["ret_decay_logit"][0].reshape(1, 8), (P, 8)),
        "b_pw1": _chunks(a["conv_b_pw1_2"][0]),
        "w_dw": a["conv_w_dw_2"][0].T.reshape(DC, P, CONV_W).transpose(1, 0, 2).reshape(P, -1),
        "b_dw": _chunks(a["conv_b_dw_2"][0]),
        "conv_ln_g": _chunks(a["conv_ln_g_2"][0]),
        "conv_ln_b": _chunks(a["conv_ln_b_2"][0]),
        "b_pw2": _chunks(a["conv_b_pw2_2"][0]),
        "ln1_g": _chunks(a["ln1_g_2"].reshape(-1)), "ln1_b": _chunks(a["ln1_b_2"].reshape(-1)),
        "ln2_g": _chunks(a["ln2_g_2"].reshape(-1)), "ln2_b": _chunks(a["ln2_b_2"].reshape(-1)),
        "ml_b_conv": _chunks(a["ml_b_conv_2"][0]),
        "ml_w_conv": a["ml_w_conv_2"][0].T.reshape(MLC, P, ML_TAPS).transpose(1, 0, 2).reshape(P, -1),
        "gn_g": _chunks(a["ml_gn_g_2"][0]),
        "skip": _chunks(a["ml_skip_2"][0]),
        "b_gate": b_gate,
    }
    vecs = np.concatenate([named[name] for name, _ in VEC_LAYOUT], axis=1)
    assert vecs.shape == (P, N_VEC)
    consts, ret_rope, ret_decay, diff_tab, sel = _constants()
    lam = np.broadcast_to(a["diff_lambda"][0].reshape(1, 256), (P, 256))
    b_o = np.broadcast_to(a["ml_b_o_2"][0].reshape(1, 4096), (P, 4096))
    w_gate = a["ml_w_gate_2"][0].reshape(3, MLC, P, 16).transpose(2, 0, 1, 3).reshape(P, 3, 256)

    arrays = {"weights": weights, "ada": ada, "c_rows": c_rows, "x_t": x_t, "ctx2_t": ctx2_t, "vecs": vecs, "consts": consts,
              "ret_rope": ret_rope, "ret_decay": ret_decay, "diff_tab": diff_tab, "lam": lam, "b_o": b_o,
              "w_gate": w_gate, "sel": sel}
    arrays = {k: np.ascontiguousarray(v) for k, v in arrays.items()}
    nc = bacc.Bacc("TRN2", target_bir_lowering=False, num_devices=1)
    args = [nc.dram_tensor(f"in_{k}", v.shape, mybir.dt.from_np(v.dtype), kind="ExternalInput").ap()
            for k, v in arrays.items()]
    out = nc.dram_tensor("out_t", (P, DC, LAT), mybir.dt.float32, kind="ExternalOutput").ap()
    program(nc, *args, out)
    r = run_bass_kernel_spmd(nc, [{f"in_{k}": v for k, v in arrays.items()}], core_ids=[0])
    got = r.results[0]["out_t"]
    return got.transpose(2, 1, 0).reshape(1, LAT, D)
```

```python
import math
from contextlib import ExitStack

import numpy as np

import concourse.bass as bass
from concourse import mybir

P = 128
D = 1024
LAT = 256
CTX = 256
TOK = LAT + CTX
DC = D // P
GRID_W = 64
RET_HEADS, RET_DK, RET_DV = 4, 256, 512
DIFF_HEADS, DIFF_DH, DIFF_DV = 8, 64, 128
FFN = 2816
FFN_C = FFN // P
MLP_HALF_C = 16
CONV_W, CONV_ROWS = 31, LAT // GRID_W
POOL_TAPS, TAP_RING = 11, 5
PE_TAPS = 5
DVE_TAPS = CONV_W - POOL_TAPS - PE_TAPS
CONV_ZERO = 17
CONV_PAD = CONV_W // 2
ROW_PADDED = GRID_W + CONV_PAD
CONV_IN = CONV_ROWS * ROW_PADDED + CTX + 2 * CONV_PAD
CONV_OUT = CONV_IN - 2 * CONV_PAD
CONV_CTX = CONV_ROWS * ROW_PADDED
ML_INNER, ML_HEADS, ML_DH, ML_TAPS = 2048, 4, 512, 5
MLC = ML_INNER // P
ML_IN = LAT + CTX + 2 * (ML_TAPS - 1)
ML_OUT = ML_IN - (ML_TAPS - 1)
ML_CTX = LAT + ML_TAPS - 1
LAMBDA_INIT = 0.8 - 0.6 * math.exp(-0.3)
ALPHA = 4 ** 0.25
EPS, LN_EPS = 1e-6, 1e-5
ADA_TILES = 48

PHASES = [("ret_qk", 16), ("ret_v", 16), ("ret_g", 16), ("ret_out", 16), ("ffn0_in", 44), ("ffn0_out", 22),
          ("diff_qk", 16), ("diff_v", 8), ("diff_out", 8), ("ffn1_in", 44), ("ffn1_out", 22),
          ("pw1", 16), ("pw2", 8),
          ("mlp0a_in", 16), ("mlp0a_out", 16), ("mlp0b_in", 16), ("mlp0b_out", 16),
          ("up_x", 16), ("up_z", 16), ("ml_v", 32), ("ml_o", 64), ("ml_q", 32), ("ml_k", 32), ("down", 16),
          ("mlp1a_in", 16), ("mlp1a_out", 16), ("mlp1b_in", 16), ("mlp1b_out", 16)]
FIRST = {}
_n = 0
for _name, _count in PHASES:
    FIRST[_name] = _n
    _n += _count
N_TILES = _n
COUNT = dict(PHASES)
BANK_PHASES = [("ret_v", 2, 8), ("ret_out", 1, 8), ("ffn0_out", 1, 8), ("diff_v", 1, 8), ("diff_out", 1, 8),
               ("ffn1_out", 1, 8), ("pw2", 1, 8), ("mlp0a_out", 1, 8), ("mlp0b_out", 1, 8), ("ml_v", 2, 8),
               ("ml_o", 4, 4), ("ml_q", 2, 8), ("ml_k", 2, 8), ("down", 1, 8), ("mlp1a_out", 1, 8),
               ("mlp1b_out", 1, 8)]
BANKS_BEFORE, BANK_GROUP = {}, {}
_n = 0
for _name, _groups, _banks in BANK_PHASES:
    BANK_GROUP[_name] = (_groups, _banks)
    for _g in range(_groups):
        BANKS_BEFORE[_name, _g] = _n
        _n += _banks - 1
SLOTS = 4
LOOKAHEAD = SLOTS - 1
ADA_FIRST = 16
ADA_VECTOR = 11

VEC_LAYOUT = [("ret_norm_g", 16), ("diff_q_g", 1), ("diff_k_g", 1), ("subln_g", 1), ("ada_b", 4 * ADA_TILES),
              ("decay", 8), ("b_pw1", 16), ("w_dw", 8 * CONV_W), ("b_dw", 8), ("conv_ln_g", 8),
              ("conv_ln_b", 8), ("b_pw2", 8), ("ln1_g", 16), ("ln1_b", 16), ("ln2_g", 16), ("ln2_b", 16),
              ("ml_b_conv", 16), ("ml_w_conv", 16 * ML_TAPS), ("gn_g", 16), ("skip", 16), ("b_gate", 1), ("gate_sel", 2 * 36),
              ("c_cols", 2 * DC)]
VEC = {}
_n = 0
for _name, _count in VEC_LAYOUT:
    VEC[_name] = _n
    _n += _count
N_VEC = _n


def program(nc, weights, ada, c_rows_d, x_t, ctx2_t, vecs_d, consts_d, ret_rope_d, ret_decay_d, diff_tab_d, lam_d,
            b_o_d, w_gate_d, sel_d, out_d):
    F32 = mybir.dt.float32
    F32R = mybir.dt.float32r
    ACT = mybir.ActivationFunctionType
    ALU = mybir.AluOpType
    AX = mybir.AxisListType
    MUL, ADD, SUB, MAX, MIN = ALU.mult, ALU.add, ALU.subtract, ALU.max, ALU.min

    ctx = ExitStack()
    with ctx:
        base = (nc.sbuf_base + 31) // 32 * 32

        def at(name, shape, offset, dt=F32):
            return nc.alloc_sbuf_tensor_at(name, shape, dt, offset=base + offset)

        K = 1024
        RAW = at("w_raw", [P, SLOTS, 1024], 0)
        WHI = at("w_hi", [P, SLOTS, 1024], 16 * K, F32R)
        WLO = at("w_lo", [P, SLOTS, 1024], 32 * K, F32R)
        X = at("x_res", [P, DC, TOK], 48 * K)
        H_AT, ARENA, TMP_AT, CONST_AT = 64 * K, 96 * K, 192 * K, 202 * K
        HHI = at("h_hi", [P, DC, TOK], H_AT, F32R)
        HLO = at("h_lo", [P, DC, TOK], H_AT + 16 * K, F32R)
        TMP = at("tmp", [P, 2560], TMP_AT)
        IDENT = at("ident", [P, P], CONST_AT)
        ONES = at("ones", [P, P], CONST_AT + 512)
        MOD = at("mod", [P, 4 * 2 * ADA_TILES], CONST_AT + 1024)
        VECS = at("vecs", [P, N_VEC], CONST_AT + 1024 + 1536)
        FUSE_AT = CONST_AT + 1024 + 1536 + 4 * (N_VEC + N_VEC % 8)
        FUSE = at("fuse", [P, 6 * DC], FUSE_AT)
        CELL = at("cell", [P, 2], FUSE_AT + 6 * DC * 4)
        assert base + FUSE_AT + 6 * DC * 4 + 8 <= nc.sbuf_usable_end

        def ada_area(name, offset):
            return (at(f"ada_junk_{name}", [P, 1024], offset), at(f"ada_ring_{name}", [P, 2, 1024], offset + 4 * K),
                    at(f"ada_rows_{name}", [P, 2, 1024], offset + 12 * K))

        C_ROWS = at("c_rows", [P, 4, 1024], ARENA + 80 * K)
        AREA_A = (at("ada_junk_a", [P, 1024], ARENA + 68 * K), at("ada_ring_a", [P, 2, 1024], ARENA + 72 * K),
                  C_ROWS[:, 0:2, :])
        AREA_B, AREA_E, AREA_F = (ada_area("b", H_AT), ada_area("e", ARENA + 44 * K), ada_area("f", ARENA + 64 * K))
        AREA_G = (at("ada_junk_g", [P, 1024], 48 * K), at("ada_ring_g", [P, 2, 1024], 52 * K),
                  at("ada_rows_g", [P, 2, 1024], ARENA + 88 * K))
        ADA_RAW = at("ada_first", [P, ADA_FIRST, 1024], ARENA)

        QK = at("ret_qk_sb", [P, 16, TOK], ARENA)
        RV = at("ret_v_sb", [P, 4, 2048], ARENA + 32 * K)
        RG = at("ret_gate", [P, 16, TOK], ARENA + 64 * K)
        ROPE = at("ret_rope", [P, 2, 2, LAT], ARENA + 64 * K)
        DECAY_E = at("ret_dist", [P, 6, 512], H_AT)
        DECAY_D = at("ret_decay", [P, 2, 2, 512], H_AT + 12 * K)
        ATT = at("ret_att", [P, 6, LAT], H_AT + 20 * K)
        ON = at("ret_on", [P, 2, 512], H_AT + 26 * K)
        RSTAT = at("ret_stat", [P, 32], H_AT + 30 * K)
        LG = at("log_gamma", [P, 8], H_AT + 30 * K + 256)
        YHI = at("ret_y_hi", [P, 16, TOK], ARENA, F32R)
        YLO = at("ret_y_lo", [P, 16, TOK], ARENA + 32 * K, F32R)
        FHI = at("ffn_hi", [P, FFN_C, TOK], ARENA, F32R)
        FLO = at("ffn_lo", [P, FFN_C, TOK], ARENA + FFN_C * TOK * 4, F32R)
        FHI1 = at("ffn1_hi", [P, FFN_C, LAT], ARENA, F32R)
        FLO1 = at("ffn1_lo", [P, FFN_C, LAT], ARENA + FFN_C * LAT * 4, F32R)
        DQ = at("diff_q", [P, 8, LAT], ARENA)
        DK = at("diff_k", [P, 8, TOK], ARENA + 8 * K)
        DV = at("diff_v", [P, 4, 1024], ARENA + 24 * K)
        DO = at("diff_o", [P, 8, LAT], ARENA + 40 * K)
        DOHI = at("diff_o_hi", [P, 8, LAT], ARENA + 48 * K, F32R)
        DOLO = at("diff_o_lo", [P, 8, LAT], ARENA + 56 * K, F32R)
        DTAB = at("diff_tab", [P, 768], ARENA + 64 * K)
        D_COS, D_SIN = DTAB[:, 0:LAT], DTAB[:, LAT:2 * LAT]
        D_BLOCK, D_ROT = DTAB[:, 512:640], DTAB[:, 640:768]
        DRAWB = at("diff_raw", [P, 4, TOK], ARENA + 68 * K)
        DSQ = at("diff_sq", [P, 2, TOK], ARENA + 76 * K)
        DRST = at("diff_rst", [P, 2, TOK], ARENA + 80 * K)
        DRT = at("diff_rt", [P, 2, LAT], ARENA + 84 * K)
        DE = at("diff_e", [P, 2, 2, TOK], ARENA + 68 * K)
        DP = at("diff_p", [P, 2, TOK], ARENA + 76 * K)
        DPT = at("diff_pt", [P, 2, TOK], ARENA + 80 * K)
        DLAM = at("diff_lam", [P, 256], ARENA + 86 * K)
        DCOL = at("diff_col", [P, 64], ARENA + 88 * K)
        CIN = at("conv_in", [P, 8, CONV_IN], ARENA)
        CTAP = at("conv_taps", [P, TAP_RING, CONV_OUT], ARENA + 20 * K)
        CACC = at("conv_acc", [P, 4, CONV_OUT], ARENA + 48 * K)
        CACCP = at("conv_acc_pool", [P, 2, CONV_OUT], ARENA + 58 * K)
        CZ = at("conv_z", [P, 8, TOK], ARENA + 32 * K)
        CDIAG = at("conv_diag", [P, 2, PE_TAPS, P], ARENA + 84 * K)
        MHI = at("mlp_hi", [P, MLP_HALF_C, TOK], ARENA, F32R)
        MLO = at("mlp_lo", [P, MLP_HALF_C, TOK], ARENA + 32 * K, F32R)
        XMHI = at("xm_hi", [P, MLC, TOK], ARENA, F32R)
        XMLO = at("xm_lo", [P, MLC, TOK], ARENA + 32 * K, F32R)
        MZ = at("ml_z", [P, MLC, LAT], ARENA + 64 * K)
        MV = at("ml_v", [P, 4, 2048], H_AT)
        BO = at("ml_b_o", [P, 4096], ARENA + 64 * K)
        MOG = at("ml_o_grp", [P, 2, 2, 1024], ARENA + 80 * K)
        XCL = at("ml_xc_lat", [P, MLC, LAT], ARENA + 64 * K)
        MQ = at("ml_q", [P, MLC, LAT], ARENA + 80 * K)
        MQC = at("ml_q_ctx", [P, 8, LAT], TMP_AT)
        XC = at("ml_xc", [P, MLC, TOK], H_AT)
        MK = at("ml_k", [P, MLC, TOK], H_AT)
        MV2 = at("ml_v2", [P, 4, 2048], ARENA)
        MH = at("ml_h", [P, 2, 2048], ARENA + 32 * K)
        MO2 = at("ml_o2", [P, 2, 2, 512], ARENA + 48 * K)
        ROWS = at("ml_rows", [36, 16, 512], ARENA + 32 * K)
        MPTS = [[at("ml_p_f0", [P, 4, LAT], TMP_AT), at("ml_p_b0", [P, 4, LAT], TMP_AT + 4 * K)],
                [at("ml_p_f1", [P, 4, LAT], ARENA + 56 * K), at("ml_p_b1", [P, 4, LAT], ARENA + 60 * K)]]

        def MPT(h, d):
            return MPTS[h % 2][d][:, :, :]
        MZ2 = at("ml_z2", [P, MLC, LAT], ARENA + 80 * K)
        MYHI = at("ml_y_hi", [P, MLC, LAT], ARENA, F32R)
        MYLO = at("ml_y_lo", [P, MLC, LAT], ARENA + 16 * K, F32R)

        M_PAD, M_ACC = TMP[:, 0:ML_IN], TMP[:, 520:520 + ML_OUT]
        COLS_AT = 4 * 512
        M_COLS, M_TRI = TMP[:, COLS_AT:COLS_AT + 48], TMP[:, COLS_AT + 256:COLS_AT + 512]
        M_DEN, M_NEG = TMP[:, COLS_AT + 48:COLS_AT + 52], TMP[:, COLS_AT + 52:COLS_AT + 56]
        GN_STATS, GN_AGGR = TMP[:, COLS_AT + 64:COLS_AT + 112], TMP[:, COLS_AT + 112:COLS_AT + 128]
        GN_VAR, GN_RSTD = TMP[:, COLS_AT + 128:COLS_AT + 136], TMP[:, COLS_AT + 136:COLS_AT + 144]
        GN_NMR = TMP[:, COLS_AT + 144:COLS_AT + 152]
        LS_RET = [TMP[:, COLS_AT + 8 * i:COLS_AT + 8 * i + 8] for i in range(5)]

        z_spill = nc.dram_tensor("z_spill", (P, MLC, LAT), F32).ap()
        v_spill = nc.dram_tensor("v_spill", (P, 4, 2048), F32).ap()
        c_spill = nc.dram_tensor("c_spill", (P, 4, 1024), F32).ap()
        x_spill = nc.dram_tensor("x_spill", (P, DC, TOK), F32).ap()
        o_spill = nc.dram_tensor("o_spill", (P, 2, 4096), F32).ap()

        o_by_head = o_spill.rearrange("p t (d h n) -> p t d h n", d=2, h=ML_HEADS)

        PS = [ctx.enter_context(nc.psum_tensor(f"bank{i}", [P, 512], F32)) for i in range(8)]

        sems = {}

        def S(name):
            if name not in sems:
                sems[name] = ctx.enter_context(nc.semaphore(name))
            return sems[name]

        raw_full = [S(f"raw_full{s}") for s in range(SLOTS)]
        ada_full = [S(f"ada_full{s}") for s in range(2)]

        def vec(name, c=0, n=1):
            return VECS[:, VEC[name] + c:VEC[name] + c + n]

        def mod(layer, chunk, c, stream):
            a = layer * 2 * ADA_TILES + (chunk * DC + c) * 2 + stream
            return MOD[:, a:a + 1]

        STREAMS = ((0, slice(0, LAT)), (1, slice(LAT, TOK)))

        def streams(T):
            return STREAMS[:T // LAT]

        def tmp(i, n=512):
            return TMP[:, 512 * i:512 * i + n]

        def hbuf(c, n=512):
            return tmp((0, 1, 3, 4)[c % 4], n)

        def raw_full_value(n, slot):
            return 4 * (n - slot) + 16

        def tiles(eng, total, body, f):
            n = total // body
            if n > 1:
                with eng.Fori(0, n) as i:
                    for s in range(body):
                        f(i * body + s, i, s)
            else:
                for s in range(n * body):
                    f(s, 0, s)
            for s in range(total - n * body):
                f(n * body + s, n, s)

        def bank_ready(eng, ph, o, group=0):
            groups, n_banks = BANK_GROUP[ph]
            if o < n_banks - 1:
                eng.wait_ge(S("bank_done"), BANKS_BEFORE[ph, group] + o + 1)
            else:
                eng.wait_ge(S("tile_done"), FIRST[ph] + COUNT[ph] // groups * (group + 1))

        class Chain:

            def __init__(self, eng, sem):
                self.eng, self.sem, self.at = eng, sem, 0

            def __call__(self, ins):
                self.at = self.at + 1
                ins.then_inc(self.sem, 1)
                self.eng.wait_ge(self.sem, self.at)

        block = ctx.enter_context(nc.Block())

        @block.sync
        def _(sp):
            sp.dma_start(C_ROWS[:, 0:2, :], c_rows_d[:, 0:2, :]).then_inc(S("c_rows_in"), 16)
            for n in range(ADA_FIRST):
                sp.dma_start(ADA_RAW[:, n, :], ada[n]).then_inc(S(f"ada_first{n // 4}"), 16)
            for n in range(SLOTS):
                sp.dma_start(RAW[:, n, :], weights[n]).then_inc(raw_full[n], 16)
            sp.dma_start(C_ROWS[:, 2:4, :], c_rows_d[:, 2:4, :]).then_inc(S("c_rows2_in"), 16)
            for n in range(SLOTS, SLOTS + LOOKAHEAD):
                sp.wait_ge(S("w_lo_done"), n + 1 - SLOTS)
                sp.dma_start(RAW[:, n % SLOTS, :], weights[n]).then_inc(raw_full[n % SLOTS], 16)

            def load_ada(g, slot, area):
                sp.dma_start(area[1][:, slot, :], ada[g + ADA_FIRST]).then_inc(ada_full[slot], 16)

            def rows_and_ada(g, layer, area):
                first = 0 if layer < 2 else 2
                sp.wait_ge(S("ada_used"), g)
                sp.dma_start(area[2][:, :, :], c_spill[:, first:first + 2, :]).then_inc(S("c_rows_back"), 16)
                for slot in range(2):
                    load_ada(g + slot, slot, area)

            def load_phase(ph, n_ada=0, g0=0, area=None, goes_on=False, at_tile=0):
                n0 = FIRST[ph] + SLOTS + LOOKAHEAD + at_tile
                total = COUNT[ph] - at_tile - (SLOTS if ph == PHASES[-1][0] else 0)
                if ph == "ffn0_in" and not at_tile:
                    total = n_ada
                paired = n_ada if goes_on or not n_ada else n_ada - 4

                def step(t, s, with_ada):
                    slot = (n0 + s) % SLOTS
                    sp.wait_ge(S("w_lo_done"), t + (n0 + 1 - SLOTS))
                    sp.dma_start(RAW[:, slot, :], weights[t + n0]).then_inc(raw_full[slot], 16)
                    if with_ada:
                        sp.wait_ge(S("ada_used"), t + (g0 + 1))
                        load_ada(t + (g0 + 2), s % 2, area)

                tiles(sp, paired, 4, lambda t, i, s: step(t, s, True))
                for t in range(paired, n_ada):
                    step(t, t, t < n_ada - 2)
                tiles(sp, total - n_ada, 4, lambda t, i, s: step(t + n_ada, s + n_ada, False))

            for slot in range(2):
                load_ada(slot, slot, AREA_A)
            load_phase("ret_qk", 16, 0, AREA_A, goes_on=True)
            sp.wait_ge(S("silu_c_done"), 3)
            sp.dma_start(c_spill, C_ROWS[:, :, :]).then_inc(S("stored"), 16)
            load_phase("ret_v", 16, 16, AREA_A)
            load_phase("ret_g")
            sp.wait_ge(S("stored"), 16)
            sp.wait_ge(S("ret_y_done"), 16)
            rows_and_ada(32, 1, AREA_B)
            load_phase("ret_out", 16, 32, AREA_B)
            sp.wait_ge(S("x_upd"), DC)
            sp.dma_start(x_spill, X[:, :, :]).then_inc(S("stored"), 16)
            sp.wait_ge(S("stored"), 32)
            sp.wait_ge(S("raw_done"), 2 * DC)
            rows_and_ada(48, 1, AREA_G)
            load_phase("ffn0_in", 32, 48, AREA_G)
            rows_and_ada(80, 3, AREA_G)
            load_phase("ffn0_in", 12, 80, AREA_G, at_tile=32)
            sp.wait_ge(S("tile_done"), FIRST["ffn0_out"])
            rows_and_ada(92, 3, AREA_B)
            sp.dma_start(X[:, :, :], x_spill).then_inc(S("x_back"), 16)
            load_phase("ffn0_out", 22, 92, AREA_B)
            load_phase("diff_qk")
            load_phase("diff_v")
            load_phase("diff_out")
            load_phase("ffn1_in")
            rows_and_ada(114, 3, AREA_E)
            load_phase("ffn1_out", 6, 114, AREA_E)
            load_phase("pw1")
            load_phase("pw2")
            rows_and_ada(120, 3, AREA_F)
            load_phase("mlp0a_in", 16, 120, AREA_F, goes_on=True)
            load_phase("mlp0a_out", 16, 136, AREA_F, goes_on=True)
            load_phase("mlp0b_in", 16, 152, AREA_F, goes_on=True)
            load_phase("mlp0b_out", 8, 168, AREA_F)
            for ph, _ in PHASES[PHASES.index(("up_x", 16)):]:
                load_phase(ph)
            sp.wait_ge(S("x_final"), DC)
            sp.dma_start(out_d, X[:, :, 0:LAT]).then_inc(S("stored"), 16)
            sp.wait_ge(S("stored"), 48)

        @block.gpsimd
        def _(pool):
            pool.dma_start(VECS[:, :], vecs_d).then_inc(S("vecs_in"), 16)
            pool.dma_start(X[:, :, :], x_t).then_inc(S("x_in"), 16)
            pool.dma_start(IDENT[:, :], consts_d[0]).then_inc(S("consts_in"), 16)
            pool.dma_start(ONES[:, :], consts_d[1]).then_inc(S("consts_in"), 16)
            pool.dma_start(ROPE[:, :, :, :], ret_rope_d).then_inc(S("consts_in"), 16)

            def lo_split(m, T):
                for c in range(DC):
                    pool.wait_ge(S("h_hi_done"), m * DC + c + 1)
                    pool.tensor_tensor(HLO[:, c, 0:T], hbuf(c, T), HHI[:, c, 0:T].bitcast(F32), SUB)\
                        .then_inc(S("h_lo_done"), 1)

            for n in range(LOOKAHEAD):
                pool.wait_ge(S("w_hi_done"), n + 1)
                pool.tensor_tensor(WLO[:, n, :], RAW[:, n, :], WHI[:, n, :].bitcast(F32), SUB)\
                    .then_inc(S("w_lo_done"), 1)
            lo_split(0, TOK)
            for t in range(16):
                pool.wait_ge(S("qk_free"), 8 + t + 1)
                pool.tensor_tensor(QK[:, t, 0:LAT], QK[:, t, 0:LAT], tmp(4)[:, t % 2 * LAT:(t % 2 + 1) * LAT], ADD)\
                    .then_inc(S("qk_rope_done"), 1)
            pool.wait_ge(S("tile_done"), FIRST["ret_g"] + COUNT["ret_g"])
            pool.dma_start(DECAY_E[:, :, :], ret_decay_d).then_inc(S("decay_in"), 16)
            lo_split(1, TOK)
            pool.wait_ge(S("tile_done"), FIRST["ffn0_out"] + COUNT["ffn0_out"])
            pool.dma_start(DTAB[:, :], diff_tab_d).then_inc(S("diff_tab_in"), 16)
            pool.dma_start(DLAM[:, :], lam_d).then_inc(S("diff_tab_in"), 16)
            lo_split(2, TOK)
            own = Chain(pool, S("pool_own"))
            for u in range(16):
                dst = DK[:, u, 0:LAT] if u < 8 else DQ[:, u - 8, :]
                pool.wait_ge(S("dqk_rot"), u + 1)
                own(pool.tensor_tensor(dst, dst, D_COS, MUL))
                pool.wait_ge(S("dqk_sin"), u + 1)
                pool.tensor_tensor(dst, dst, DRT[:, u % 2, :], ADD).then_inc(S("dqk_rope"), 1)
            for h in range(DIFF_HEADS):
                pool.wait_ge(S("do_hi_done"), h + 1)
                pool.tensor_tensor(DOLO[:, h, :], DO[:, h, :], DOHI[:, h, :].bitcast(F32), SUB)\
                    .then_inc(S("do_lo_done"), 1)
            lo_split(3, LAT)
            pool.wait_ge(S("h_lo_done"), 3 * DC)
            pool.dma_start(X[:, :, LAT:TOK], ctx2_t).then_inc(S("x_in"), 16)
            pool.wait_ge(S("tile_done"), FIRST["ffn1_out"] + COUNT["ffn1_out"])
            own(pool.memset(CIN[:, :, :], 0.0))
            lo_split(4, TOK)
            for p in range(DC):
                if p >= 2:
                    pool.wait_ge(S("conv_acc_done"), p - 1)
                acc = CACCP[:, p % 2, :]
                for j in range(1, POOL_TAPS):
                    n = POOL_TAPS * p + j
                    pool.wait_ge(S("tap_done"), n + 1)
                    first = CTAP[:, (n - 1) % TAP_RING, :] if j == 1 else acc
                    own(pool.tensor_tensor(acc, first, CTAP[:, n % TAP_RING, :], ADD))
            def relu_lo(j, T):
                for n in range(2):
                    def tile(t, i, s, done=16 * (2 * j + n)):
                        pool.wait_ge(S("m_sq_done"), t + (done + 1))
                        pool.wait_ge(S("m_hi_done"), t + (done + 1))
                        pool.tensor_tensor(MLO[:, t, 0:T], tmp(s % 2, T), MHI[:, t, 0:T].bitcast(F32), SUB)\
                            .then_inc(S("mlp_free"), 1)
                    tiles(pool, 16, 8, tile)

            lo_split(5, TOK)
            relu_lo(0, TOK)
            lo_split(6, TOK)
            pool.dma_start(X[:, 0:3, LAT:TOK], w_gate_d).then_inc(S("ml_tables_in"), 16)
            pool.wait_ge(S("z_free"), 8 + MLC)
            pool.dma_start(z_spill, MZ[:, :, :]).then_inc(S("z_spilled"), 16)
            pool.wait_ge(S("z_spilled"), 16)
            pool.dma_start(BO[:, :], b_o_d).then_inc(S("ml_tables_in"), 16)
            pool.wait_ge(S("v_done"), 16)
            pool.dma_start(v_spill, MV[:, :, :]).then_inc(S("v_spilled"), 16)
            for g in range(4):
                pool.wait_ge(S("o_done"), 4 * (g + 1))
                pool.dma_start(o_spill[:, :, 1024 * g:1024 * (g + 1)], MOG[:, g % 2, :, :])\
                    .then_inc(S(f"o_spilled{g % 2}"), 16)
            pool.wait_ge(S("tile_done"), FIRST["ml_k"] + COUNT["ml_k"])
            pool.wait_ge(S("v_spilled"), 16)
            pool.dma_start(MV2[:, :, :], v_spill).then_inc(S("v_back"), 16)
            pool.dma_start(ROWS[0:36, 10, :], sel_d).then_inc(S("v_back"), 16)
            pool.wait_ge(S("rows_done"), 1)
            pool.dma_start(tmp(4)[:, 256:512], consts_d[2:4].rearrange("a p n -> p a n")).then_inc(S("tri_in"), 16)
            pool.wait_ge(S("rb_copy"), 8)
            for g in range(2):
                pool.wait_ge(S(f"o_spilled{g}"), 32)
            for h in range(ML_HEADS):
                if h:
                    pool.wait_ge(S("head_done"), 2 * h)
                pool.dma_start(MO2[:, :, :, :], o_by_head[:, :, :, h, :])\
                    .then_inc(S("o_back"), 16)
            pool.wait_ge(S("ml_scores_done"), ML_HEADS)
            pool.dma_start(MZ2[:, :, :], z_spill).then_inc(S("z_back"), 16)
            for c in range(MLC):
                pool.wait_ge(S("ml_y_hi"), c + 1)
                pool.tensor_tensor(MYLO[:, c, :], tmp(c % 4, LAT), MYHI[:, c, :].bitcast(F32), SUB)\
                    .then_inc(S("ml_y_lo"), 1)
            lo_split(7, LAT)
            relu_lo(1, LAT)

        @block.tensor
        def _(pe):
            mm = nc.tensor.matmul

            def split_mm(out, lhs, rhs, start, stop):
                mm(out, lhs[0], rhs[0], start=start, stop=False)
                mm(out, lhs[0], rhs[1], start=False, stop=False)
                return mm(out, lhs[1], rhs[0], start=False, stop=stop)

            def w(slot, a, n):
                return WHI[:, slot, a:a + n], WLO[:, slot, a:a + n]

            def gemm_rows(ph, T, m, free, body=8, granted=0, upd0=None, before=None, after=None):
                g0, kinds = FIRST[ph], len(free)
                for name in free:
                    pe.sem_inc(S(name), 8 // kinds)

                def tile(t, i, s):
                    slot, bank = (g0 + s) % SLOTS, s % 8
                    pe.wait_ge(S("w_lo_done"), t + (g0 + 1))
                    pe.wait_ge(S(free[s % kinds]), i * (body // kinds) + (granted + s // kinds + 1))
                    if upd0 is not None and isinstance(t, int) and t < 8:
                        pe.wait_ge(S("x_upd"), upd0 + t + 1)
                    for k in range(DC):
                        last = split_mm(PS[bank][:, 0:T], w(slot, k * P, P), (HHI[:, k, 0:T], HLO[:, k, 0:T]),
                                        k == 0, k == DC - 1)
                    last.then_inc(S("tile_done"), 1)

                for s in range(LOOKAHEAD):
                    pe.wait_ge(S("w_lo_done"), g0 + s + 1)
                    pe.wait_ge(S(free[s % kinds]), granted + s // kinds + 1)
                if upd0 is not None:
                    pe.wait_ge(S("x_upd"), upd0 + LOOKAHEAD)
                for k in range(DC):
                    pe.wait_ge(S("h_lo_done"), m * DC + k + 1)
                    for s in range(LOOKAHEAD):
                        last = split_mm(PS[s][:, 0:T], w((g0 + s) % SLOTS, k * P, P),
                                        (HHI[:, k, 0:T], HLO[:, k, 0:T]), k == 0, k == DC - 1)
                        if k == DC - 1:
                            last.then_inc(S("tile_done"), 1)
                if after:
                    after(LOOKAHEAD - 1)
                for s in range(LOOKAHEAD, body):
                    if before:
                        before(s)
                    tile(s, 0, s)
                    if after:
                        after(s)
                n = COUNT[ph] // body
                if n > 2:
                    with pe.Fori(1, n) as i:
                        for s in range(body):
                            tile(i * body + s, i, s)
                for t in range(n * body if n > 2 else body, COUNT[ph]):
                    tile(t, t // body, t % body)

            def gemm_cols(ph, T, hi, lo, ready, ready_base, bank_left=None):
                g0, n = FIRST[ph], COUNT[ph]
                for k in range(n):
                    slot = (g0 + k) % SLOTS
                    pe.wait_ge(S("w_lo_done"), g0 + k + 1)
                    pe.wait_ge(S(ready), ready_base + k + 1)
                    for o in range(DC):
                        if k == 0 and bank_left is not None:
                            pe.wait_ge(S(bank_left[0]), bank_left[1] + o + 1)
                        last = split_mm(PS[o][:, 0:T], w(slot, o * P, P), (hi[:, k, 0:T], lo[:, k, 0:T]),
                                        k == 0, k == n - 1)
                        if k == n - 1 and o < DC - 1:
                            last.then_inc(S("bank_done"), 1)
                    last.then_inc(S("tile_done"), 1)

            def gemm_tokens(ph, group, n_k, hi, lo, n_t, bank0, first_wait):
                g0 = FIRST[ph] + group * n_k
                for k in range(n_k):
                    slot = (g0 + k) % SLOTS
                    pe.wait_ge(S("w_lo_done"), g0 + k + 1)
                    for t in range(n_t):
                        tok = slice(t * P, (t + 1) * P)
                        for half in range(2):
                            if k == 0:
                                first_wait(2 * t + half)
                            last = split_mm(PS[bank0 + 2 * t + half][:, :], (hi[:, k, tok], lo[:, k, tok]),
                                            w(slot, half * 512, 512), k == 0, k == n_k - 1)
                            if k == n_k - 1 and (t, half) != (n_t - 1, 1):
                                last.then_inc(S("bank_done"), 1)
                    last.then_inc(S("tile_done"), 1)

            def square_sums(q, T, bank):
                for c in range(DC):
                    pe.wait_ge(S("sq_done"), q * DC + c + 1)
                    mm(PS[bank][:, 0:T], ONES[:, :], tmp(3 + c % 2, T), start=c == 0, stop=c == DC - 1)\
                        .then_inc(S("sq_used"), 1)

            def feature_sums(z, T, ready, ready_base, bank):
                for c in range(DC):
                    pe.wait_ge(S(ready), ready_base + c + 1)
                    last = mm(PS[bank][:, 0:T], ONES[:, :], z[:, c, 0:T], start=c == 0, stop=c == DC - 1)
                last.then_inc(S("ln_sum_done"), 1)

            pe.wait_ge(S("consts_in"), 48)
            square_sums(0, TOK, 0)
            pe.wait_ge(S("silu_c_done"), 1)
            for n in range(ADA_VECTOR, ADA_FIRST):
                pe.wait_ge(S(f"ada_first{n // 4}"), 16 * 4)
                col = 2 * (n - ADA_VECTOR)
                for k in range(DC):
                    last = mm(PS[7][:, col:col + 2], ADA_RAW[:, n, k * P:(k + 1) * P], vec("c_cols", 2 * k, 2),
                              start=k == 0, stop=k == DC - 1)
            last.then_inc(S("ada_pe_done"), 1)
            pe.wait_ge(S("var_done"), 1)
            gemm_rows("ret_qk", TOK, 0, ["qk_free"], 16)
            for grp in range(2):
                def rv_free(b, grp=grp):
                    if grp == 0:
                        pe.wait_ge(S("qk_free"), 8 + 8 + b + 1)
                    elif b == 0:
                        pe.wait_ge(S("v_free"), 8)
                gemm_tokens("ret_v", grp, 8, HHI, HLO, 4, 0, rv_free)
            pe.wait_ge(S("v_free"), 16)
            gemm_rows("ret_g", TOK, 0, ["rg_free"])
            pe.wait_ge(S("rg_free"), 8 + 16)

            pe.wait_ge(S("qk_rope_done"), 16)
            for h in range(RET_HEADS):
                if h:
                    pe.wait_ge(S("att_done"), 3 * h)
                for b, (key0, q0) in enumerate(((0, 0), (LAT, 0), (LAT, LAT))):
                    for j in range(2):
                        for d in range(2):
                            last = mm(PS[b][:, j * LAT:(j + 1) * LAT],
                                      QK[:, 8 + 2 * h + d, key0 + j * P:key0 + (j + 1) * P],
                                      QK[:, 2 * h + d, q0:q0 + LAT], start=d == 0, stop=d == 1)
                    last.then_inc(S("score_done"), 1)

                def ret_values(t):
                    pe.wait_ge(S("att_done"), 3 * h + (2 if t < 2 else 3))
                    if h:
                        pe.wait_ge(S("on_done"), 4 * (h - 1) + t + 1)
                    i0 = (t % 2) * P
                    keys = ((0, 0), (1, 1), (2, 2), (3, 3)) if t < 2 else ((4, 2), (5, 3))
                    for n, (a, v) in enumerate(keys):
                        last = mm(PS[3 + t][:, :], ATT[:, a, i0:i0 + P], RV[:, v, 512 * h:512 * (h + 1)],
                                  start=n == 0, stop=n == len(keys) - 1)
                    last.then_inc(S("ret_o_done"), 1)

                for t in range(4):
                    ret_values(t)
                for t in range(4):
                    pe.wait_ge(S("on_done"), 4 * h + t + 1)
                    if h or t:
                        pe.wait_ge(S("ret_y_done"), 4 * h + t)
                    for f in range(4):
                        last = nc.tensor.transpose(PS[7][:, f * P:(f + 1) * P], ON[:, t % 2, f * P:(f + 1) * P],
                                                   IDENT[:, :])
                    last.then_inc(S("on_t_done"), 1)
            pe.wait_ge(S("ret_y_done"), 16)
            gemm_cols("ret_out", TOK, YHI, YLO, "ret_y_lo_done", 0)

            def ffn(layer, T, q, m, xbase, in_free):
                pe.wait_ge(S("x_upd"), xbase - DC + 1)
                square_sums(q, T, 0)
                pe.wait_ge(S("var_done"), q + 1)
                gemm_rows(f"ffn{layer}_in", T, m, in_free)
                for name in in_free:
                    pe.wait_ge(S(name), 4 + 22)
                fhi, flo = (FHI, FLO) if layer == 0 else (FHI1, FLO1)
                gemm_cols(f"ffn{layer}_out", T, fhi, flo, "f_lo_done", FFN_C * layer)

            ffn(0, TOK, 1, 1, 8, ["ffn0_a_free", "ffn0_g_free"])

            pe.wait_ge(S("x_upd"), 16 - DC + 1)
            square_sums(2, TOK, 0)
            pe.wait_ge(S("var_done"), 3)
            g0 = FIRST["diff_qk"]
            for t in range(16 + 3):
                if t == 0:
                    for a in range(LOOKAHEAD):
                        pe.wait_ge(S("w_lo_done"), g0 + a + 1)
                    for k in range(DC):
                        pe.wait_ge(S("h_lo_done"), 2 * DC + k + 1)
                        for a in range(LOOKAHEAD):
                            last = split_mm(PS[a][:, :], w((g0 + a) % SLOTS, k * P, P), (HHI[:, k, :], HLO[:, k, :]),
                                            k == 0, k == DC - 1)
                            if k == DC - 1:
                                last.then_inc(S("tile_done"), 1)
                elif LOOKAHEAD <= t < 16:
                    T = TOK if t < 8 else LAT
                    slot = (g0 + t) % SLOTS
                    pe.wait_ge(S("w_lo_done"), g0 + t + 1)
                    if t >= 4:
                        pe.wait_ge(S("dqk_raw"), t - 3)
                    for k in range(DC):
                        last = split_mm(PS[t % 4][:, 0:T], w(slot, k * P, P), (HHI[:, k, 0:T], HLO[:, k, 0:T]),
                                        k == 0, k == DC - 1)
                    last.then_inc(S("tile_done"), 1)
                u = t - 1
                if u == 0:
                    pe.wait_ge(S("diff_tab_in"), 32)
                if 0 <= u < 16:
                    T = TOK if u < 8 else LAT
                    pe.wait_ge(S("dqk_sq"), u + 1)
                    if u >= 2:
                        pe.wait_ge(S("dqk_var"), u - 1)
                    mm(PS[4 + u % 2][:, 0:T], D_BLOCK, DSQ[:, u % 2, 0:T], start=True, stop=True)\
                        .then_inc(S("dqk_stat"), 1)
                u = t - 3
                if 0 <= u < 16:
                    pe.wait_ge(S("dqk_norm"), u + 1)
                    if u >= 2:
                        pe.wait_ge(S("dqk_sin"), u - 1)
                    src = DK[:, u, 0:LAT] if u < 8 else DQ[:, u - 8, :]
                    mm(PS[6 + u % 2][:, 0:LAT], D_ROT, src, start=True, stop=True).then_inc(S("dqk_rot"), 1)

            def dv_free(b):
                if b < 4:
                    pe.wait_ge(S("dqk_raw"), 12 + b + 1)
                elif b < 6:
                    pe.wait_ge(S("dqk_var"), 14 + b - 4 + 1)
                else:
                    pe.wait_ge(S("dqk_sin"), 14 + b - 6 + 1)
            gemm_tokens("diff_v", 0, 8, HHI, HLO, 4, 0, dv_free)
            pe.wait_ge(S("v_free"), 24)
            pe.wait_ge(S("dqk_rope"), 16)
            for u in range(16 + 3):
                if u < 16:
                    h, t = u // 2, u % 2
                    if u >= 2:
                        pe.wait_ge(S("d_exp"), 2 * (u - 1))
                    for m in range(2):
                        part = slice(64 * m, 64 * (m + 1))
                        mm(PS[2 * (u % 2) + m][:, :], DQ[part, h, t * P:(t + 1) * P], DK[part, h, :],
                           start=True, stop=True).then_inc(S("d_score"), 1)
                a = u - 2
                if 0 <= a < 16:
                    pe.wait_ge(S("d_p"), a + 1)
                    if a >= 2:
                        pe.wait_ge(S("d_pt"), a - 1)
                    for c in range(4):
                        last = nc.tensor.transpose(PS[4 + a % 2][:, c * P:(c + 1) * P],
                                                   DP[:, a % 2, c * P:(c + 1) * P], IDENT[:, :])
                    last.then_inc(S("d_tr"), 1)
                b = u - 3
                if 0 <= b < 16:
                    h, t = b // 2, b % 2
                    pe.wait_ge(S("d_pt"), b + 1)
                    if h >= 2:
                        pe.wait_ge(S("d_ocopy"), h - 1)
                    for c in range(4):
                        last = mm(PS[6 + h % 2][:, t * P:(t + 1) * P], DV[:, c, h * P:(h + 1) * P],
                                  DPT[:, b % 2, c * P:(c + 1) * P], start=c == 0, stop=c == 3)
                    last.then_inc(S("d_pv"), 1)
            for h in range(DIFF_HEADS):
                pe.wait_ge(S("do_sq"), h + 1)
                if h >= 2:
                    pe.wait_ge(S("do_var"), h - 1)
                mm(PS[h % 2][:, 0:LAT], ONES[:, :], tmp(3 + h % 2, LAT), start=True, stop=True)\
                    .then_inc(S("do_stat"), 1)
            pe.wait_ge(S("do_var"), 8)
            gemm_cols("diff_out", LAT, DOHI, DOLO, "do_lo_done", 0)
            ffn(1, LAT, 3, 3, 24, ["ffn1_a_free", "ffn1_g_free"])

            pe.wait_ge(S("x_upd"), 32)
            def conv_bank_left(t):
                if t >= 8 and t % 2 == 0:
                    pe.wait_ge(S("conv_acc_done"), (t - 8) // 2 + 1)

            def conv_taps(t):
                if t % 2 and t < 15:
                    return
                p = t // 2 if t == 15 else t // 2 - 1
                pe.wait_ge(S("conv_diag_done"), p + 1)
                pe.wait_ge(S("pw1_a_free"), 4 + p + 1)
                for out0, rows, in0, pitch, n in ((0, CONV_ROWS, 0, ROW_PADDED, GRID_W), (LAT, 1, CONV_CTX, CTX, CTX)):
                    for j in range(PE_TAPS):
                        first = in0 + DVE_TAPS + j
                        last = mm(PS[2 * p % 8][:, out0:out0 + rows * n], CDIAG[:, p % 2, j, :],
                                  CIN[:, p, first:first + rows * pitch].rearrange("p (r w) -> p r w", w=pitch)[:, :, 0:n],
                                  start=j == 0, stop=j == PE_TAPS - 1)
                last.then_inc(S("conv_pe_done"), 1)

            gemm_rows("pw1", TOK, 4, ["pw1_gate_free", "pw1_a_free"], 16, before=conv_bank_left, after=conv_taps)
            pe.wait_ge(S("pw1_a_free"), 4 + 8)
            feature_sums(CZ, TOK, "conv_z_done", 0, 0)
            square_sums(4, TOK, 1)
            pe.wait_ge(S("var_done"), 5)
            gemm_cols("pw2", TOK, HHI, HLO, "cz_lo_done", 0)

            def mlp(j, T, q, m, xbase):
                feature_sums(X, T, "x_upd", xbase, 0)
                square_sums(q, T, 1)
                pe.wait_ge(S("var_done"), q + 1)
                for n, half in enumerate("ab"):
                    before = 24 * (2 * j + n)
                    gemm_rows(f"mlp{j}{half}_in", T, m, ["mlp_free"], granted=before, upd0=xbase + 8 if n else None)
                    gemm_cols(f"mlp{j}{half}_out", T, MHI, MLO, "mlp_free", before + 8,
                              ("m_relu_done", 16 * (2 * j + n) + 8))
                feature_sums(X, T, "x_upd", xbase + 16, 0)
                square_sums(q + 1, T, 1)
                pe.wait_ge(S("var_done"), q + 2)

            mlp(0, TOK, 5, 5, 32 + 0)

            gemm_rows("up_x", TOK, 6, ["up_free"])
            pe.wait_ge(S("up_free"), 8 + 16)
            gemm_rows("up_z", LAT, 6, ["z_free"])
            pe.wait_ge(S("z_free"), 8 + 16)
            for grp in range(2):
                def mv_free(b, grp=grp):
                    if grp and b == 0:
                        pe.wait_ge(S("v_done"), 8)
                gemm_tokens("ml_v", grp, 16, XMHI, XMLO, 4, 0, mv_free)
            pe.wait_ge(S("v_done"), 16)
            pe.wait_ge(S("ml_tables_in"), 32)

            def gate_part(part, f):
                return X[:, part, LAT + 16 * f:LAT + 16 * f + 16]

            for f in range(MLC + 1):
                if f < MLC:
                    if f >= 2:
                        pe.wait_ge(S("vt_done"), f - 1)
                    for t in range(4):
                        last = nc.tensor.transpose(PS[1 + f % 2][:, t * P:(t + 1) * P],
                                                   MV[:, t, f * P:(f + 1) * P], IDENT[:, :])
                    last.then_inc(S("vt_tr"), 1)
                if f:
                    pe.wait_ge(S("vt_done"), f)
                    last = mm(PS[0][0:16, :], gate_part(2, f - 1), tmp((f - 1) % 2), start=f == 1, stop=f == MLC)
                    last.then_inc(S("gate_mm"), 1)
            for grp in range(4):
                def mo_free(b, grp=grp):
                    if b == 0 and grp == 0:
                        pe.wait_ge(S("gate_acc"), 1)
                    elif b == 0 and grp >= 2:
                        pe.wait_ge(S("o_add"), 4 * (grp - 1))
                gemm_tokens("ml_o", grp, 16, XMHI, XMLO, 2, 4 * (grp % 2), mo_free)
            pe.wait_ge(S("o_add"), 16)

            def gemm_inner(ph, grp, x_base, kdone):
                g0 = FIRST[ph] + 16 * grp
                for k in range(MLC):
                    slot = (g0 + k) % SLOTS
                    pe.wait_ge(S("w_lo_done"), g0 + k + 1)
                    pe.wait_ge(S("xc_lo_done"), k + 1)
                    for o in range(DC):
                        last = split_mm(PS[o][:, :], w(slot, o * P, P), (XMHI[:, k, :], XMLO[:, k, :]),
                                        k == 0, k == MLC - 1)
                        if k == MLC - 1 and o < DC - 1:
                            last.then_inc(S("bank_done"), 1)
                    last.then_inc(S("tile_done"), 1)
                pe.wait_ge(S(kdone), 8 * (grp + 1))

            for grp in range(2):
                gemm_inner("ml_q", grp, 0, "q_done")
                for c in range(DC):
                    wg = gate_part(0, 8 * grp + c)
                    mm(PS[0][0:16, 0:LAT], wg, MQ[:, 8 * grp + c, :], start=c == 0, stop=c == DC - 1)\
                        .then_inc(S("gate_mm"), 1)
                for c in range(DC):
                    wg = gate_part(0, 8 * grp + c)
                    mm(PS[0][0:16, LAT:TOK], wg, MQC[:, c, :], start=c == 0, stop=c == DC - 1)\
                        .then_inc(S("gate_mm"), 1)
                pe.wait_ge(S("gate_acc"), 2 + grp)
            for grp in range(2):
                gemm_inner("ml_k", grp, 0, "k_done")
                for c in range(DC):
                    mm(PS[0][0:16, :], gate_part(1, 8 * grp + c), MK[:, 8 * grp + c, :], start=c == 0, stop=c == DC - 1)\
                        .then_inc(S("gate_mm"), 1)
                pe.wait_ge(S("gate_acc"), 4 + grp)

            def ml_scores(h):
                if h >= 2:
                    pe.wait_ge(S("ml_p"), 4 * (h - 1))
                for j in range(4):
                    for d in range(4):
                        last = mm(PS[2 * (h % 2) + j // 2][:, (j % 2) * LAT:(j % 2 + 1) * LAT],
                                  MK[:, 4 * h + d, j * P:(j + 1) * P], MQ[:, 4 * h + d, :],
                                  start=d == 0, stop=d == 3)
                last.then_inc(S("ml_scores_done"), 1)

            for g in range(2):
                mm(PS[4 + g][0:36, :], vec("gate_sel", 36 * g, 36)[0:16, :], tmp(4)[0:16, :], start=True, stop=True)\
                    .then_inc(S("gate_rows"), 1)
            for h in range(2):
                ml_scores(h)
            pe.wait_ge(S("rows_done"), 1)
            for d in range(2):
                part = slice(32 * d, 32 * d + 4)
                for j in range(6):
                    if d:
                        row = ROWS[part, 12 if j < 4 else 14, (j % 4) * P:(j % 4 + 1) * P]
                    else:
                        a = (CTX if j < 2 or j >= 4 else 0) + (j % 2) * P
                        row = ROWS[part, 5 if j < 4 else 6, a:a + P]
                    last = mm(PS[4 + 3 * d][:, (d * 6 + j) * 4:(d * 6 + j) * 4 + 4], row, IDENT[part, part],
                              start=True, stop=True)
                last.then_inc(S("ml_cols"), 1)
            pe.wait_ge(S("v_back"), 32)
            for h in range(ML_HEADS):
                for d in range(2):
                    part = slice(32 * d, 32 * d + 4)
                    row = ROWS[part, 14, LAT:2 * LAT] if d else ROWS[part, 9, CTX:TOK]
                    n = 2 * h + d
                    if n >= 2:
                        pe.wait_ge(S("rb_copy"), n - 1)
                    mm(PS[5 + n % 2][:, 0:LAT], ROWS[part, 10, h * P:(h + 1) * P], row,
                       start=True, stop=True).then_inc(S("rb_mm"), 1)
            pe.wait_ge(S("rb_copy"), 8)
            pe.wait_ge(S("ml_cols_copy"), 1)
            for h in range(ML_HEADS):
                parts = [(d, t, [j for j in range(4) if j >= 2 or (j <= t if d == 0 else j >= t)])
                         for d in range(2) for t in range(2)]
                pe.wait_ge(S("ml_p"), 4 * h + 4)
                if h >= 2:
                    pe.wait_ge(S("ml_h_done"), 4 * (h - 1))
                for n, (d, t, keys) in enumerate(parts):
                    for i, j in enumerate(keys):
                        last = mm(PS[4 + h % 2][:, n:n + 1], MPT(h, d)[:, j, t * P:(t + 1) * P], ONES[:, 0:1],
                                  start=i == 0, stop=i == len(keys) - 1)
                last.then_inc(S("ml_den"), 1)
                for n, (d, t, keys) in enumerate(parts):
                    m = 4 * h + n
                    if m >= 2:
                        pe.wait_ge(S("ml_h_done"), m - 1)
                    for i, j in enumerate(keys):
                        last = mm(PS[6 + n % 2][:, :], MPT(h, d)[:, j, t * P:(t + 1) * P],
                                  MV2[:, j, 512 * h:512 * (h + 1)], start=i == 0, stop=i == len(keys) - 1)
                    last.then_inc(S("ml_num"), 1)
                if h + 2 < ML_HEADS:
                    ml_scores(h + 2)
            pe.wait_ge(S("hn_done"), 8)
            for f in range(MLC):
                if f >= 4:
                    pe.wait_ge(S("ml_y_done"), f - 3)
                for t in range(2):
                    last = nc.tensor.transpose(PS[f % 4][:, t * P:(t + 1) * P], MH[:, t, f * P:(f + 1) * P],
                                               IDENT[:, :])
                last.then_inc(S("hn_tr"), 1)
            pe.wait_ge(S("ml_y_done"), 16)
            gemm_cols("down", LAT, MYHI, MYLO, "ml_y_lo", 0)
            mlp(1, LAT, 7, 7, 32 + 8 + 16)


        @block.scalar
        def _(act):
            def f(out, in_, func, **kw):
                return nc.scalar.activation(out, in_, func, **kw)

            own = Chain(act, S("act_own"))

            def hi(n, slot, first=False):
                act.wait_ge(raw_full[slot], raw_full_value(n, slot))
                if not first:
                    act.wait_ge(S("tile_done"), n - LOOKAHEAD)
                f(WHI[:, slot, :], RAW[:, slot, :], ACT.Copy).then_inc(S("w_hi_done"), 1)

            def hi_ahead(ph, t, s):
                n0 = FIRST[ph] + LOOKAHEAD
                hi(t + n0, (n0 + s) % SLOTS, first=isinstance(t, int) and t + n0 < SLOTS)

            def weights_only(ph):
                tiles(act, COUNT[ph], SLOTS, lambda t, i, s: hi_ahead(ph, t, s))

            def squares(q, T, z, ready, ready_base):
                for c in range(DC):
                    act.wait_ge(S(ready), ready_base + c + 1)
                    if c >= 2:
                        act.wait_ge(S("sq_used"), q * DC + c - 1)
                    f(tmp(3 + c % 2, T), z[:, c, 0:T], ACT.Square).then_inc(S("sq_done"), 1)
                f(CELL[:, 1:2], ONES[:, 0:1], ACT.Sqrt)
                act.wait_ge(S("var_done"), q + 1)
                f(tmp(2, T), tmp(2, T), ACT.Sqrt).then_inc(S("std_done"), 1)

            def h_hi(m, T):
                for c in range(DC):
                    act.wait_ge(S("raw_done"), m * DC + c + 1)
                    f(HHI[:, c, 0:T], hbuf(c, T), ACT.Copy).then_inc(S("h_hi_done"), 1)

            def log_sigmoid(q, a, e, u, l):
                act.wait_ge(S("ls_abs"), q + 1)
                f(e, a, ACT.Exp, scale=-1.0).then_inc(S("ls_exp"), 1)
                act.wait_ge(S("ls_u"), q + 1)
                f(l, u, ACT.Ln).then_inc(S("ls_ln"), 1)

            act.wait_ge(S("vecs_in"), 16)
            act.wait_ge(S("c_rows_in"), 16)
            f(vec("c_cols", 0, 2 * DC), vec("c_cols", 0, 2 * DC), ACT.Silu).then_inc(S("silu_c_done"), 1)
            f(C_ROWS[:, 0:2, :], C_ROWS[:, 0:2, :], ACT.Silu).then_inc(S("silu_c_done"), 1)
            act.wait_ge(S("x_in"), 16)
            for c in range(DC):
                if c >= 2:
                    act.wait_ge(S("sq_used"), c - 1)
                f(tmp(3 + c % 2), X[:, c, :], ACT.Square).then_inc(S("sq_done"), 1)
            act.wait_ge(S("var_done"), 1)
            f(tmp(2), tmp(2), ACT.Sqrt).then_inc(S("std_done"), 1)
            for n in range(LOOKAHEAD):
                hi(n, n, first=True)
            h_hi(0, TOK)
            act.wait_ge(S("c_rows2_in"), 16)
            f(C_ROWS[:, 2:4, :], C_ROWS[:, 2:4, :], ACT.Silu).then_inc(S("silu_c_done"), 1)

            for t in range(16):
                hi_ahead("ret_qk", t, t)
            for grp in range(2):
                for k in range(8):
                    hi_ahead("ret_v", 8 * grp + k, 8 * grp + k)
                for b in range(1, 8, 2):
                    bank_ready(act, "ret_v", b, grp)
                    f(RV[:, b // 2, 1024 * grp + 512:1024 * grp + 1024], PS[b][:, :], ACT.Copy)\
                        .then_inc(S("v_free"), 1)

            def ret_gate(t, i, s):
                hi_ahead("ret_g", t, s)
                act.wait_ge(S("tile_done"), t + (FIRST["ret_g"] + 1))
                f(RG[:, t, :], PS[s % 8][:, :], ACT.Silu).then_inc(S("rg_free"), 1)
            tiles(act, 16, 8, ret_gate)

            log_sigmoid(0, LS_RET[0], LS_RET[1], LS_RET[2], LS_RET[3])
            act.wait_ge(S("log_gamma_done"), 1)
            act.wait_ge(S("decay_in"), 16)
            for h in range(RET_HEADS):
                if h:
                    act.wait_ge(S("decay_used"), h)
                for n, (table, col) in enumerate(((0, h), (1, 4 + h), (4, h), (5, 4 + h))):
                    last = f(tmp(n), DECAY_E[:, table, :], ACT.Exp, scale=LG[:, col:col + 1])
                last.then_inc(S("decay_exp"), 1)
                for t in range(4):
                    n = 4 * h + t
                    st = 16 * (t % 2)
                    act.wait_ge(S("ret_var"), n + 1)
                    f(RSTAT[:, st + 9:st + 10], RSTAT[:, st + 8:st + 9], ACT.Sqrt).then_inc(S("ret_std"), 1)
                    act.wait_ge(S("ret_nmr"), n + 1)
                    if n >= 2:
                        act.wait_ge(S("on_t_done"), n - 1)
                    f(ON[:, t % 2, :], PS[3 + t][:, :], ACT.Identity, scale=RSTAT[:, st + 10:st + 11],
                      bias=RSTAT[:, st + 11:st + 12]).then_inc(S("on_done"), 1)
            act.wait_ge(S("ret_y_done"), 16)
            for c in range(16):
                f(YHI[:, c, :], RG[:, c, :], ACT.Copy).then_inc(S("ret_y_hi_done"), 1)
            weights_only("ret_out")

            def ffn(layer, T, q, m, x0):
                squares(q, T, X, "x_upd", x0)
                h_hi(m, T)
                ph = f"ffn{layer}_in"
                fhi = FHI if layer == 0 else FHI1

                def tile(t, i, s):
                    hi_ahead(ph, t, s)
                    p = i * 4 + s // 2
                    if s % 2 == 0:
                        act.wait_ge(S("tile_done"), t + (FIRST[ph] + 1))
                        act.wait_ge(S(f"ffn{layer}_g_free"), p + 3)
                        f(tmp(3 + s // 2 % 2, T), PS[s][:, 0:T], ACT.Silu).then_inc(S(f"ffn{layer}_a_free"), 1)
                    else:
                        act.wait_ge(S(f"ffn{layer}_g_free"), p + 5)
                        f(fhi[:, p, 0:T], tmp(s // 2 % 2, T), ACT.Copy).then_inc(S("f_hi_done"), 1)
                tiles(act, COUNT[ph], 8, tile)
                weights_only(f"ffn{layer}_out")

            ffn(0, TOK, 1, 1, 0)

            squares(2, TOK, X, "x_upd", 8)
            h_hi(2, TOK)
            for t in range(16 + 3):
                if t < 16:
                    T = TOK if t < 8 else LAT
                    hi_ahead("diff_qk", t, t)
                    act.wait_ge(S("tile_done"), FIRST["diff_qk"] + t + 1)
                    if t >= 2:
                        act.wait_ge(S("dqk_stat"), t - 1)
                    f(DSQ[:, t % 2, 0:T], PS[t % 4][:, 0:T], ACT.Square).then_inc(S("dqk_sq"), 1)
                    if t >= 4:
                        act.wait_ge(S("dqk_norm"), t - 3)
                    f(DRAWB[:, t % 4, 0:T], PS[t % 4][:, 0:T], ACT.Copy).then_inc(S("dqk_raw"), 1)
                u = t - 1
                if 0 <= u < 16:
                    T = TOK if u < 8 else LAT
                    act.wait_ge(S("dqk_var"), u + 1)
                    f(DRST[:, u % 2, 0:T], DRST[:, u % 2, 0:T], ACT.Sqrt).then_inc(S("dqk_std"), 1)
            for k in range(8):
                hi_ahead("diff_v", k, k)
            for b in range(1, 8, 2):
                bank_ready(act, "diff_v", b)
                f(DV[:, b // 2, 512:1024], PS[b][:, :], ACT.Copy).then_inc(S("v_free"), 1)
            act.wait_ge(S("lam_dot"), 1)
            f(DCOL[:, 2:4], DCOL[:, 2:4], ACT.Exp).then_inc(S("lam_exp"), 1)
            scale = DIFF_DH ** -0.5
            for u in range(16 + 2):
                if u < 16:
                    for m in range(2):
                        col = 4 + 2 * (u % 2) + m
                        act.wait_ge(S("d_max"), 2 * u + m + 1)
                        if m == 0 and u >= 2:
                            act.wait_ge(S("d_p"), u - 1)
                        f(DE[:, u % 2, m, :], PS[2 * (u % 2) + m][:, :], ACT.Exp, scale=scale,
                          bias=DCOL[:, col:col + 1], accum_out=DCOL[:, col + 4:col + 5]).then_inc(S("d_exp"), 1)
                a = u - 2
                if 0 <= a < 16:
                    act.wait_ge(S("d_tr"), a + 1)
                    if a >= 2:
                        act.wait_ge(S("d_pv"), a - 1)
                    f(DPT[:, a % 2, :], PS[4 + a % 2][:, :], ACT.Copy).then_inc(S("d_pt"), 1)
            for h in range(DIFF_HEADS + 1):
                if h < DIFF_HEADS:
                    act.wait_ge(S("d_ocopy"), h + 1)
                    if h >= 2:
                        act.wait_ge(S("do_stat"), h - 1)
                    f(tmp(3 + h % 2, LAT), DO[:, h, :], ACT.Square).then_inc(S("do_sq"), 1)
                g = h - 1
                if 0 <= g:
                    act.wait_ge(S("do_var"), g + 1)
                    f(tmp(1 + g % 2, LAT), tmp(1 + g % 2, LAT), ACT.Sqrt).then_inc(S("do_std"), 1)
            for h in range(DIFF_HEADS):
                act.wait_ge(S("do_norm"), h + 1)
                f(DOHI[:, h, :], DO[:, h, :], ACT.Copy).then_inc(S("do_hi_done"), 1)
            weights_only("diff_out")
            ffn(1, LAT, 3, 3, 16)

            h_hi(4, TOK)
            def conv_z(p):
                acc = CACC[:, 2 * (p % 2), :]
                act.wait_ge(S("conv_acc_done"), p + 1)
                f(CZ[:, p, 0:LAT].rearrange("p (r w) -> p r w", w=GRID_W),
                  acc[:, 0:CONV_CTX].rearrange("p (r w) -> p r w", w=ROW_PADDED)[:, :, 0:GRID_W],
                  ACT.Identity, bias=vec("b_dw", p))
                f(CZ[:, p, LAT:TOK], acc[:, CONV_CTX:CONV_CTX + CTX], ACT.Identity, bias=vec("b_dw", p))\
                    .then_inc(S("conv_z_done"), 1)

            def conv_diag(p):
                if p >= 2:
                    act.wait_ge(S("conv_pe_done"), p - 1)
                for j in range(PE_TAPS):
                    last = f(CDIAG[:, p % 2, j, :], IDENT[:, :], ACT.Copy, scale=vec("w_dw", p * CONV_W + DVE_TAPS + j))
                last.then_inc(S("conv_diag_done"), 1)

            conv_diag(0)
            for t in range(16):
                p, bank = t // 2, t % 8
                hi_ahead("pw1", t, t)
                if t % 2 == 0:
                    act.wait_ge(S("tile_done"), FIRST["pw1"] + t + 1)
                    act.wait_ge(S("pw1_a_free"), p + 3)
                    f(tmp(3 + p % 2), PS[bank][:, :], ACT.Sigmoid, bias=vec("b_pw1", 8 + p))\
                        .then_inc(S("pw1_gate_free"), 1)
                else:
                    act.wait_ge(S("pw1_a_free"), 4 + p + 1)
                    for j in range(POOL_TAPS):
                        n, tap = POOL_TAPS * p + j, CONV_W - POOL_TAPS + j
                        if n >= TAP_RING:
                            before = n - TAP_RING
                            act.wait_ge(S("pool_own"), CONV_ZERO + (POOL_TAPS - 1) * (before // POOL_TAPS)
                                        + max(before % POOL_TAPS, 1))
                        f(CTAP[:, n % TAP_RING, :], CIN[:, p, tap:tap + CONV_OUT], ACT.Copy,
                          scale=vec("w_dw", p * CONV_W + tap)).then_inc(S("tap_done"), 1)
                    if p + 1 < DC:
                        conv_diag(p + 1)
                    if p:
                        conv_z(p - 1)
            conv_z(DC - 1)
            squares(4, TOK, CZ, "z_centered", 0)
            for c in range(DC):
                act.wait_ge(S("cz_norm"), c + 1)
                if c >= 2:
                    act.wait_ge(S("cz_lo_done"), c - 1)
                own(f(tmp(c % 2), CZ[:, c, :], ACT.Silu, scale=vec("conv_ln_g", c), bias=vec("conv_ln_b", c)))
                f(HHI[:, c, :], tmp(c % 2), ACT.Copy).then_inc(S("cz_hi_done"), 1)
            weights_only("pw2")

            def mlp(j, T, q, m, ln):
                squares(q, T, X, "z_centered", ln * DC)
                h_hi(m, T)
                for n, half in enumerate("ab"):
                    ph, before, done = f"mlp{j}{half}_in", 24 * (2 * j + n), 16 * (2 * j + n)

                    def tile(t, i, s):
                        hi_ahead(ph, t, s)
                        act.wait_ge(S("tile_done"), t + (FIRST[ph] + 1))
                        act.wait_ge(S("mlp_free"), t + (before + 7))
                        f(tmp(3 + s % 2, T), PS[s][:, 0:T], ACT.Relu).then_inc(S("m_relu_done"), 1)
                        act.wait_ge(S("m_relu_done"), t + (done + 1))
                        f(MHI[:, t, 0:T], tmp(3 + s % 2, T), ACT.Square).then_inc(S("m_hi_done"), 1)
                    tiles(act, 16, 8, tile)
                    weights_only(f"mlp{j}{half}_out")
                squares(q + 1, T, X, "z_centered", (ln + 1) * DC)

            mlp(0, TOK, 5, 5, 1)

            h_hi(6, TOK)

            def up_x(t, i, s):
                hi_ahead("up_x", t, s)
                act.wait_ge(S("tile_done"), t + (FIRST["up_x"] + 1))
                f(XMHI[:, t, :], PS[s][:, :], ACT.Copy).then_inc(S("up_hi_done"), 1)
            tiles(act, 16, 8, up_x)

            def up_z(t, i, s):
                hi_ahead("up_z", t, s)
                act.wait_ge(S("tile_done"), t + (FIRST["up_z"] + 1))
                f(MZ[:, t, :], PS[s][:, 0:LAT], ACT.Silu).then_inc(S("z_free"), 1)
            tiles(act, 16, 8, up_z)
            for grp in range(2):
                for k in range(16):
                    hi_ahead("ml_v", 16 * grp + k, 16 * grp + k)
                for b in range(1, 8, 2):
                    bank_ready(act, "ml_v", b, grp)
                    f(MV[:, b // 2, 1024 * grp + 512:1024 * grp + 1024], PS[b][:, :], ACT.Copy)\
                        .then_inc(S("v_done"), 1)
            for c in range(MLC):
                act.wait_ge(S("vt_tr"), c + 1)
                if c >= 2:
                    act.wait_ge(S("gate_mm"), c - 1)
                f(tmp(c % 2), PS[1 + c % 2][:, :], ACT.Copy).then_inc(S("vt_done"), 1)
            def x_conv(k):
                act.wait_ge(S("mconv_done"), k + 1)
                f(XC[:, k, 0:LAT], M_ACC[:, 0:LAT], ACT.Silu, bias=vec("ml_b_conv", k))
                f(XC[:, k, LAT:TOK], M_ACC[:, ML_CTX:ML_CTX + CTX], ACT.Silu, bias=vec("ml_b_conv", k))\
                    .then_inc(S("xc_done"), 1)

            act.wait_ge(S("v_spilled"), 16)
            for g in range(4):
                for k in range(16):
                    t = 16 * g + k
                    hi_ahead("ml_o", t, t)
                    if t % 4 == 3:
                        x_conv(t // 4)
                for n in range(4):
                    t, half = n // 2, n % 2
                    o = MOG[:, g % 2, t, half * 512:(half + 1) * 512]
                    act.wait_ge(S("o_add"), 4 * g + n + 1)
                    f(o, o, ACT.Sigmoid).then_inc(S("o_done"), 1)
            act.wait_ge(S("tile_done"), FIRST["ml_q"])
            for k in range(-2, 32):
                if k >= 0:
                    hi_ahead("ml_q", k, k)
                if k + 2 < MLC:
                    f(XMHI[:, k + 2, :], XC[:, k + 2, :], ACT.Copy).then_inc(S("xc_hi_done"), 1)
                if k >= 0 and k % MLC == MLC - 1:
                    grp = k // MLC
                    if grp:
                        act.wait_ge(S("gate_mm"), 32)
                    else:
                        for g in range(2):
                            act.wait_ge(S(f"o_spilled{g}"), 32)
                    for o in range(1, DC, 2):
                        bank_ready(act, "ml_q", o, grp)
                        f(MQ[:, 8 * grp + o, :], PS[o][:, 0:LAT], ACT.Copy)
                        f(MQC[:, o, :], PS[o][:, LAT:TOK], ACT.Copy).then_inc(S("q_done"), 1)
            for grp in range(2):
                for k in range(MLC):
                    hi_ahead("ml_k", MLC * grp + k, MLC * grp + k)
                for o in range(1, DC, 2):
                    bank_ready(act, "ml_k", o, grp)
                    f(MK[:, 8 * grp + o, :], PS[o][:, :], ACT.Copy).then_inc(S("k_done"), 1)
            log_sigmoid(1, ROWS[0:36, 4, :], ROWS[0:36, 5, :], ROWS[0:36, 6, :], ROWS[0:36, 7, :])
            def rb_copies(n0, n1):
                for n in range(n0, n1):
                    act.wait_ge(S("rb_mm"), n + 1)
                    f(X[:, n, LAT:TOK], PS[5 + n % 2][:, 0:LAT], ACT.Copy).then_inc(S("rb_copy"), 1)

            def ml_exps(h, d):
                act.wait_ge(S("ml_arg"), 2 * h + d + 1)
                f(MPT(h, d), MPT(h, d), ACT.Exp).then_inc(S("ml_exp"), 1)

            rb_copies(0, 4)
            ml_exps(0, 0)
            rb_copies(4, 6)
            ml_exps(0, 1)
            rb_copies(6, 8)
            act.wait_ge(S("ml_cols_copy"), 1)
            for d in range(2):
                a = (d * 6 + 4) * 4
                last = f(M_COLS[:, a:a + 8], M_COLS[:, a:a + 8], ACT.Exp)
            last.then_inc(S("exp_m_done"), 1)
            for h in range(1, ML_HEADS):
                for d in range(2):
                    ml_exps(h, d)
            act.wait_ge(S("ret_var"), 17)
            f(GN_VAR, GN_VAR, ACT.Sqrt).then_inc(S("ret_std"), 1)
            act.wait_ge(S("ret_nmr"), 17)
            for h in range(ML_HEADS):
                z = MH[:, 0, 512 * h:512 * (h + 1)]
                f(z, z, ACT.Identity, scale=GN_RSTD[:, h:h + 1], bias=GN_NMR[:, h:h + 1]).then_inc(S("hn_done"), 1)
            for c in range(MLC):
                act.wait_ge(S("ml_y_raw"), c + 1)
                f(MYHI[:, c, :], tmp(c % 4, LAT), ACT.Copy).then_inc(S("ml_y_hi"), 1)
            weights_only("down")
            mlp(1, LAT, 7, 7, 3)

        @block.vector
        def _(dve):
            V = nc.vector
            own = Chain(dve, S("dve_own"))

            def lo(n, slot):
                dve.wait_ge(S("w_hi_done"), n + 1)
                V.tensor_tensor(WLO[:, slot, :], RAW[:, slot, :], WHI[:, slot, :].bitcast(F32), SUB)\
                    .then_inc(S("w_lo_done"), 1)

            def lo_ahead(ph, t, s):
                n0 = FIRST[ph] + LOOKAHEAD
                lo(t + n0, (n0 + s) % SLOTS)

            def ada_product(a, tile, area):
                junk, _, rows = area
                for st in range(2):
                    ins = V.scalar_tensor_tensor(junk[:, :] if st == 0 else tile, tile, 1.0, rows[:, st, :], MUL, MUL,
                                                 accum_out=MOD[:, bass.ds(a * 2 + st, 1)])
                return ins

            def ada_tile(t, i, s, body, g0, area):
                dve.wait_ge(ada_full[s % 2], i * (8 * body) + 16 * ((g0 + s) // 2 + 1))
                if g0 or not isinstance(t, int) or t:
                    dve.wait_ge(S("ada_used"), t + g0)
                ada_product(t + (g0 + ADA_FIRST), area[1][:, s % 2, :], area).then_inc(S("ada_used"), 1)

            def ada_finish(a0, a1):
                for st in range(2):
                    own(V.tensor_tensor(MOD[:, 2 * a0 + st:2 * a1:2], MOD[:, 2 * a0 + st:2 * a1:2],
                                        vec("ada_b", a0, a1 - a0), ADD))
                for a in range(a0, a1, DC):
                    if a // DC % 6 in (1, 4):
                        own(V.tensor_scalar(MOD[:, 2 * a:2 * (a + DC)], MOD[:, 2 * a:2 * (a + DC)], 1.0, None, ADD))

            def rows_back(n):
                dve.wait_ge(S("c_rows_back"), 16 * n)

            def weights_only(ph, n_ada=0, g0=0, area=None):
                def both(t, i, s):
                    lo_ahead(ph, t, s)
                    ada_tile(t, i, s, SLOTS, g0, area)
                tiles(dve, n_ada, SLOTS, both)
                tiles(dve, COUNT[ph] - n_ada, SLOTS, lambda t, i, s: lo_ahead(ph, t + n_ada, s + n_ada))

            def variance(q, T, bank, eps):
                dve.wait_ge(S("sq_used"), DC * (q + 1))
                V.tensor_scalar(tmp(2, T), PS[bank][:, 0:T], 1.0 / D, eps, MUL, ADD).then_inc(S("var_done"), 1)
                dve.wait_ge(S("std_done"), q + 1)
                own(V.reciprocal(tmp(2, T), tmp(2, T)))

            def modulate(m, T, scale, shift, normed=True):
                for c in range(DC):
                    if c >= 4:
                        dve.wait_ge(S("h_lo_done"), m * DC + c - 3)
                    src = X[:, c, :]
                    if normed:
                        src = hbuf(c)
                        own(V.tensor_tensor(hbuf(c, T), X[:, c, 0:T], tmp(2, T), MUL))
                    for st, cols in streams(T):
                        last = V.tensor_scalar(hbuf(c)[:, cols], src[:, cols], scale(c, st), shift(c, st), MUL, ADD)
                    last.then_inc(S("raw_done"), 1)

            def mods(layer, first):
                return (lambda c, st: mod(layer, first + 1, c, st)), (lambda c, st: mod(layer, first, c, st))

            def residual(ph, T, layer, gate, x0):
                for o in range(DC):
                    bank_ready(dve, ph, o)
                    for st, cols in streams(T):
                        last = V.scalar_tensor_tensor(X[:, o, cols], PS[o][:, cols], mod(layer, gate, o, st),
                                                      X[:, o, cols], MUL, ADD)
                    last.then_inc(S("x_upd"), 1)
                dve.wait_ge(S("x_upd"), x0 + DC)

            def layer_norm(ln, q, T, z):
                dve.wait_ge(S("ln_sum_done"), ln + 1)
                own(V.tensor_scalar(tmp(2, T), PS[0][:, 0:T], 1.0 / D, None, MUL))
                for c in range(DC):
                    V.tensor_tensor(z[:, c, 0:T], z[:, c, 0:T], tmp(2, T), SUB).then_inc(S("z_centered"), 1)
                dve.wait_ge(S("z_centered"), DC * (ln + 1))
                variance(q, T, 1, LN_EPS)

            def log_sigmoid(q, x, a, e, u, l, t1, out):
                V.scalar_tensor_tensor(a, x, -1.0, x, MUL, MAX).then_inc(S("ls_abs"), 1)
                dve.wait_ge(S("ls_exp"), q + 1)
                V.tensor_scalar(u, e, 1.0, None, ADD).then_inc(S("ls_u"), 1)
                dve.wait_ge(S("ls_u"), q + 1)
                own(V.tensor_scalar(t1, u, -1.0, None, ADD))
                own(V.tensor_tensor(e, e, t1, SUB))
                own(V.reciprocal(t1, u))
                own(V.tensor_tensor(e, e, t1, MUL))
                dve.wait_ge(S("ls_ln"), q + 1)
                own(V.tensor_tensor(e, e, l, ADD))
                own(V.tensor_scalar(a, x, 0.0, None, MIN))
                own(V.tensor_tensor(out, a, e, SUB))

            dve.wait_ge(S("silu_c_done"), 2)
            for n in range(ADA_VECTOR):
                dve.wait_ge(S(f"ada_first{n // 4}"), 16 * 4)
                own(ada_product(n, ADA_RAW[:, n, :], AREA_A))
                if n == 7:
                    variance(0, TOK, 0, EPS)
            dve.wait_ge(S("ada_pe_done"), 1)
            own(V.tensor_copy(MOD[:, 2 * ADA_VECTOR:2 * ADA_FIRST], PS[7][:, 0:2 * (ADA_FIRST - ADA_VECTOR)]))
            dve.wait_ge(S("vecs_in"), 16)
            ada_finish(0, ADA_FIRST)
            dve.wait_ge(S("x_in"), 16)
            modulate(0, TOK, *mods(0, 0))

            dve.wait_ge(S("consts_in"), 48)
            for t in range(16):
                lo_ahead("ret_qk", t, t)
                rot = tmp(4)[:, t % 2 * LAT:(t % 2 + 1) * LAT]
                if t >= 2:
                    dve.wait_ge(S("qk_rope_done"), t - 1)
                dve.wait_ge(S("tile_done"), FIRST["ret_qk"] + t + 1)
                ps, par = PS[t % 8], t % 2
                V.tensor_tensor(QK[:, t, 0:LAT], ps[:, 0:LAT], ROPE[:, 0, par, :], MUL)
                V.tensor_tensor(rot[0:64, :], ps[64:128, 0:LAT], ROPE[64:128, 1, par, :], MUL)
                V.tensor_tensor(rot[64:128, :], ps[0:64, 0:LAT], ROPE[0:64, 1, par, :], MUL)
                V.tensor_copy(QK[:, t, LAT:TOK], ps[:, LAT:TOK]).then_inc(S("qk_free"), 1)
                ada_tile(t, 0, t, 16, 0, AREA_A)
            for grp in range(2):
                for k in range(8):
                    lo_ahead("ret_v", 8 * grp + k, 8 * grp + k)
                    ada_tile(8 * grp + k, 0, 8 * grp + k, 16, 16, AREA_A)
                for b in range(0, 8, 2):
                    bank_ready(dve, "ret_v", b, grp)
                    V.tensor_copy(RV[:, b // 2, 1024 * grp:1024 * grp + 512], PS[b][:, :]).then_inc(S("v_free"), 1)

            dve.wait_ge(S("ada_used"), 32)
            ada_finish(ADA_FIRST, 48)

            def ret_gate(t, i, s):
                lo_ahead("ret_g", t, s)
                dve.wait_ge(S("rg_free"), t + 9)
                V.tensor_scalar(RG[:, t, :], RG[:, t, :], VECS[:, bass.ds(t + VEC["ret_norm_g"], 1)], None, MUL)\
                    .then_inc(S("rg_scaled"), 1)
            tiles(dve, 16, 8, ret_gate)
            dve.wait_ge(S("rg_scaled"), 16)
            dve.wait_ge(S("qk_rope_done"), 16)

            log_sigmoid(0, vec("decay", 0, 8), *LS_RET, LG[:, :])
            dve.sem_inc(S("log_gamma_done"), 1)
            dve.wait_ge(S("decay_in"), 16)
            for h in range(RET_HEADS):
                same, cross = DECAY_D[:, h % 2, 0, :], DECAY_D[:, h % 2, 1, :]
                dve.wait_ge(S("decay_exp"), h + 1)
                own(V.tensor_tensor(same, tmp(0), DECAY_E[:, 2, :], MUL))
                own(V.tensor_tensor(tmp(1), tmp(1), DECAY_E[:, 3, :], MUL))
                own(V.tensor_tensor(same, same, tmp(1), ADD))
                V.tensor_tensor(cross, tmp(2), tmp(3), ADD).then_inc(S("decay_used"), 1)
                dve.wait_ge(S("decay_used"), h + 1)
                if h:
                    dve.wait_ge(S("ret_o_done"), 4 * h)
                for b, decay in enumerate((same, cross, same)):
                    dve.wait_ge(S("score_done"), 3 * h + b + 1)
                    V.scalar_tensor_tensor(ATT[:, 2 * b:2 * b + 2, :].rearrange("p a n -> p (a n)"), PS[b][:, :],
                                           RET_DK ** -0.5, decay, MUL, MUL).then_inc(S("att_done"), 1)
                for t in range(4):
                    n, st = 4 * h + t, 16 * (t % 2)
                    dve.wait_ge(S("ret_o_done"), n + 1)
                    if n >= 2:
                        dve.wait_ge(S("on_done"), n - 1)
                    own(V.bn_stats(RSTAT[:, st:st + 6], PS[3 + t][:, :]))
                    own(V.bn_aggr(RSTAT[:, st + 6:st + 8], RSTAT[:, st:st + 6]))
                    V.tensor_scalar(RSTAT[:, st + 8:st + 9], RSTAT[:, st + 7:st + 8], EPS, None, ADD)\
                        .then_inc(S("ret_var"), 1)
                    dve.wait_ge(S("ret_std"), n + 1)
                    own(V.reciprocal(RSTAT[:, st + 10:st + 11], RSTAT[:, st + 9:st + 10]))
                    V.scalar_tensor_tensor(RSTAT[:, st + 11:st + 12], RSTAT[:, st + 6:st + 7], -1.0,
                                           RSTAT[:, st + 10:st + 11], MUL, MUL).then_inc(S("ret_nmr"), 1)
                for t in range(4):
                    dve.wait_ge(S("on_t_done"), 4 * h + t + 1)
                    y = RG[:, 4 * h:4 * h + 4, t * P:(t + 1) * P]
                    V.tensor_tensor(y, PS[7][:, :].rearrange("p (f n) -> p f n", f=4), y, MUL)\
                        .then_inc(S("ret_y_done"), 1)
            dve.wait_ge(S("ret_y_done"), 16)
            for c in range(16):
                dve.wait_ge(S("ret_y_hi_done"), c + 1)
                V.tensor_tensor(YLO[:, c, :], RG[:, c, :], YHI[:, c, :].bitcast(F32), SUB)\
                    .then_inc(S("ret_y_lo_done"), 1)
            rows_back(1)
            weights_only("ret_out", 16, 32, AREA_B)
            dve.wait_ge(S("ada_used"), 48)
            ada_finish(48, 64)
            residual("ret_out", TOK, 0, 2, 0)

            def ffn(layer, T, q, m, x0):
                variance(q, T, 0, EPS)
                modulate(m, T, *mods(layer, 3))
                ph = f"ffn{layer}_in"
                fhi, flo = (FHI, FLO) if layer == 0 else (FHI1, FLO1)

                def tile(t, i, s, t0=0):
                    lo_ahead(ph, t + t0, s + t0)
                    if layer == 0:
                        ada_tile(t, i, s, 8, 48 + t0, AREA_G)
                    if s % 2:
                        p = i * 4 + (s // 2 + t0 // 2)
                        raw = tmp(s // 2 % 2, T)
                        dve.wait_ge(S("tile_done"), t + (FIRST[ph] + t0 + 1))
                        dve.wait_ge(S(f"ffn{layer}_a_free"), p + 5)
                        V.tensor_tensor(raw, PS[s % 8][:, 0:T], tmp(3 + s // 2 % 2, T), MUL)\
                            .then_inc(S(f"ffn{layer}_g_free"), 1)
                        dve.wait_ge(S("f_hi_done"), p + (FFN_C * layer + 1))
                        V.tensor_tensor(flo[:, p, 0:T], raw, fhi[:, p, 0:T].bitcast(F32), SUB)\
                            .then_inc(S("f_lo_done"), 1)
                        dve.wait_ge(S("f_lo_done"), p + (FFN_C * layer + 1))
                if layer == 0:
                    rows_back(2)
                    tiles(dve, 32, 8, tile)
                    rows_back(3)
                    tiles(dve, 12, 8, lambda t, i, s: tile(t, i, s, 32))
                    rows_back(4)
                    weights_only("ffn0_out", 22, 92, AREA_B)
                    dve.wait_ge(S("ada_used"), 114)
                    ada_finish(64, 128)
                    dve.wait_ge(S("x_back"), 16)
                else:
                    tiles(dve, COUNT[ph], 8, tile)
                    rows_back(5)
                    weights_only("ffn1_out", 6, 114, AREA_E)
                    dve.wait_ge(S("ada_used"), 120)
                    ada_finish(128, 136)
                residual(f"ffn{layer}_out", T, layer, 5, x0)

            ffn(0, TOK, 1, 1, 8)

            variance(2, TOK, 0, EPS)
            modulate(2, TOK, *mods(1, 0))
            for t in range(16 + 3):
                if t < 16:
                    lo_ahead("diff_qk", t, t)
                if t == 1:
                    dve.wait_ge(S("diff_tab_in"), 32)
                u = t - 1
                if 0 <= u < 16:
                    T = TOK if u < 8 else LAT
                    dve.wait_ge(S("dqk_stat"), u + 1)
                    if u >= 2:
                        dve.wait_ge(S("dqk_norm"), u - 1)
                    V.tensor_scalar(DRST[:, u % 2, 0:T], PS[4 + u % 2][:, 0:T], 1.0 / DIFF_DH, EPS, MUL, ADD)\
                        .then_inc(S("dqk_var"), 1)
                u = t - 2
                if 0 <= u < 16:
                    T = TOK if u < 8 else LAT
                    dst = DK[:, u, :] if u < 8 else DQ[:, u - 8, :]
                    dve.wait_ge(S("dqk_std"), u + 1)
                    own(V.reciprocal(DRST[:, u % 2, 0:T], DRST[:, u % 2, 0:T]))
                    dve.wait_ge(S("dqk_raw"), u + 1)
                    V.scalar_tensor_tensor(dst, DRAWB[:, u % 4, 0:T], vec("diff_k_g" if u < 8 else "diff_q_g"),
                                           DRST[:, u % 2, 0:T], MUL, MUL).then_inc(S("dqk_norm"), 1)
                u = t - 3
                if 0 <= u < 16:
                    dve.wait_ge(S("dqk_rot"), u + 1)
                    if u >= 2:
                        dve.wait_ge(S("dqk_rope"), u - 1)
                    V.tensor_tensor(DRT[:, u % 2, :], PS[6 + u % 2][:, 0:LAT], D_SIN, MUL).then_inc(S("dqk_sin"), 1)
            for k in range(8):
                lo_ahead("diff_v", k, k)
            for b in range(0, 8, 2):
                bank_ready(dve, "diff_v", b)
                V.tensor_copy(DV[:, b // 2, 0:512], PS[b][:, :]).then_inc(S("v_free"), 1)
            own(V.tensor_tensor(DLAM[:, 0:64], DLAM[:, 0:64], DLAM[:, 64:128], MUL))
            own(V.tensor_tensor(DLAM[:, 128:192], DLAM[:, 128:192], DLAM[:, 192:256], MUL))
            own(V.reduce_sum(DCOL[:, 2:3], DLAM[:, 0:64], AX.X))
            V.reduce_sum(DCOL[:, 3:4], DLAM[:, 128:192], AX.X).then_inc(S("lam_dot"), 1)
            own(V.tensor_scalar(DCOL[:, 1:2], vec("subln_g"), 1.0 - LAMBDA_INIT, None, MUL))
            dve.wait_ge(S("lam_exp"), 1)
            own(V.tensor_tensor(DCOL[:, 0:1], DCOL[:, 3:4], DCOL[:, 2:3], SUB))
            own(V.tensor_scalar(DCOL[:, 0:1], DCOL[:, 0:1], -LAMBDA_INIT, None, ADD))
            scale = DIFF_DH ** -0.5
            for u in range(16 + 3):
                if u < 16:
                    if u >= 2:
                        dve.wait_ge(S("d_exp"), 2 * (u - 1))
                    for m in range(2):
                        col = 4 + 2 * (u % 2) + m
                        dve.wait_ge(S("d_score"), 2 * u + m + 1)
                        own(V.reduce_max(DCOL[:, col + 12:col + 13], PS[2 * (u % 2) + m][:, :], AX.X))
                        V.tensor_scalar(DCOL[:, col:col + 1], DCOL[:, col + 12:col + 13], -scale, None, MUL)\
                            .then_inc(S("d_max"), 1)
                a = u - 1
                if 0 <= a < 16:
                    c = 8 + 2 * (a % 2)
                    dve.wait_ge(S("d_exp"), 2 * (a + 1))
                    own(V.reciprocal(DCOL[:, c + 16:c + 18], DCOL[:, c:c + 2]))
                    own(V.tensor_tensor(DCOL[:, c + 17:c + 18], DCOL[:, c + 17:c + 18], DCOL[:, 0:1], MUL))
                    if a >= 2:
                        dve.wait_ge(S("d_tr"), a - 1)
                    own(V.tensor_scalar(DP[:, a % 2, :], DE[:, a % 2, 0, :], DCOL[:, c + 16:c + 17], None, MUL))
                    V.scalar_tensor_tensor(DP[:, a % 2, :], DE[:, a % 2, 1, :], DCOL[:, c + 17:c + 18],
                                           DP[:, a % 2, :], MUL, ADD).then_inc(S("d_p"), 1)
                    dve.wait_ge(S("d_p"), a + 1)
                b = u - 3
                if 0 <= b < 16 and b % 2:
                    h = b // 2
                    dve.wait_ge(S("d_pv"), b + 1)
                    V.tensor_copy(DO[:, h, :], PS[6 + h % 2][:, 0:LAT]).then_inc(S("d_ocopy"), 1)
            for h in range(DIFF_HEADS + 1):
                if h < DIFF_HEADS:
                    dve.wait_ge(S("do_stat"), h + 1)
                    if h >= 2:
                        dve.wait_ge(S("do_norm"), h - 1)
                    V.tensor_scalar(tmp(1 + h % 2, LAT), PS[h % 2][:, 0:LAT], 1.0 / DIFF_DV, EPS, MUL, ADD)\
                        .then_inc(S("do_var"), 1)
                g = h - 1
                if 0 <= g:
                    dve.wait_ge(S("do_std"), g + 1)
                    own(V.reciprocal(tmp(1 + g % 2, LAT), tmp(1 + g % 2, LAT)))
                    V.scalar_tensor_tensor(DO[:, g, :], DO[:, g, :], DCOL[:, 1:2], tmp(1 + g % 2, LAT), MUL, MUL)\
                        .then_inc(S("do_norm"), 1)
            weights_only("diff_out")
            residual("diff_out", LAT, 1, 2, 16)
            ffn(1, LAT, 3, 3, 24)

            dve.wait_ge(S("x_in"), 32)
            modulate(4, TOK, *mods(2, 0), normed=False)
            dve.wait_ge(S("pool_own"), CONV_ZERO)
            def conv_sum(p):
                acc0 = CACC[:, 2 * (p % 2), :]
                dve.wait_ge(S("pool_own"), CONV_ZERO + (POOL_TAPS - 1) * (p + 1))
                own(V.tensor_tensor(acc0, acc0, CACCP[:, p % 2, :], ADD))
                dve.wait_ge(S("conv_pe_done"), p + 1)
                rows = acc0[:, 0:CONV_CTX].rearrange("p (r w) -> p r w", w=ROW_PADDED)[:, :, 0:GRID_W]
                V.tensor_tensor(rows, rows, PS[2 * p % 8][:, 0:LAT].rearrange("p (r w) -> p r w", w=GRID_W), ADD)
                V.tensor_tensor(acc0[:, CONV_CTX:CONV_CTX + CTX], acc0[:, CONV_CTX:CONV_CTX + CTX],
                                PS[2 * p % 8][:, LAT:TOK], ADD).then_inc(S("conv_acc_done"), 1)

            for t in range(16):
                lo_ahead("pw1", t, t)
                if t % 2 == 0:
                    continue
                p, ps = t // 2, PS[t % 8]
                dve.wait_ge(S("tile_done"), FIRST["pw1"] + t + 1)
                dve.wait_ge(S("pw1_gate_free"), 4 + p + 1)
                V.scalar_tensor_tensor(
                    CIN[:, p, 0:CONV_CTX].rearrange("p (r w) -> p r w", w=ROW_PADDED)[:, :, CONV_PAD:CONV_PAD + GRID_W],
                    ps[:, 0:LAT].rearrange("p (r w) -> p r w", w=GRID_W), vec("b_pw1", p),
                    tmp(3 + p % 2)[:, 0:LAT].rearrange("p (r w) -> p r w", w=GRID_W), ADD, MUL)
                V.scalar_tensor_tensor(CIN[:, p, CONV_CTX + CONV_PAD:CONV_CTX + CONV_PAD + CTX], ps[:, LAT:TOK],
                                       vec("b_pw1", p), tmp(3 + p % 2)[:, LAT:TOK], ADD, MUL)\
                    .then_inc(S("pw1_a_free"), 1)
                dve.wait_ge(S("pw1_a_free"), 4 + p + 1)
                if p:
                    conv_sum(p - 1)
                if p >= 2:
                    dve.wait_ge(S("conv_z_done"), p - 1)
                acc0, acc1 = CACC[:, 2 * (p % 2), :], CACC[:, 2 * (p % 2) + 1, :]
                for j in range(DVE_TAPS):
                    acc, x_j, w_j = (acc0, acc1)[j % 2], CIN[:, p, j:j + CONV_OUT], vec("w_dw", p * CONV_W + j)
                    if j < 2:
                        ins = V.tensor_scalar(acc, x_j, w_j, None, MUL)
                    else:
                        ins = V.scalar_tensor_tensor(acc, x_j, w_j, acc, MUL, ADD)
                    own.at += 1
                    ins.then_inc(S("dve_own"), 1)
                    if j:
                        dve.wait_ge(S("dve_own"), own.at - 1)
                dve.wait_ge(S("dve_own"), own.at)
                own(V.tensor_tensor(acc0, acc0, acc1, ADD))
            conv_sum(DC - 1)
            dve.wait_ge(S("conv_z_done"), 8)
            layer_norm(0, 4, TOK, CZ)
            for c in range(DC):
                V.tensor_tensor(CZ[:, c, :], CZ[:, c, :], tmp(2), MUL).then_inc(S("cz_norm"), 1)
            for c in range(DC):
                dve.wait_ge(S("cz_hi_done"), c + 1)
                V.tensor_tensor(HLO[:, c, :], tmp(c % 2), HHI[:, c, :].bitcast(F32), SUB).then_inc(S("cz_lo_done"), 1)
            for c in range(DC):
                for st, cols in STREAMS:
                    g = mod(2, 2, c, st)
                    own(V.tensor_tensor(FUSE[:, 0:1], vec("b_pw2", c), g, MUL))
                    last = V.tensor_scalar(X[:, c, cols], X[:, c, cols], ALPHA, FUSE[:, 0:1], MUL, ADD)
                    own(last)
            weights_only("pw2")
            residual("pw2", TOK, 2, 2, 32)

            def norm_x(ln, q, T, g, b, j):
                layer_norm(ln, q, T, X)
                for c in range(DC):
                    last = V.tensor_tensor(X[:, c, 0:T], X[:, c, 0:T], tmp(2, T), MUL)
                own(last)
                for c in range(DC):
                    V.tensor_scalar(X[:, c, 0:T], X[:, c, 0:T], vec(g, 8 * j + c), vec(b, 8 * j + c), MUL, ADD)\
                        .then_inc(S("x_final"), 1)

            def norm_modulate(ln, q, m, T, g, b, j, layer, first, keep):
                a = layer * 2 * ADA_TILES
                sc, sh = (MOD[:, a + 2 * DC * k:a + 2 * DC * (k + 1)] for k in (first + 1, first))
                gain, bias = vec(g, 8 * j, DC), vec(b, 8 * j, DC)
                f_gain, f_bias = FUSE[:, 0:2 * DC], FUSE[:, 2 * DC:4 * DC]
                a_gain, a_bias = FUSE[:, 4 * DC:5 * DC], FUSE[:, 5 * DC:6 * DC]
                for st in range(2):
                    V.tensor_tensor(f_gain[:, st::2], sc[:, st::2], gain, MUL)
                    V.tensor_tensor(f_bias[:, st::2], sc[:, st::2], bias, MUL)
                V.tensor_scalar(a_gain, gain, ALPHA, None, MUL)
                own(V.tensor_scalar(a_bias, bias, ALPHA, None, MUL))
                own(V.tensor_tensor(f_bias, f_bias, sh, ADD))
                layer_norm(ln, q, T, X)
                modulate(m, T, lambda c, st: f_gain[:, 2 * c + st:2 * c + st + 1],
                         lambda c, st: f_bias[:, 2 * c + st:2 * c + st + 1])
                for c in range(DC):
                    last = V.tensor_tensor(X[:, c, 0:keep], X[:, c, 0:keep], tmp(2, keep), MUL)
                own(last)
                for c in range(DC):
                    last = V.tensor_scalar(X[:, c, 0:keep], X[:, c, 0:keep], a_gain[:, c:c + 1], a_bias[:, c:c + 1],
                                           MUL, ADD)
                own(last)

            def mlp(j, T, q, m, ln, x0):
                layer = 2 + j
                norm_modulate(ln, q, m, T, "ln1_g", "ln1_b", j, layer, 3, T)
                for n, half in enumerate("ab"):
                    ph, before, done = f"mlp{j}{half}_in", 24 * (2 * j + n), 16 * (2 * j + n)

                    def tile(t, i, s):
                        lo_ahead(ph, t, s)
                        if j == 0:
                            ada_tile(t, i, s, 8, 120 + 32 * n, AREA_F)
                        raw, r = tmp(s % 2, T), tmp(3 + s % 2, T)
                        dve.wait_ge(S("m_relu_done"), t + (done + 1))
                        dve.wait_ge(S("mlp_free"), t + (before + 7))
                        V.tensor_tensor(raw, r, r, MUL).then_inc(S("m_sq_done"), 1)
                    if j == 0 and n == 0:
                        rows_back(6)
                    tiles(dve, 16, 8, tile)
                    if j == 0 and n == 0:
                        dve.wait_ge(S("ada_used"), 136)
                        ada_finish(136, 144)
                        weights_only("mlp0a_out", 16, 136, AREA_F)
                    elif j == 0:
                        weights_only("mlp0b_out", 8, 168, AREA_F)
                        dve.wait_ge(S("ada_used"), 176)
                        ada_finish(144, 192)
                    else:
                        weights_only(f"mlp{j}{half}_out")
                    residual(f"mlp{j}{half}_out", T, layer, 5, x0 + 8 * n)
                if j == 0:
                    norm_modulate(ln + 1, q + 1, 6, T, "ln2_g", "ln2_b", j, 3, 0, LAT)
                else:
                    norm_x(ln + 1, q + 1, T, "ln2_g", "ln2_b", j)

            mlp(0, TOK, 5, 5, 1, 40)


            def up_x(t, i, s):
                lo_ahead("up_x", t, s)
                dve.wait_ge(S("up_hi_done"), t + 1)
                V.tensor_tensor(XMLO[:, t, :], PS[s][:, :], XMHI[:, t, :].bitcast(F32), SUB).then_inc(S("up_free"), 1)
            tiles(dve, 16, 8, up_x)
            weights_only("up_z")
            for grp in range(2):
                for k in range(16):
                    lo_ahead("ml_v", 16 * grp + k, 16 * grp + k)
                for b in range(0, 8, 2):
                    bank_ready(dve, "ml_v", b, grp)
                    V.tensor_copy(MV[:, b // 2, 1024 * grp:1024 * grp + 512], PS[b][:, :]).then_inc(S("v_done"), 1)

            GT = tmp(4)[0:16, :]

            def gate_add(n, mms):
                dve.wait_ge(S("gate_mm"), mms)
                if n == 0:
                    ins = V.tensor_scalar(GT, PS[0][0:16, :], vec("b_gate")[0:16, :], None, ADD)
                else:
                    ins = V.tensor_tensor(GT, PS[0][0:16, :], GT, ADD)
                ins.then_inc(S("gate_acc"), 1)
                dve.wait_ge(S("gate_acc"), n + 1)

            gate_add(0, 16)
            dve.wait_ge(S("ml_tables_in"), 32)
            own(V.memset(M_PAD, 0.0))

            def conv_chunk(k):
                for dst, cols in ((2, slice(0, LAT)), (ML_CTX + 2, slice(LAT, TOK))):
                    last = V.tensor_tensor(M_PAD[:, dst:dst + LAT], XMHI[:, k, cols].bitcast(F32),
                                           XMLO[:, k, cols].bitcast(F32), ADD)
                own(last)
                if k:
                    dve.wait_ge(S("xc_done"), k)
                for j in range(ML_TAPS):
                    x_j, w_j = M_PAD[:, j:j + ML_OUT], vec("ml_w_conv", k * ML_TAPS + j)
                    if j == 0:
                        own(V.tensor_scalar(M_ACC, x_j, w_j, None, MUL))
                    elif j < ML_TAPS - 1:
                        own(V.scalar_tensor_tensor(M_ACC, x_j, w_j, M_ACC, MUL, ADD))
                    else:
                        V.scalar_tensor_tensor(M_ACC, x_j, w_j, M_ACC, MUL, ADD).then_inc(S("mconv_done"), 1)
                        dve.wait_ge(S("mconv_done"), k + 1)

            for g in range(4):
                for k in range(16):
                    lo_ahead("ml_o", 16 * g + k, 16 * g + k)
                    if k % 4 == 0:
                        conv_chunk(4 * g + k // 4)
                if g >= 2:
                    dve.wait_ge(S(f"o_spilled{g % 2}"), 16)
                for n in range(4):
                    bank_ready(dve, "ml_o", n, g)
                    a = 1024 * g + 512 * (n % 2)
                    V.tensor_tensor(MOG[:, g % 2, n // 2, 512 * (n % 2):512 * (n % 2) + 512], PS[4 * (g % 2) + n][:, :],
                                    BO[:, a:a + 512], ADD).then_inc(S("o_add"), 1)
            for grp in range(2):
                for k in range(-2 if grp == 0 else 0, MLC):
                    if k >= 0:
                        lo_ahead("ml_q", MLC * grp + k, MLC * grp + k)
                    if grp == 0 and k + 2 < MLC:
                        dve.wait_ge(S("xc_hi_done"), k + 3)
                        V.tensor_tensor(XMLO[:, k + 2, :], XC[:, k + 2, :], XMHI[:, k + 2, :].bitcast(F32), SUB)\
                            .then_inc(S("xc_lo_done"), 1)
                if grp == 0:
                    for g in range(2):
                        dve.wait_ge(S(f"o_spilled{g}"), 32)
                else:
                    dve.wait_ge(S("gate_mm"), 32)
                for o in range(0, DC, 2):
                    bank_ready(dve, "ml_q", o, grp)
                    V.tensor_copy(MQ[:, 8 * grp + o, :], PS[o][:, 0:LAT])
                    V.tensor_copy(MQC[:, o, :], PS[o][:, LAT:TOK]).then_inc(S("q_done"), 1)
                gate_add(1 + grp, 16 + 16 * (grp + 1))
                if grp == 0:
                    for k in range(MLC):
                        last = V.tensor_scalar(XCL[:, k, :], XC[:, k, 0:LAT], vec("skip", k), None, MUL)
                    own(last)
            for grp in range(2):
                for k in range(MLC):
                    lo_ahead("ml_k", MLC * grp + k, MLC * grp + k)
                for o in range(0, DC, 2):
                    bank_ready(dve, "ml_k", o, grp)
                    V.tensor_copy(MK[:, 8 * grp + o, :], PS[o][:, :]).then_inc(S("k_done"), 1)
                gate_add(3 + grp, 48 + 8 * (grp + 1))

            def R(i):
                return ROWS[0:36, i, :]

            BACK = slice(32, 36)
            dve.wait_ge(S("gate_rows"), 2)
            own(V.memset(R(11), 0.0))
            for g, dst in ((0, R(0)), (1, R(2))):
                V.tensor_copy(dst[:, 0:CTX], PS[4 + g][0:36, LAT:TOK])
                own(V.tensor_copy(dst[:, CTX:TOK], PS[4 + g][0:36, 0:LAT]))
                own(V.tensor_copy(dst[BACK, :], PS[4 + g][BACK, ::-1]))
            log_sigmoid(1, R(2), R(4), R(5), R(6), R(7), R(8), R(4))
            own(V.tensor_tensor_scan(R(8), R(4), R(11), 0.0, ADD, ADD))
            own(V.tensor_tensor(R(5), R(0), R(8), SUB))
            own(V.tensor_tensor_scan(R(9), R(5), R(5), 0.0, MAX, MAX))
            own(V.tensor_tensor(R(6), R(8), R(9), ADD))
            V.tensor_scalar(R(6), R(6), -1.0, None, MUL)
            own(V.tensor_scalar(R(9), R(9), -1.0, None, MUL))
            V.tensor_copy(ROWS[BACK, 12, :], ROWS[BACK, 5, ::-1])
            V.tensor_copy(ROWS[BACK, 14, 0:LAT], ROWS[BACK, 6, ::-1][:, 0:LAT])
            V.tensor_copy(ROWS[BACK, 14, LAT:TOK], ROWS[BACK, 9, ::-1][:, 0:LAT]).then_inc(S("rows_done"), 1)
            dve.wait_ge(S("ml_cols"), 2)
            V.tensor_copy(M_COLS[:, 0:24], PS[4][:, 0:24])
            V.tensor_copy(M_COLS[:, 24:48], PS[7][:, 24:48]).then_inc(S("ml_cols_copy"), 1)
            dve.wait_ge(S("ml_cols_copy"), 1)

            def ml_args(h):
                if h >= 2:
                    dve.wait_ge(S("ml_num"), 4 * (h - 1))
                for d in range(2):
                    dve.wait_ge(S("rb_copy"), 2 * h + d + 1)
                    for j in range(4):
                        col = (d * 6 + j) * 4 + h
                        last = V.tensor_scalar(MPT(h, d)[:, j, :], X[:, 2 * h + d, LAT:TOK], M_COLS[:, col:col + 1],
                                               0.0, ADD, MIN)
                    last.then_inc(S("ml_arg"), 1)

            def ml_probs(h):
                for d in range(2):
                    dve.wait_ge(S("ml_exp"), 2 * h + d + 1)
                    for t in range(2):
                        diag = MPT(h, d)[:, t, t * P:(t + 1) * P]
                        last = V.tensor_tensor(diag, diag, M_TRI[:, d * P:(d + 1) * P], MUL)
                    own(last)
                    dve.wait_ge(S("ml_scores_done"), h + 1)
                    for b in range(2):
                        p_b = MPT(h, d)[:, 2 * b:2 * b + 2, :].rearrange("p a n -> p (a n)")
                        V.scalar_tensor_tensor(p_b, PS[2 * (h % 2) + b][:, :], ML_DH ** -0.5, p_b, MUL, MUL)\
                            .then_inc(S("ml_p"), 1)

            def ml_out(h):
                den = PS[4 + h % 2][:, 0:4]
                exp_m = M_COLS.rearrange("p (d j h) -> p d j h", d=2, j=6)[:, :, 4:6, h]
                dve.wait_ge(S("ml_den"), h + 1)
                own(V.tensor_scalar(M_NEG, den, -1.0, None, MUL))
                own(V.tensor_tensor(M_DEN, den, M_NEG, MAX))
                own(V.tensor_tensor(M_DEN.rearrange("p (d t) -> p d t", d=2), M_DEN.rearrange("p (d t) -> p d t", d=2),
                                    exp_m, MAX))
                own(V.reciprocal(M_DEN, M_DEN))
                dve.wait_ge(S("o_back"), 16 * (h + 1))
                for d in range(2):
                    for t in range(2):
                        n = 2 * d + t
                        dst = MH[:, t, 512 * h:512 * (h + 1)] if d == 0 else MO2[:, t, 1, :]
                        dve.wait_ge(S("ml_num"), 4 * h + n + 1)
                        V.scalar_tensor_tensor(dst, PS[6 + n % 2][:, :], M_DEN[:, n:n + 1], MO2[:, t, d, :], MUL, MUL)\
                            .then_inc(S("ml_h_done"), 1)
                dve.wait_ge(S("ml_h_done"), 4 * h + 4)
                for t in range(2):
                    hs = MH[:, t, 512 * h:512 * (h + 1)]
                    V.tensor_tensor(hs, hs, MO2[:, t, 1, :], ADD).then_inc(S("head_done"), 1)
                for t in range(2):
                    r = t * ML_HEADS + h
                    dve.wait_ge(S("head_done"), 2 * h + t + 1)
                    last = V.bn_stats(GN_STATS[:, 6 * r:6 * r + 6], MH[:, t, 512 * h:512 * (h + 1)])
                own(last)
                for t in range(2):
                    r = t * ML_HEADS + h
                    last = V.bn_aggr(GN_AGGR[:, 2 * r:2 * r + 2], GN_STATS[:, 6 * r:6 * r + 6])
                own(last)

            ml_args(0)
            dve.wait_ge(S("tri_in"), 16)
            dve.wait_ge(S("rb_copy"), 8)
            ml_args(1)
            dve.wait_ge(S("exp_m_done"), 1)
            for h in range(ML_HEADS):
                ml_probs(h)
                if h:
                    ml_out(h - 1)
                    if h + 1 < ML_HEADS:
                        ml_args(h + 1)
            ml_out(ML_HEADS - 1)
            V.tensor_scalar(GN_VAR, GN_AGGR[:, 1:16:2], LN_EPS, None, ADD).then_inc(S("ret_var"), 1)
            dve.wait_ge(S("ret_std"), 17)
            own(V.reciprocal(GN_RSTD, GN_VAR))
            V.scalar_tensor_tensor(GN_NMR, GN_AGGR[:, 0:16:2], -1.0, GN_RSTD, MUL, MUL).then_inc(S("ret_nmr"), 1)
            dve.wait_ge(S("ret_nmr"), 17)
            for h in range(ML_HEADS):
                z, r = MH[:, 1, 512 * h:512 * (h + 1)], ML_HEADS + h
                V.tensor_scalar(z, z, GN_RSTD[:, r:r + 1], GN_NMR[:, r:r + 1], MUL, ADD).then_inc(S("hn_done"), 1)
            dve.wait_ge(S("z_back"), 16)
            for c in range(MLC):
                y = tmp(c % 4, LAT)
                if c >= 4:
                    dve.wait_ge(S("ml_y_lo"), c - 3)
                dve.wait_ge(S("hn_tr"), c + 1)
                V.scalar_tensor_tensor(y, PS[c % 4][:, 0:LAT], vec("gn_g", c), XCL[:, c, :], MUL, ADD)\
                    .then_inc(S("ml_y_done"), 1)
                dve.wait_ge(S("ml_y_done"), c + 1)
                V.tensor_tensor(y, y, MZ2[:, c, :], MUL).then_inc(S("ml_y_raw"), 1)
            weights_only("down")
            residual("down", LAT, 3, 2, 56)
            mlp(1, LAT, 7, 7, 3, 64)


def _rope_angles(quarter):
    inv = np.power(np.float32(10000.0), -np.arange(quarter, dtype=np.float32) / np.float32(quarter))
    pos = np.arange(LAT)
    row = (pos // GRID_W).astype(np.float32)
    col = (pos % GRID_W).astype(np.float32)
    return row[None, :] * inv[:, None], col[None, :] * inv[:, None]


def _constants():
    f32 = np.float32
    p = np.arange(P)
    ident = np.eye(P, dtype=f32)
    ones = np.ones((P, P), f32)
    tri_f = (p[None, :] >= p[:, None]).astype(f32)
    tri_b = (p[None, :] <= p[:, None]).astype(f32)
    consts = np.stack([ident, ones, tri_f, tri_b])
    ret_rope = np.zeros((P, 2, 2, LAT), f32)
    for par, ang in enumerate(_rope_angles(RET_DK // 4)):
        ret_rope[:, 0, par] = np.cos(np.concatenate([ang, ang]))
        ret_rope[:, 1, par] = np.sin(np.concatenate([ang, -ang]))
    j = (np.arange(2) * P)[None, :, None] + p[:, None, None]
    i = np.arange(LAT)[None, None, :]
    ret_decay = np.stack([np.maximum(i - j, 0), np.maximum(j - i, 0), i >= j, i <= j,
                          CTX + i - j, LAT - i + j], axis=1).astype(f32).reshape(P, 6, 512)
    row, col = _rope_angles(DIFF_DH // 4)
    ang = np.concatenate([row, row, col, col] * 2)
    block = (p[:, None] // DIFF_DH == p[None, :] // DIFF_DH).astype(f32)
    rot = np.zeros((P, P), f32)
    for m in range(P):
        if m % 32 < 16:
            rot[m + 16, m] = -1.0
        else:
            rot[m - 16, m] = 1.0
    diff_tab = np.concatenate([np.cos(ang), np.sin(ang), block, rot], axis=1).astype(f32)
    sel = np.zeros((36, ML_HEADS * P), f32)
    for d in range(2):
        sel[32 * d:32 * d + ML_HEADS] = np.repeat(np.eye(ML_HEADS, dtype=f32), P, axis=1)
    return consts, ret_rope, ret_decay, diff_tab, sel


def _rows(w):
    n = w.shape[1] // P
    return w.reshape(DC, P, n, P).transpose(2, 1, 0, 3).reshape(n, P, 1024)


def _pairs(a, b):
    return np.stack([a, b], axis=1).reshape(-1, P, 1024)


def _cols(w):
    k, n = w.shape
    return w.reshape(k // P, P, n // 1024, 1024).transpose(2, 0, 1, 3).reshape(-1, P, 1024)


def _chunks(v):
    return v.reshape(-1, P).T


def kernel(**inputs):
    import concourse.bacc as bacc
    from concourse.bass_utils import run_bass_kernel_spmd

    a = {k: np.asarray(v) for k, v in inputs.items()}
    f32 = np.float32

    def ffn(layer):
        w = a["ffn_w_in"][layer]
        return [_pairs(_rows(w[:, :FFN]), _rows(w[:, FFN:])), _cols(a["ffn_w_out"][layer])]

    def mlp(j):
        w1, w2 = _rows(a["mlp_w1_2"][j]), _cols(a["mlp_w2_2"][j])
        return [w1[:16], w2[:16], w1[16:], w2[16:]]

    ret, diff, pw1 = a["ret_w_in"][0], a["diff_w_in"][0], a["conv_w_pw1_2"][0]
    up = a["ml_w_up_2"][0]
    diff_rows = _rows(diff[:, :2048])
    parts = [_rows(ret[:, :2048]), _cols(ret[:, 2048:4096]), _rows(ret[:, 4096:]), _cols(a["ret_w_out"][0]),
             *ffn(0), diff_rows[8:], diff_rows[:8], _cols(diff[:, 2048:]), _cols(a["diff_w_out"][0]), *ffn(1),
             _pairs(_rows(pw1[:, D:]), _rows(pw1[:, :D])), _cols(a["conv_w_pw2_2"][0]), *mlp(0),
             _rows(up[:, :ML_INNER]), _rows(up[:, ML_INNER:]), _cols(a["ml_w_v_2"][0]), _cols(a["ml_w_o_2"][0]),
             _cols(a["ml_w_q_2"][0]), _cols(a["ml_w_k_2"][0]), _cols(a["ml_w_down_2"][0]), *mlp(1),
             np.zeros((LOOKAHEAD, P, 1024), f32)]
    weights = np.concatenate(parts)
    assert weights.shape[0] == N_TILES + LOOKAHEAD
    ada = np.concatenate([w.T.reshape(ADA_TILES, P, D) for w in (a["ada_w"][0], a["ada_w"][1],
                                                                 a["ada_w_2"][0], a["ada_w_2"][1])])
    for n in range(ADA_VECTOR, ADA_FIRST):
        ada[n] = a["ada_w"][0][:, n * P:(n + 1) * P].reshape(DC, P, P).transpose(1, 0, 2).reshape(P, D)
    c_rows = np.broadcast_to(np.stack([a["c"][0], a["c_ctx"], a["c_2"][0], a["c_ctx_2"]])[None], (P, 4, D))

    def tokens(x):
        return x.T.reshape(DC, P, -1).transpose(1, 0, 2)

    x_t = np.concatenate([tokens(a["x"][0]), tokens(a["ctx"][0])], axis=2)
    ctx2_t = tokens(a["ctx_2"][0])
    b_gate = np.zeros((P, 1), f32)
    b_gate[:16, 0] = a["ml_b_gate_2"][0]
    gate_sel = np.zeros((P, 2, 36), f32)
    for h in range(ML_HEADS):
        for d in range(2):
            for g in range(2):
                gate_sel[8 * d + 4 * g + h, g, 32 * d + h] = 1.0
    gate_sel = gate_sel.reshape(P, 72)
    named = {
        "c_cols": np.stack([a["c"][0].reshape(DC, P).T, a["c_ctx"].reshape(DC, P).T], axis=2).reshape(P, 2 * DC),
        "ret_norm_g": _chunks(a["ret_norm_g"][0]),
        "diff_q_g": np.tile(a["diff_q_norm_g"][0], 2)[:, None],
        "diff_k_g": np.tile(a["diff_k_norm_g"][0], 2)[:, None],
        "subln_g": a["diff_subln_g"][0][:, None],
        "ada_b": np.concatenate([_chunks(a["ada_b"][0]), _chunks(a["ada_b"][1]), _chunks(a["ada_b_2"][0]),
                                 _chunks(a["ada_b_2"][1])], axis=1),
        "decay": np.broadcast_to(a["ret_decay_logit"][0].reshape(1, 8), (P, 8)),
        "b_pw1": _chunks(a["conv_b_pw1_2"][0]),
        "w_dw": a["conv_w_dw_2"][0].T.reshape(DC, P, CONV_W).transpose(1, 0, 2).reshape(P, -1),
        "b_dw": _chunks(a["conv_b_dw_2"][0]),
        "conv_ln_g": _chunks(a["conv_ln_g_2"][0]),
        "conv_ln_b": _chunks(a["conv_ln_b_2"][0]),
        "b_pw2": _chunks(a["conv_b_pw2_2"][0]),
        "ln1_g": _chunks(a["ln1_g_2"].reshape(-1)), "ln1_b": _chunks(a["ln1_b_2"].reshape(-1)),
        "ln2_g": _chunks(a["ln2_g_2"].reshape(-1)), "ln2_b": _chunks(a["ln2_b_2"].reshape(-1)),
        "ml_b_conv": _chunks(a["ml_b_conv_2"][0]),
        "ml_w_conv": a["ml_w_conv_2"][0].T.reshape(MLC, P, ML_TAPS).transpose(1, 0, 2).reshape(P, -1),
        "gn_g": _chunks(a["ml_gn_g_2"][0]),
        "skip": _chunks(a["ml_skip_2"][0]),
        "b_gate": b_gate,
        "gate_sel": gate_sel,
    }
    vecs = np.concatenate([named[name] for name, _ in VEC_LAYOUT], axis=1)
    assert vecs.shape == (P, N_VEC)
    consts, ret_rope, ret_decay, diff_tab, sel = _constants()
    lam = np.broadcast_to(a["diff_lambda"][0].reshape(1, 256), (P, 256))
    b_o = np.broadcast_to(a["ml_b_o_2"][0].reshape(1, 4096), (P, 4096))
    w_gate = a["ml_w_gate_2"][0].reshape(3, MLC, P, 16).transpose(2, 0, 1, 3).reshape(P, 3, 256)

    arrays = {"weights": weights, "ada": ada, "c_rows": c_rows, "x_t": x_t, "ctx2_t": ctx2_t, "vecs": vecs, "consts": consts,
              "ret_rope": ret_rope, "ret_decay": ret_decay, "diff_tab": diff_tab, "lam": lam, "b_o": b_o,
              "w_gate": w_gate, "sel": sel}
    arrays = {k: np.ascontiguousarray(v) for k, v in arrays.items()}
    nc = bacc.Bacc("TRN2", target_bir_lowering=False, num_devices=1)
    args = [nc.dram_tensor(f"in_{k}", v.shape, mybir.dt.from_np(v.dtype), kind="ExternalInput").ap()
            for k, v in arrays.items()]
    out = nc.dram_tensor("out_t", (P, DC, LAT), mybir.dt.float32, kind="ExternalOutput").ap()
    program(nc, *args, out)
    r = run_bass_kernel_spmd(nc, [{f"in_{k}": v for k, v in arrays.items()}], core_ids=[0])
    got = r.results[0]["out_t"]
    return got.transpose(2, 1, 0).reshape(1, LAT, D)
```
